# Optimizing a Trainium2 kernel written in Bass

```python
import jax, jax.numpy as jnp
from jax import lax
import numpy as np

D_MODEL = 1024
BATCH = 1
SEQ = 512
DEPTH = 2

D_MIX = D_MODEL
LRU_WIDTH = D_MIX // 4
LRU_BLOCKS = 4
LRU_BLOCK_W = LRU_WIDTH // LRU_BLOCKS
CONV_WIDTH = 4
LRU_C = 8.0
MLA_HEADS = 6
MLA_NOPE = 64
MLA_ROPE = 32
MLA_V = 64
MLA_Q_RANK = 192
MLA_KV_RANK = 128
NSA_HEADS = 6
NSA_KV_HEADS = 2
NSA_GROUP = NSA_HEADS // NSA_KV_HEADS
NSA_HEAD_DIM = 64
NSA_KV = NSA_KV_HEADS * NSA_HEAD_DIM
CMP_LEN = 32
CMP_STRIDE = 16
CMP_HIDDEN = 128
SEL_LEN = 64
SEL_TOPK = 16
WINDOW = 512
FORCE_BONUS = 1.0e3
Q_BLOCK = 128
D_FF = 2816
N_EXPERTS = 8
TOP_K = 2
D_FF_EXPERT = 1408
N_DENSE = (DEPTH + 1) // 2
N_MOE = DEPTH // 2
ROPE_THETA = 10000.0
EPS = 1e-6
NEG_INF = -1.0e30
IN_SPLITS = (LRU_WIDTH, LRU_WIDTH,
             MLA_Q_RANK, MLA_KV_RANK, MLA_ROPE,
             NSA_HEADS * NSA_HEAD_DIM, NSA_KV, NSA_KV, NSA_KV, NSA_KV, NSA_KV, NSA_KV, 3 * NSA_HEADS)
IN_COLS = sum(IN_SPLITS)

kernel_name = 'hymba_style_lru_mla_nsa_moe_block'

def rmsnorm(x, g):
    xf = x.astype(jnp.float32)
    y = xf * lax.rsqrt(jnp.mean(xf * xf, axis=-1, keepdims=True) + EPS)
    return (y * g.astype(jnp.float32)).astype(x.dtype)

def masked_softmax(s, mask):
    s = jnp.where(mask, s, NEG_INF)
    m = jnp.max(s, axis=-1, keepdims=True)
    e = jnp.where(mask, jnp.exp(s - m), 0.0)
    return e / jnp.maximum(jnp.sum(e, axis=-1, keepdims=True), 1e-30)

def rope(x, pos):
    d = x.shape[-1]
    half = d // 2
    inv = ROPE_THETA ** (-jnp.arange(half, dtype=jnp.float32) * 2.0 / d)
    ang = pos.astype(jnp.float32)[:, None] * inv[None, :]
    cos = jnp.cos(ang)[None, :, None, :].astype(x.dtype)
    sin = jnp.sin(ang)[None, :, None, :].astype(x.dtype)
    x1, x2 = x[..., :half], x[..., half:]
    return jnp.concatenate([x1 * cos - x2 * sin, x2 * cos + x1 * sin], axis=-1)

def causal_conv(x, w, b):
    S = x.shape[1]
    xp = jnp.pad(x, ((0, 0), (CONV_WIDTH - 1, 0), (0, 0)))
    out = b
    for k in range(CONV_WIDTH):
        out = out + xp[:, k:k + S] * w[k]
    return out

def block_diag(x, w, b):
    B, S, _ = x.shape
    y = jnp.einsum('bsnc,ncd->bsnd', x.reshape(B, S, LRU_BLOCKS, LRU_BLOCK_W), w)
    return y.reshape(B, S, LRU_WIDTH) + b

def rg_lru(x, wa, ba, wx, bx, lam):
    r = jax.nn.sigmoid(block_diag(x, wa, ba)).astype(jnp.float32)
    i = jax.nn.sigmoid(block_diag(x, wx, bx)).astype(jnp.float32)
    log_a = -LRU_C * r * jax.nn.softplus(-lam.astype(jnp.float32))
    a = jnp.exp(log_a)
    b = jnp.sqrt(-jnp.expm1(2.0 * log_a)) * (i * x.astype(jnp.float32))

    def combine(lhs, rhs):
        a1, b1 = lhs
        a2, b2 = rhs
        return a1 * a2, a2 * b1 + b2

    _, h = lax.associative_scan(combine, (a, b), axis=1)
    return h.astype(x.dtype)

def recurrent_group(x_in, y_in, conv_w, conv_b, wa, ba, wx, bx, lam):
    xc = causal_conv(x_in, conv_w, conv_b)
    return rg_lru(xc, wa, ba, wx, bx, lam) * jax.nn.gelu(y_in)

def causal_block_attention(q, k, v, scale):
    B, S, H, Dk = q.shape
    Dv = v.shape[-1]
    nb = S // Q_BLOCK
    qb = q.reshape(B, nb, Q_BLOCK, H, Dk).transpose(1, 0, 2, 3, 4)
    kpos = jnp.arange(S)

    def one(args):
        qi, bidx = args
        qpos = bidx * Q_BLOCK + jnp.arange(Q_BLOCK)
        s = jnp.einsum('bqhd,bkhd->bhqk', qi, k).astype(jnp.float32) * scale
        p = masked_softmax(s, (kpos[None, :] <= qpos[:, None])[None, None])
        return jnp.einsum('bhqk,bkhd->bqhd', p.astype(v.dtype), v)

    o = lax.map(one, (qb, jnp.arange(nb)))
    return o.transpose(1, 0, 2, 3, 4).reshape(B, S, H * Dv)

def mla_group(q_dn, kv_dn, k_pe, pos, q_norm, w_uq, kv_norm, w_ukv):
    B, S, _ = q_dn.shape
    q = (rmsnorm(q_dn, q_norm) @ w_uq).reshape(B, S, MLA_HEADS, MLA_NOPE + MLA_ROPE)
    q = jnp.concatenate([q[..., :MLA_NOPE], rope(q[..., MLA_NOPE:], pos)], axis=-1)
    kv = (rmsnorm(kv_dn, kv_norm) @ w_ukv).reshape(B, S, MLA_HEADS, MLA_NOPE + MLA_V)
    k_rope = jnp.broadcast_to(rope(k_pe[:, :, None, :], pos), (B, S, MLA_HEADS, MLA_ROPE))
    k = jnp.concatenate([kv[..., :MLA_NOPE], k_rope], axis=-1)
    v = kv[..., MLA_NOPE:]
    return causal_block_attention(q, k, v, (MLA_NOPE + MLA_ROPE) ** -0.5)

def compress(kv, pos_emb, w1, w2):
    B, S = kv.shape[0], kv.shape[1]
    nc = (S - CMP_LEN) // CMP_STRIDE + 1
    idx = jnp.arange(nc)[:, None] * CMP_STRIDE + jnp.arange(CMP_LEN)[None, :]
    win = kv[:, idx] + pos_emb[None, None, :, None, :]
    flat = win.transpose(0, 1, 3, 2, 4).reshape(B, nc, NSA_KV_HEADS, CMP_LEN * NSA_HEAD_DIM)
    return jax.nn.gelu(flat @ w1) @ w2

def nsa_group(q_in, kc_in, vc_in, ks_in, vs_in, kw_in, vw_in, g_in, gate_b, pos, cmp_pos, cmp_w1, cmp_w2):
    B, S, _ = q_in.shape
    G, P, D = NSA_KV_HEADS, NSA_GROUP, NSA_HEAD_DIM
    q = rope(q_in.reshape(B, S, NSA_HEADS, D), pos)
    kc = compress(rope(kc_in.reshape(B, S, G, D), pos), cmp_pos[0], cmp_w1[0], cmp_w2[0])
    vc = compress(vc_in.reshape(B, S, G, D), cmp_pos[1], cmp_w1[1], cmp_w2[1])
    nc = kc.shape[1]
    ns = S // SEL_LEN
    n_top = min(SEL_TOPK, ns)
    ks_blk = rope(ks_in.reshape(B, S, G, D), pos).reshape(B, ns, SEL_LEN, G, D).transpose(0, 3, 1, 2, 4)
    vs_blk = vs_in.reshape(B, ns, SEL_LEN, G, D).transpose(0, 3, 1, 2, 4)
    pad = ((0, 0), (WINDOW, 0), (0, 0), (0, 0))
    kw_p = jnp.pad(rope(kw_in.reshape(B, S, G, D), pos), pad)
    vw_p = jnp.pad(vw_in.reshape(B, S, G, D), pad)
    gates = jax.nn.sigmoid(g_in + gate_b)

    cmp_start = jnp.arange(nc) * CMP_STRIDE
    cmp_end = cmp_start + CMP_LEN - 1
    sel_start = jnp.arange(ns) * SEL_LEN
    overlap = ((cmp_start[:, None] < sel_start[None, :] + SEL_LEN)
               & (cmp_end[:, None] >= sel_start[None, :])).astype(jnp.float32)
    scale = D ** -0.5
    nb = S // Q_BLOCK
    qb = q.reshape(B, nb, Q_BLOCK, G, P, D).transpose(1, 0, 2, 3, 4, 5)
    gb = gates.reshape(B, nb, Q_BLOCK, G, P, 3).transpose(1, 0, 2, 3, 4, 5)
    b_ix = jnp.arange(B)[:, None, None, None]
    g_ix = jnp.arange(G)[None, :, None, None]

    def one(args):
        qi, gt, bidx = args
        dt = qi.dtype
        qpos = bidx * Q_BLOCK + jnp.arange(Q_BLOCK)
        s_c = jnp.einsum('bqgpd,bngd->bgpqn', qi, kc).astype(jnp.float32) * scale
        p_c = masked_softmax(s_c, cmp_end[None, :] <= qpos[:, None])
        o_c = jnp.einsum('bgpqn,bngd->bqgpd', p_c.astype(dt), vc)
        imp = jnp.einsum('bgpqn,ns->bgqs', p_c, overlap)
        valid = sel_start[None, :] <= qpos[:, None]
        forced = (sel_start[None, :] == 0) | (sel_start[None, :] == ((qpos // SEL_LEN) * SEL_LEN)[:, None])
        score = jnp.where(valid, imp, -1.0)
        score = jnp.where(forced, score + FORCE_BONUS, score)
        top_val, top_idx = lax.top_k(score, n_top)
        k_sel = ks_blk[b_ix, g_ix, top_idx]
        v_sel = vs_blk[b_ix, g_ix, top_idx]
        kpos = top_idx[..., None] * SEL_LEN + jnp.arange(SEL_LEN)
        m_s = (kpos <= qpos[None, None, :, None, None]) & (top_val >= 0.0)[..., None]
        s_s = jnp.einsum('bqgpd,bgqkld->bgpqkl', qi, k_sel).astype(jnp.float32) * scale
        p_s = masked_softmax(s_s.reshape(B, G, P, Q_BLOCK, n_top * SEL_LEN),
                             m_s.reshape(B, G, 1, Q_BLOCK, n_top * SEL_LEN))
        o_s = jnp.einsum('bgpqkl,bgqkld->bqgpd',
                         p_s.reshape(B, G, P, Q_BLOCK, n_top, SEL_LEN).astype(dt), v_sel)
        k_win = lax.dynamic_slice_in_dim(kw_p, bidx * Q_BLOCK, Q_BLOCK + WINDOW, axis=1)
        v_win = lax.dynamic_slice_in_dim(vw_p, bidx * Q_BLOCK, Q_BLOCK + WINDOW, axis=1)
        wpos = bidx * Q_BLOCK - WINDOW + jnp.arange(Q_BLOCK + WINDOW)
        dist = qpos[:, None] - wpos[None, :]
        m_w = (wpos[None, :] >= 0) & (dist >= 0) & (dist < WINDOW)
        s_w = jnp.einsum('bqgpd,bkgd->bgpqk', qi, k_win).astype(jnp.float32) * scale
        p_w = masked_softmax(s_w, m_w)
        o_w = jnp.einsum('bgpqk,bkgd->bqgpd', p_w.astype(dt), v_win)
        out = gt[..., 0:1] * o_c + gt[..., 1:2] * o_s + gt[..., 2:3] * o_w
        return out.reshape(B, Q_BLOCK, NSA_HEADS * D)

    o = lax.map(one, (qb, gb, jnp.arange(nb)))
    return o.transpose(1, 0, 2, 3).reshape(B, S, NSA_HEADS * D)

def mixer(h, pos, w_in, conv_w, conv_b, wa, ba, wx, bx, lam, q_norm, w_uq, kv_norm, w_ukv,
          cmp_pos, cmp_w1, cmp_w2, gate_b, w_out):
    u = h @ w_in
    (x_lru, y_lru, q_dn, kv_dn, k_pe, q_n, kc, vc, ks, vs, kw, vw, g_n) = jnp.split(
        u, np.cumsum(IN_SPLITS)[:-1].tolist(), axis=-1)
    a_out = recurrent_group(x_lru, y_lru, conv_w, conv_b, wa, ba, wx, bx, lam)
    b_out = mla_group(q_dn, kv_dn, k_pe, pos, q_norm, w_uq, kv_norm, w_ukv)
    c_out = nsa_group(q_n, kc, vc, ks, vs, kw, vw, g_n, gate_b, pos, cmp_pos, cmp_w1, cmp_w2)
    return jnp.concatenate([a_out, b_out, c_out], axis=-1) @ w_out

def swiglu(x, wg, wu, wd):
    return (jax.nn.silu(x @ wg) * (x @ wu)) @ wd

def moe_ffn(x, router_w, wg, wu, wd):
    logits = (x @ router_w).astype(jnp.float32)
    top_val, top_idx = lax.top_k(logits, TOP_K)
    w = jax.nn.softmax(top_val, axis=-1)
    gate = jnp.sum(jax.nn.one_hot(top_idx, N_EXPERTS, dtype=jnp.float32) * w[..., None], axis=-2).astype(x.dtype)
    y = jnp.zeros_like(x)
    for e in range(N_EXPERTS):
        y = y + gate[..., e:e + 1] * swiglu(x, wg[e], wu[e], wd[e])
    return y

def setup_inputs(seed: int = 0) -> dict:
    key = jax.random.key(seed)
    keys = iter(jax.random.split(key, 32))
    f32 = jnp.float32

    def nrm(shape, fan):
        return jax.random.normal(next(keys), shape, f32) * fan ** -0.5

    def small(shape, s=0.01):
        return jax.random.normal(next(keys), shape, f32) * s

    def gain(shape):
        return 1.0 + small(shape)

    x = jax.random.normal(next(keys), (BATCH, SEQ, D_MODEL), f32)
    norm_mix = gain((DEPTH, D_MODEL))
    w_in = nrm((DEPTH, D_MODEL, IN_COLS), D_MODEL)
    lru_conv_w = nrm((DEPTH, CONV_WIDTH, LRU_WIDTH), CONV_WIDTH)
    lru_conv_b = small((DEPTH, LRU_WIDTH))
    lru_wa = nrm((DEPTH, LRU_BLOCKS, LRU_BLOCK_W, LRU_BLOCK_W), LRU_BLOCK_W)
    lru_ba = small((DEPTH, LRU_WIDTH))
    lru_wx = nrm((DEPTH, LRU_BLOCKS, LRU_BLOCK_W, LRU_BLOCK_W), LRU_BLOCK_W)
    lru_bx = small((DEPTH, LRU_WIDTH))
    a_c = jax.random.uniform(next(keys), (DEPTH, LRU_WIDTH), f32, minval=0.9, maxval=0.999)
    a0 = a_c ** (1.0 / LRU_C)
    lru_lambda = jnp.log(a0) - jnp.log1p(-a0)
    mla_q_norm = gain((DEPTH, MLA_Q_RANK))
    mla_w_uq = nrm((DEPTH, MLA_Q_RANK, MLA_HEADS * (MLA_NOPE + MLA_ROPE)), MLA_Q_RANK)
    mla_kv_norm = gain((DEPTH, MLA_KV_RANK))
    mla_w_ukv = nrm((DEPTH, MLA_KV_RANK, MLA_HEADS * (MLA_NOPE + MLA_V)), MLA_KV_RANK)
    nsa_cmp_pos = small((DEPTH, 2, CMP_LEN, NSA_HEAD_DIM), 0.02)
    nsa_cmp_w1 = nrm((DEPTH, 2, CMP_LEN * NSA_HEAD_DIM, CMP_HIDDEN), CMP_LEN * NSA_HEAD_DIM)
    nsa_cmp_w2 = nrm((DEPTH, 2, CMP_HIDDEN, NSA_HEAD_DIM), CMP_HIDDEN)
    nsa_gate_b = small((DEPTH, 3 * NSA_HEADS))
    w_out = nrm((DEPTH, D_MIX, D_MODEL), D_MIX)
    norm_ffn = gain((DEPTH, D_MODEL))
    ffn_w_gate = nrm((N_DENSE, D_MODEL, D_FF), D_MODEL)
    ffn_w_up = nrm((N_DENSE, D_MODEL, D_FF), D_MODEL)
    ffn_w_down = nrm((N_DENSE, D_FF, D_MODEL), D_FF)
    router_w = nrm((N_MOE, D_MODEL, N_EXPERTS), D_MODEL)
    moe_w_gate = nrm((N_MOE, N_EXPERTS, D_MODEL, D_FF_EXPERT), D_MODEL)
    moe_w_up = nrm((N_MOE, N_EXPERTS, D_MODEL, D_FF_EXPERT), D_MODEL)
    moe_w_down = nrm((N_MOE, N_EXPERTS, D_FF_EXPERT, D_MODEL), D_FF_EXPERT)
    norm_final = gain((D_MODEL,))
    return {'x': x, 'norm_mix': norm_mix, 'w_in': w_in, 'lru_conv_w': lru_conv_w, 'lru_conv_b': lru_conv_b,
            'lru_wa': lru_wa, 'lru_ba': lru_ba, 'lru_wx': lru_wx, 'lru_bx': lru_bx, 'lru_lambda': lru_lambda,
            'mla_q_norm': mla_q_norm, 'mla_w_uq': mla_w_uq, 'mla_kv_norm': mla_kv_norm, 'mla_w_ukv': mla_w_ukv,
            'nsa_cmp_pos': nsa_cmp_pos, 'nsa_cmp_w1': nsa_cmp_w1, 'nsa_cmp_w2': nsa_cmp_w2, 'nsa_gate_b': nsa_gate_b,
            'w_out': w_out, 'norm_ffn': norm_ffn, 'ffn_w_gate': ffn_w_gate, 'ffn_w_up': ffn_w_up,
            'ffn_w_down': ffn_w_down, 'router_w': router_w, 'moe_w_gate': moe_w_gate, 'moe_w_up': moe_w_up,
            'moe_w_down': moe_w_down, 'norm_final': norm_final}

def reference(x, norm_mix, w_in, lru_conv_w, lru_conv_b, lru_wa, lru_ba, lru_wx, lru_bx, lru_lambda,
              mla_q_norm, mla_w_uq, mla_kv_norm, mla_w_ukv, nsa_cmp_pos, nsa_cmp_w1, nsa_cmp_w2, nsa_gate_b,
              w_out, norm_ffn, ffn_w_gate, ffn_w_up, ffn_w_down, router_w, moe_w_gate, moe_w_up,
              moe_w_down, norm_final):
    pos = jnp.arange(x.shape[1])
    for l in range(DEPTH):
        h = rmsnorm(x, norm_mix[l])
        x = x + mixer(h, pos, w_in[l], lru_conv_w[l], lru_conv_b[l], lru_wa[l], lru_ba[l], lru_wx[l],
                      lru_bx[l], lru_lambda[l], mla_q_norm[l], mla_w_uq[l], mla_kv_norm[l], mla_w_ukv[l],
                      nsa_cmp_pos[l], nsa_cmp_w1[l], nsa_cmp_w2[l], nsa_gate_b[l], w_out[l])
        h = rmsnorm(x, norm_ffn[l])
        if l % 2 == 0:
            j = l // 2
            x = x + swiglu(h, ffn_w_gate[j], ffn_w_up[j], ffn_w_down[j])
        else:
            j = l // 2
            x = x + moe_ffn(h, router_w[j], moe_w_gate[j], moe_w_up[j], moe_w_down[j])
    return rmsnorm(x, norm_final)


_drawn_inputs = setup_inputs


def setup_inputs(seed=0):
    import zlib

    import numpy as np

    out = dict(_drawn_inputs(seed))
    spreads = {}
    factors = {'norm_mix': 3.092,
     'lru_ba': 6.315,
     'lru_bx': 8.0,
     'mla_q_norm': 8.0,
     'mla_kv_norm': 8.0,
     'nsa_gate_b': 21.184,
     'norm_final': 38.863,
     'nsa_cmp_pos': 8.0,
     'norm_ffn': 6.697}
    for name, (base, spread) in spreads.items():
        noise = np.random.default_rng([zlib.crc32(name.encode()), seed]).standard_normal(out[name].shape)
        drawn = base * np.exp(spread * noise) if base else spread * noise
        out[name] = __import__('jax').numpy.asarray(drawn.astype(out[name].dtype))
    for name, factor in factors.items():
        out[name] = (out[name] * factor).astype(out[name].dtype)
    return out
```

```python
from contextlib import ExitStack

import concourse.bass as bass
from concourse import mybir

ALU = mybir.AluOpType
ACT = mybir.ActivationFunctionType
F32 = mybir.dt.float32
AX_X = mybir.AxisListType.X

P = 128
T = 512
TT = T // P
DM = 1024
KC = DM // P
DEPTH = 2
EPS = 1e-6
LRU_W = 256
LC = LRU_W // P
CONV = 4
HEADS = 6
NOPE, ROPE, HD = 64, 32, 64
DQK = NOPE + ROPE
Q_RANK, KV_RANK = 192, 128
CMP_LEN, CMP_STRIDE = 32, 16
NCMP = (T - CMP_LEN) // CMP_STRIDE + 1
LP = CMP_LEN // 2
GATES = 3 * HEADS
TOKW = 2 * P + GATES
FE = 1408
FC = FE // P
NE = 8
NEG = -1.0e30
SCALE_MLA = float(DQK) ** -0.5
SCALE_NSA = float(HD) ** -0.5

FEAT = [("x", 0, P, 0), ("x", 1, P, 0), ("y", 0, P, 0), ("y", 1, P, 0),
        ("qdn", 0, P, 0), ("qdn", 1, Q_RANK - P, 0), ("kvdn", 0, P, 0), ("kpe", 0, ROPE, NOPE),
        ("q", 0, P, 0), ("q", 1, P, 0), ("q", 2, P, 0),
        ("kc", 0, P, 0), ("vc", 0, P, 0), ("ks", 0, P, 0), ("kw", 0, P, 0)]
NF = len(FEAT)
NW = NF + KC
WR = 4

PC = {}
_at = 0
for _n, _w in (("norm_mix", KC), ("norm_ffn", KC), ("conv_w", LC * CONV), ("conv_b", LC), ("ba", LC), ("bx", LC),
               ("lam", LC), ("q_norm", 2), ("kv_norm", 1), ("gate_b", GATES)):
    PC[_n] = _at
    _at += _w
NPP = _at

UNITS = []
for _c in range(3):
    for _h in (_c, _c + 3):
        UNITS += [("nsa", _h, 1), ("nsa", _h, 2)]
for _h in range(HEADS):
    UNITS.append(("mla", _h, 0))
NU = len(UNITS)


def unit_out(u):
    kind, h, br = UNITS[u]
    if kind == "nsa":
        return 5 + h % 3, 64 * (h // 3), br == 1, h >= 3 and br == 2
    return 2 + h // 2, 64 * (h % 2), True, h % 2 == 1


def trunk(nc, io, known):
    with ExitStack() as ctx:
        def sb(name, cols):
            return ctx.enter_context(nc.sbuf_tensor(name, [P, cols], F32))

        def sem(name):
            return ctx.enter_context(nc.semaphore(name))

        family_sem, raised, raised_to = {}, {}, {}

        def sem_of(family):
            if family not in family_sem:
                family_sem[family] = sem(family)
            return family_sem[family]

        def signal(family, *item, by=1):
            raised[family] = raised.get(family, 0) + by
            raised_to[(family,) + item] = raised[family]
            return sem_of(family), by

        def ready(family, *item):
            return sem_of(family), known[(family,) + item] if known else 1

        xT_ = sb("xT", KC * T)
        hT_ = sb("hT", KC * T)
        xT = xT_[:, :].rearrange("p (k t) -> p k t", k=KC)
        hT = hT_[:, :].rearrange("p (k t) -> p k t", k=KC)
        mixT = hT
        ident = sb("ident", P)
        rot64 = sb("rot64", P)
        rot32 = sb("rot32", ROPE)
        ones = sb("ones", P)
        diag = sb("diag", P)
        cmask = sb("cmask", TT * NCMP)[:, :].rearrange("p (i n) -> p i n", i=TT)
        crow = sb("crow", TT)
        tri = sb("tri", NE * NE)
        eps = sb("eps", 1)
        cos64, sin64 = sb("cos64", T), sb("sin64", T)
        cos32, sin32 = sb("cos32", T), sb("sin32", T)
        pp = sb("pp", DEPTH * NPP)
        gfin = sb("gfin", KC)
        small = sb("small", 256)
        wrt = sb("wrt", KC * NE)[:, :].rearrange("p (k e) -> p k e", k=KC)
        wring = sb("wring", WR * KC * P)[:, :].rearrange("p (s k m) -> p s k m", s=WR, k=KC)

        ARENA = 37600
        arena = sb("arena", ARENA)
        used = [0]

        def room(cols):
            a = used[0]
            used[0] += cols
            assert used[0] <= ARENA, used[0]
            return arena[:, a:a + cols]

        wtok = room(KC * TOKW).rearrange("p (k m) -> p k m", k=KC)
        xl = room(LC * (T + CONV - 1)).rearrange("p (c t) -> p c t", c=LC)
        yl = room(LC * T).rearrange("p (c t) -> p c t", c=LC)
        qdn = room(2 * T).rearrange("p (c t) -> p c t", c=2)
        kvdn = room(T)
        kpe = room(T)
        qn = room(3 * T).rearrange("p (c t) -> p c t", c=3)
        kcT, vcT, ksT, kwT = room(T), room(T), room(T), room(T)
        vtok = room(TT * TOKW).rearrange("p (i m) -> p i m", i=TT)
        wuq = room(2 * HEADS * DQK).rearrange("p (c m) -> p c m", c=2)
        wukv = room(2 * HEADS * HD).rearrange("p (v m) -> p v m", v=2)
        cw1_ = room(2 * LP * P)
        cw1 = cw1_.rearrange("p (s l m) -> p s l m", s=2, l=LP)
        PT = cw1_.rearrange("p (s k t) -> p s k t", s=2, k=TT)
        cw2 = room(2 * HD).rearrange("p (s m) -> p s m", s=2)
        cpos = room(2 * LP).rearrange("p (s l) -> p s l", s=2)
        lruw = room(2 * LC * P).rearrange("p (w c m) -> p w c m", w=2, c=LC)
        qh = room(HEADS * T).rearrange("p (h t) -> p h t", h=HEADS)
        kh = room(HEADS * T).rearrange("p (h t) -> p h t", h=HEADS)
        vm = room(TT * HEADS * HD).rearrange("p (i m) -> p i m", i=TT)
        NP_ = sum((i + 1) * P for i in range(TT))
        Pt = room(2 * NP_).rearrange("p (s n) -> p s n", s=2)
        OFF = [sum((j + 1) * P for j in range(i)) for i in range(TT)]
        shared_ = room(HEADS * T)
        PTc = shared_.rearrange("p (h t) -> p h t", h=HEADS)
        kcg = shared_[:, 0:2 * T].rearrange("p (g t) -> p g t", g=2)
        win = shared_[:, 2 * T:2 * T + LP * 2 * NCMP].rearrange("p (l g n) -> p l g n", l=LP, g=2)
        hid = room(2 * NCMP)
        kcs = room(NCMP)
        vcs = room(2 * HD)
        Sc = room(TT * HEADS * NCMP).rearrange("p (i h n) -> p i h n", i=TT, h=HEADS)
        tmp = room(4 * T).rearrange("p (s t) -> p s t", s=4)
        sq = room(2 * T).rearrange("p (s t) -> p s t", s=2)
        rms, rstd = room(T), room(T)
        sq_at = used[0]
        used[0] = 0
        gu = room(4 * 2 * KC * P).rearrange("p (s g k m) -> p s g k m", s=4, g=2, k=KC)
        wd = room(FC * DM).rearrange("p (f m) -> p f m", f=FC)
        actT = room(FC * T).rearrange("p (f t) -> p f t", f=FC)
        sg = room(2 * T).rearrange("p (s t) -> p s t", s=2)
        gateB_ = room(NE * T)
        gateB = gateB_.rearrange("p (e t) -> p e t", e=NE)
        lg = room(TT * NE).rearrange("p (i e) -> p i e", i=TT)
        gate = room(TT * NE).rearrange("p (i e) -> p i e", i=TT)
        cmp1 = room(TT * NE * NE).rearrange("p (i e j) -> p i e j", i=TT, e=NE)
        cmp2 = room(TT * NE * NE).rearrange("p (i e j) -> p i e j", i=TT, e=NE)
        assert used[0] <= sq_at - 4 * T, (used[0], sq_at)

        mx = small[:, 0:8]
        nmx = small[:, 8:16]
        ssum = small[:, 16:24].rearrange("p (s i) -> p s i", s=2)
        rsum = small[:, 24:32].rearrange("p (s i) -> p s i", s=2)
        cmx = small[:, 32:56].rearrange("p (i h) -> p i h", i=TT)
        csum = small[:, 56:80].rearrange("p (i h) -> p i h", i=TT)
        lc = small[:, 80:100]
        rmx = small[:, 100:104]
        rsm = small[:, 104:108]

        bank = [ctx.enter_context(nc.psum_tensor(f"bank{i}", [P, T], F32)) for i in range(8)]
        RING = 2
        score_bank = [bank[2], bank[3]]
        turn_bank = [bank[4], bank[5]]
        out_bank = [bank[6], bank[7]]
        ring_of = {}
        jobs = []

        ffn_sems = [{n: sem(f"{n}_{l}") for n in ("gate_mm", "up_mm", "silu", "act_ready", "down_mm",
                                                  "y_added", "wd_loaded")} for l in range(DEPTH)]
        gu_loaded = [[sem(f"gu_loaded{s}_{l}") for s in range(4)] for l in range(DEPTH)]
        EXPERTS = [2, NE]

        def x_ready(l, stage):
            if stage == 1:
                return ready("x_mixed", l, KC - 1)
            if l == 0:
                return ready("x_loaded", 0)
            return ffn_sems[l - 1]["y_added"], KC * (EXPERTS[l - 1] + 1)

        def par(l, name, i=0, n=1):
            a = l * NPP + PC[name] + i
            return pp[:, a:a + n]

        def rope_list(l):
            return ([("q", c, qn[:, c, :], 64) for c in range(3)] + [("kc", 0, kcT, 64), ("ks", 0, ksT, 64),
                    ("kw", 0, kwT, 64), ("kpe", 0, kpe[NOPE:DQK, :], 32)])

        def feat_index(name, c):
            return [(f[0], f[1]) for f in FEAT].index((name, c))

        def mla_rot(pe, take, l, h):
            b = take(("qrot", l, h), ("qrope", l, h))
            pe.wait_ge(*ready("uq", l, h))
            pe.matmul(b[NOPE:DQK, :], rot32[NOPE:DQK, :], qh[NOPE:DQK, h, :], start=True,
                      stop=True).then_inc(*signal("qrot_mm", l, h))

        block = ctx.enter_context(nc.Block())

        @block.tensor
        def _(pe):
            def take(job, reader):
                n = len(jobs)
                if n >= RING:
                    pe.wait_ge(*ready(*jobs[n - RING]))
                jobs.append(reader)
                ring_of[job] = n % RING
                return bank[n % RING]

            def norm_sum(tag, chunks, rows):
                b = take(("ssq",) + tag, ("rms",) + tag)
                for k in range(chunks):
                    pe.wait_ge(*ready("sq", *tag, k))
                    r = rows[k]
                    pe.matmul(b[:, :], ones[0:r, :], sq[0:r, k % 2, :], start=(k == 0),
                              stop=(k == chunks - 1)).then_inc(*signal("ssq", *tag, k))

            pe.wait_ge(*ready("consts"))
            for l in range(DEPTH):
                norm_sum((l, "mix"), KC, [P] * KC)
                for j, (name, c, rows, p0) in enumerate(FEAT):
                    b = take(("feat", l, j), ("feat", l, j))
                    J = NW * l + j
                    pe.wait_ge(*ready(f"wring{J % WR}", J))
                    for k in range(KC):
                        if j == 0:
                            pe.wait_ge(*ready("h", l, "mix", k))
                        mm = pe.matmul(b[p0:p0 + rows, :], wring[:, J % WR, k, 0:rows], hT[:, k, :],
                                       start=(k == 0), stop=(k == KC - 1))
                    mm.then_inc(*signal("w_used", J))
                pe.wait_ge(*ready("wtok", l))
                for i in range(TT):
                    b = take(("tok", l, i), ("tok", l, i))
                    for k in range(KC):
                        mm = pe.matmul(b[:, 0:TOKW], hT[:, k, i * P:(i + 1) * P], wtok[:, k, :],
                                       start=(k == 0), stop=(k == KC - 1))
                    mm.then_inc(*signal("tok_mm", l, i))
                for name, c, src, tab in rope_list(l):
                    b = take(("rot", l, name, c), ("roped", l, name, c))
                    pe.wait_ge(*ready("feat", l, feat_index(name, c)))
                    if name == "kpe":
                        mm = pe.matmul(b[NOPE:DQK, :], rot32[NOPE:DQK, :], src, start=True, stop=True)
                    else:
                        mm = pe.matmul(b[:, :], rot64[:, :], src, start=True, stop=True)
                    mm.then_inc(*signal("rot_mm", l, name, c))
                norm_sum((l, "q"), 2, [P, Q_RANK - P])
                norm_sum((l, "kv"), 1, [P])
                pe.wait_ge(*ready("mla_w", l))
                pe.wait_ge(*ready("latent", l, "q", 1))
                for h in range(HEADS):
                    b = take(("uq", l, h), ("uq", l, h))
                    pe.matmul(b[0:DQK, :], wuq[:, 0, h * DQK:(h + 1) * DQK], qdn[:, 0, :], start=True, stop=False)
                    pe.matmul(b[0:DQK, :], wuq[0:Q_RANK - P, 1, h * DQK:(h + 1) * DQK], qdn[0:Q_RANK - P, 1, :],
                              start=False, stop=True).then_inc(*signal("uq_mm", l, h))
                    if h >= 1:
                        mla_rot(pe, take, l, h - 1)
                mla_rot(pe, take, l, HEADS - 1)
                pe.wait_ge(*ready("latent", l, "kv", 0))
                for h in range(HEADS):
                    b = take(("uk", l, h), ("uk", l, h))
                    pe.matmul(b[0:NOPE, :], wukv[:, 0, h * HD:(h + 1) * HD], kvdn, start=True,
                              stop=True).then_inc(*signal("uk_mm", l, h))
                for i in range(TT):
                    b = take(("uv", l, i), ("uv", l, i))
                    pe.matmul(b[:, 0:HEADS * HD], kvdn[:, i * P:(i + 1) * P], wukv[:, 1, :], start=True,
                              stop=True).then_inc(*signal("uv_mm", l, i))
                pe.wait_ge(*ready("cmp_w", l))
                for s in range(2):
                    b = take(("hid", l, s), ("hid", l, s))
                    pe.wait_ge(*ready("win", l, s))
                    for lp in range(LP):
                        mm = pe.matmul(b[:, 0:2 * NCMP], cw1[:, s, lp, :], win[:, lp, :, :],
                                       start=(lp == 0), stop=(lp == LP - 1))
                    mm.then_inc(*signal("hid_mm", l, s))
                    b = take(("cmp", l, s), ("cmp", l, s))
                    pe.wait_ge(*ready("hid", l, s))
                    for g in range(2):
                        if s == 0:
                            mm = pe.matmul(b[g * HD:(g + 1) * HD, 0:NCMP], cw2[:, 0, :],
                                           hid[:, g * NCMP:(g + 1) * NCMP], start=True, stop=True)
                        else:
                            mm = pe.matmul(b[0:NCMP, g * HD:(g + 1) * HD], hid[:, g * NCMP:(g + 1) * NCMP],
                                           cw2[:, 1, :], start=True, stop=True)
                    mm.then_inc(*signal("cmp_mm", l, s))
                pe.wait_ge(*ready("cmp", l, 0))
                pe.wait_ge(*ready("roped", l, "q", 2))
                for i in range(TT):
                    for g in range(2):
                        b = take(("sc", l, i, g), ("sc", l, i, g))
                        for c in range(3):
                            mm = pe.matmul(b[:, c * NCMP:(c + 1) * NCMP], qn[g * HD:(g + 1) * HD, c, i * P:(i + 1) * P],
                                           kcs[g * HD:(g + 1) * HD, :], start=True, stop=True)
                        mm.then_inc(*signal("sc_mm", l, i, g))
                pe.wait_ge(*ready("lru_w", l))
                for c in range(LC):
                    pe.wait_ge(*ready("conv", l, c))
                    for w in range(2):
                        b = take(("lru", l, c, w), ("lru", l, c, w))
                        pe.matmul(b[:, :], lruw[:, w, c, :], tmp[:, c, :], start=True,
                                  stop=True).then_inc(*signal("lru_mm", l, c, w))
                pe.wait_ge(*ready("pc", l))
                for h in range(HEADS):
                    b = take(("pct", l, h), ("pct", l, h))
                    for i in range(TT):
                        mm = pe.transpose(b[0:NCMP, i * P:(i + 1) * P], Sc[:, i, h, :], ident[:, :])
                    mm.then_inc(*signal("pct_mm", l, h))

                def scores(u):
                    kind, h, br = UNITS[u]
                    if u == 0:
                        pe.wait_ge(*ready("roped", l, "ks", 0))
                        pe.wait_ge(*ready("roped", l, "kw", 0))
                    if kind == "mla" and h == 0:
                        pe.wait_ge(*ready("roped", l, "kpe", 0))
                        pe.wait_ge(*ready("uk", l, HEADS - 1))
                        pe.wait_ge(*ready("qrope", l, HEADS - 1))
                    for i in range(TT):
                        n = u * TT + i
                        if n >= 2:
                            pe.wait_ge(*ready("p", l, n - 2))
                        N = (i + 1) * P
                        if kind == "nsa":
                            g = h // 3
                            lo, hi = g * HD, (g + 1) * HD
                            q, k = qn[lo:hi, h % 3, i * P:N], (ksT if br == 1 else kwT)[lo:hi, 0:N]
                        else:
                            q, k = qh[0:DQK, h, i * P:N], kh[0:DQK, h, 0:N]
                        pe.matmul(score_bank[n % 2][:, 0:N], q, k, start=True,
                                  stop=True).then_inc(*signal("s_mm", l, n))

                def values(u):
                    kind, h, br = UNITS[u]
                    chunk, p0, opens, closes = unit_out(u)
                    for i in range(TT):
                        n = u * TT + i
                        pe.wait_ge(*ready("pn", l, n))
                        if n >= 2:
                            pe.wait_ge(*ready("pt", l, n - 2))
                        for kb in range(i + 1):
                            mm = pe.transpose(turn_bank[n % 2][:, kb * P:(kb + 1) * P],
                                              Pt[:, u % 2, OFF[i] + kb * P:OFF[i] + (kb + 1) * P], ident[:, :])
                        mm.then_inc(*signal("pt_mm", l, n))
                    ob = out_bank[chunk % 2]
                    if opens and p0 == 0:
                        before = {5: None, 6: None, 7: 5, 2: 6, 3: 7, 4: 2}[chunk]
                        if before is not None:
                            pe.wait_ge(*ready("mix", l, before))
                    if opens and kind == "nsa":
                        pe.wait_ge(*ready("pct", l, h))
                        g = h // 3
                        pe.matmul(ob[p0:p0 + HD, :], vcs[0:NCMP, g * HD:(g + 1) * HD], PTc[0:NCMP, h, :],
                                  start=True, stop=False)
                    pe.wait_ge(*ready("pt", l, u * TT + TT - 1))
                    last = kind == "mla" or br == 2
                    for kb in range(TT):
                        if kind == "nsa":
                            g = h // 3
                            a = (br - 1) * P + g * HD
                            v = vtok[:, kb, a:a + HD]
                        else:
                            v = vm[:, kb, h * HD:(h + 1) * HD]
                        mm = pe.matmul(ob[p0:p0 + HD, kb * P:T], v, PT[:, u % 2, kb, kb * P:T],
                                       start=(kb == 0 and kind == "mla"), stop=(last and kb == TT - 1))
                    mm.then_inc(*signal("pv", l, u))

                for u in range(NU):
                    scores(u)
                    if u >= 1:
                        values(u - 1)
                values(NU - 1)
                for m in range(KC):
                    J = NW * l + NF + m
                    b = take(("out", l, m), ("x_mixed", l, m))
                    pe.wait_ge(*ready(f"wring{J % WR}", J))
                    if m == 0:
                        pe.wait_ge(*ready("mix", l, 4))
                        pe.wait_ge(*ready("lru_out", l, LC - 1))
                    for k in range(KC):
                        mm = pe.matmul(b[:, :], wring[:, J % WR, k, :], mixT[:, k, :], start=(k == 0),
                                       stop=(k == KC - 1))
                    mm.then_inc(*signal("w_used", J))
                norm_sum((l, "ffn"), KC, [P] * KC)
                pe.wait_ge(*ready("h", l, "ffn", KC - 1))
                if l == 1:
                    pe.wait_ge(*ready("router_w"))
                    b = take(("router", l), ("lg", l))
                    for i in range(TT):
                        for k in range(KC):
                            mm = pe.matmul(b[:, i * NE:(i + 1) * NE], hT[:, k, i * P:(i + 1) * P],
                                           wrt[:, k, :], start=(k == 0), stop=(k == KC - 1))
                    mm.then_inc(*signal("router_mm", l))
                    pe.wait_ge(*ready("gate", l))
                    for e in range(NE):
                        b = take(("gateb", l, e), ("gateb", l, e))
                        for i in range(TT):
                            mm = pe.matmul(b[:, i * P:(i + 1) * P], gate[:, i, e:e + 1].broadcast_to([P, P]),
                                           ident[:, :], start=True, stop=True)
                        mm.then_inc(*signal("gateb_mm", l, e))
                s = ffn_sems[l]
                pe.sem_inc(s["up_mm"], FC)
                pe.sem_inc(s["down_mm"], KC)
                pe.wait_ge(*ready(*jobs[-1]))
                pe.wait_ge(*ready(*jobs[-2]))
                with pe.Fori(0, EXPERTS[l]) as e:
                    for f in range(FC):
                        slot = f % 4
                        per = (FC - slot + 3) // 4
                        pe.wait_ge(gu_loaded[l][slot], e * (16 * per) + 16 * (f // 4 + 1))
                        before = f - 2 if f >= 2 else (FC - 1 - f) - FC
                        pe.wait_ge(s["act_ready"], e * FC + FC + before + 1)
                        for k in range(KC):
                            mm = pe.matmul(bank[2 * (f % 2)][:, :], gu[:, slot, 0, k, :], hT[:, k, :],
                                           start=(k == 0), stop=(k == KC - 1))
                        mm.then_inc(s["gate_mm"], 1)
                        for k in range(KC):
                            mm = pe.matmul(bank[2 * (f % 2) + 1][:, :], gu[:, slot, 1, k, :], hT[:, k, :],
                                           start=(k == 0), stop=(k == KC - 1))
                        mm.then_inc(s["up_mm"], 1)
                    pe.wait_ge(s["act_ready"], e * FC + 2 * FC)
                    pe.wait_ge(s["wd_loaded"], e * (16 * FC) + 16 * FC)
                    for m in range(KC):
                        pe.wait_ge(s["y_added"], e * KC + KC + m - 4 + 1)
                        for f in range(FC):
                            mm = pe.matmul(bank[4 + m % 4][:, :], wd[:, f, m * P:(m + 1) * P], actT[:, f, :],
                                           start=(f == 0), stop=(f == FC - 1))
                        mm.then_inc(s["down_mm"], 1)
                pe.wait_ge(s["y_added"], KC * (EXPERTS[l] + 1))
            norm_sum((DEPTH, "final"), KC, [P] * KC)

        @block.scalar
        def _(act):
            norms = []

            def norm_rms(tag, parts, width):
                for k, (src, r, wait) in enumerate(parts):
                    if wait is not None:
                        act.wait_ge(*wait)
                    if k >= 2:
                        act.wait_ge(*ready("ssq", *tag, k - 2))
                    act.activation(sq[0:r, k % 2, :], src, ACT.Square).then_inc(*signal("sq", *tag, k))
                act.wait_ge(*ready("ssq", *tag, len(parts) - 1))
                if norms:
                    act.wait_ge(*ready("rstd", *norms[-1]))
                norms.append(tag)
                act.activation(rms[:, :], bank[ring_of[("ssq",) + tag]][:, :], ACT.Sqrt, bias=eps[:, 0:1],
                               scale=1.0 / width).then_inc(*signal("rms", *tag))

            act.wait_ge(*ready("consts"))
            for l in range(DEPTH):
                act.wait_ge(*ready("lam_abs", l))
                act.activation(lc[:, 4:6], lc[:, 2:4], ACT.Exp, scale=-1.0).then_inc(*signal("lam_exp", l))
                norm_rms((l, "mix"), [(xT[:, k, :], P, x_ready(l, 0) if k == 0 else None) for k in range(KC)], DM)
                home = {"x": lambda c: xl[:, c, CONV - 1:], "y": lambda c: yl[:, c, :], "qdn": lambda c: qdn[:, c, :],
                        "kvdn": lambda c: kvdn, "kpe": lambda c: kpe, "q": lambda c: qn[:, c, :], "kc": lambda c: kcT,
                        "vc": lambda c: vcT, "ks": lambda c: ksT, "kw": lambda c: kwT}
                for j, (name, c, rows, p0) in enumerate(FEAT):
                    act.wait_ge(*ready("w_used", NW * l + j))
                    act.copy(home[name](c)[p0:p0 + rows, :],
                             bank[ring_of[("feat", l, j)]][p0:p0 + rows, :]).then_inc(*signal("feat", l, j))
                for i in range(TT):
                    act.wait_ge(*ready("tok_mm", l, i))
                    act.copy(vtok[:, i, :], bank[ring_of[("tok", l, i)]][:, 0:TOKW]).then_inc(*signal("tok", l, i))
                norm_rms((l, "q"), [(qdn[:, 0, :], P, ready("feat", l, NF - 1)),
                                    (qdn[0:Q_RANK - P, 1, :], Q_RANK - P, None)], Q_RANK)
                norm_rms((l, "kv"), [(kvdn, P, None)], KV_RANK)
                for h in range(HEADS):
                    act.wait_ge(*ready("uq_mm", l, h))
                    act.copy(qh[0:DQK, h, :], bank[ring_of[("uq", l, h)]][0:DQK, :]).then_inc(*signal("uq", l, h))
                for h in range(HEADS):
                    act.wait_ge(*ready("uk_mm", l, h))
                    act.copy(kh[0:NOPE, h, :], bank[ring_of[("uk", l, h)]][0:NOPE, :]).then_inc(*signal("uk", l, h))
                for i in range(TT):
                    act.wait_ge(*ready("uv_mm", l, i))
                    act.copy(vm[:, i, :], bank[ring_of[("uv", l, i)]][:, 0:HEADS * HD]).then_inc(*signal("uv", l, i))
                for s in range(2):
                    act.wait_ge(*ready("hid_mm", l, s))
                    if s == 1:
                        act.wait_ge(*ready("cmp_mm", l, 0))
                    act.activation(hid, bank[ring_of[("hid", l, s)]][:, 0:2 * NCMP],
                                   ACT.Gelu_apprx_tanh).then_inc(*signal("hid", l, s))
                    act.wait_ge(*ready("cmp_mm", l, s))
                    b = bank[ring_of[("cmp", l, s)]]
                    if s == 0:
                        act.copy(kcs, b[:, 0:NCMP]).then_inc(*signal("cmp", l, s))
                    else:
                        act.copy(vcs[0:NCMP, :], b[0:NCMP, 0:2 * HD]).then_inc(*signal("cmp", l, s))
                for c in range(LC):
                    ins = act.activation(yl[:, c, :], yl[:, c, :], ACT.Gelu_apprx_tanh)
                ins.then_inc(*signal("gelu_y", l))
                act.wait_ge(*ready("gate_sum", l))
                act.activation(vtok[:, :, 2 * P:], vtok[:, :, 2 * P:], ACT.Sigmoid).then_inc(*signal("gates", l))
                for c in range(LC):
                    act.wait_ge(*ready("lru_mm", l, c, 0))
                    if c == 0:
                        act.wait_ge(*ready("latent", l, "kv", 0))
                    act.activation(sq[:, c, :], bank[ring_of[("lru", l, c, 0)]][:, :], ACT.Sigmoid,
                                   bias=par(l, "ba", c)).then_inc(*signal("lru", l, c, 0))
                    act.wait_ge(*ready("lru_mm", l, c, 1))
                    act.activation([rms, rstd][c], bank[ring_of[("lru", l, c, 1)]][:, :], ACT.Sigmoid,
                                   bias=par(l, "bx", c)).then_inc(*signal("lru", l, c, 1))
                act.wait_ge(*ready("decay", l))
                act.wait_ge(*ready("lru", l, LC - 1, 1))
                for c in range(LC):
                    act.activation(xl[:, c, 0:T], sq[:, c, :], ACT.Exp, scale=lc[:, 10 + c:11 + c])
                    act.activation(tmp[:, 2 + c, :], sq[:, c, :], ACT.Tanh,
                                   scale=lc[:, 12 + c:13 + c]).then_inc(*signal("lru_tanh", l, c))
                act.wait_ge(*ready("sc_sub", l))
                act.activation(Sc, Sc, ACT.Exp, scale=SCALE_NSA).then_inc(*signal("sc_exp", l))
                for c in range(LC):
                    act.wait_ge(*ready("lru_quot", l, c))
                    act.activation(tmp[:, 2 + c, :], tmp[:, 2 + c, :], ACT.Sqrt,
                                   scale=2.0).then_inc(*signal("lru_root", l, c))
                for h in range(HEADS):
                    act.wait_ge(*ready("pct_mm", l, h))
                    act.copy(PTc[0:NCMP, h, :], bank[ring_of[("pct", l, h)]][0:NCMP, :]).then_inc(*signal("pct", l, h))

                def exps(u):
                    if u >= 2:
                        act.wait_ge(*ready("pt_mm", l, (u - 2) * TT + TT - 1))
                        act.wait_ge(*ready("scale", l, u - 2))
                    for i in range(TT):
                        n = u * TT + i
                        N = (i + 1) * P
                        act.wait_ge(*ready("nmx", l, n))
                        act.activation(Pt[:, u % 2, OFF[i]:OFF[i] + N], score_bank[n % 2][:, 0:N], ACT.Exp,
                                       bias=nmx[:, n % 8:n % 8 + 1],
                                       scale=SCALE_NSA if UNITS[u][0] == "nsa" else SCALE_MLA,
                                       accum_out=ssum[:, u % 2, i:i + 1]).then_inc(*signal("p", l, n))

                def turned(u):
                    if u >= 2:
                        act.wait_ge(*ready("pv", l, u - 2))
                    for i in range(TT):
                        n = u * TT + i
                        act.wait_ge(*ready("pt_mm", l, n))
                        act.copy(PT[:, u % 2, 0:i + 1, i * P:(i + 1) * P],
                                 turn_bank[n % 2][:, 0:(i + 1) * P].rearrange("p (k q) -> p k q", q=P)
                                 ).then_inc(*signal("pt", l, n))

                for u in range(NU):
                    exps(u)
                    if u >= 1:
                        turned(u - 1)
                turned(NU - 1)
                norm_rms((l, "ffn"), [(xT[:, k, :], P, ready("x_mixed", l, k)) for k in range(KC)], DM)
                if l == 1:
                    act.wait_ge(*ready("lg_sub", l))
                    act.activation(lg, lg, ACT.Exp).then_inc(*signal("lg_exp", l))
                    for e in range(NE):
                        act.wait_ge(*ready("gateb_mm", l, e))
                        act.copy(gateB[:, e, :], bank[ring_of[("gateb", l, e)]][:, :]).then_inc(*signal("gateb", l, e))
                s = ffn_sems[l]
                with act.Fori(0, EXPERTS[l]) as e:
                    for f in range(FC):
                        act.wait_ge(s["gate_mm"], e * FC + f + 1)
                        before = f - 2 if f >= 2 else (FC - 1 - f) - FC
                        act.wait_ge(s["act_ready"], e * FC + FC + before + 1)
                        act.activation(sg[:, f % 2, :], bank[2 * (f % 2)][:, :], ACT.Silu).then_inc(s["silu"], 1)
            norm_rms((DEPTH, "final"), [(xT[:, k, :], P, x_ready(DEPTH, 0) if k == 0 else None)
                                        for k in range(KC)], DM)

        @block.vector
        def _(dve):
            chained = sem("dve_chained")
            chain = [0]

            def link(ins):
                chain[0] += 1
                ins.then_inc(chained, 1)
                dve.wait_ge(chained, chain[0])

            def normed(tag, parts, name):
                dve.wait_ge(*ready("rms", *tag))
                dve.reciprocal(rstd, rms).then_inc(*signal("rstd", *tag))
                dve.wait_ge(*ready("rstd", *tag))
                for k, (dst, src, gain, r) in enumerate(parts):
                    dve.scalar_tensor_tensor(out=dst, in0=src, scalar=gain, in1=rstd[0:r, :], op0=ALU.mult,
                                             op1=ALU.mult).then_inc(*signal(name, *tag, k))

            def rope(dst, src, rotated, cos, sin, a, b, label):
                link(dve.tensor_tensor(a, src, cos, ALU.mult))
                link(dve.tensor_tensor(b, rotated, sin, ALU.mult))
                if dst.shape != a.shape:
                    a, b = (v.unsqueeze(1).broadcast_to(list(dst.shape)) for v in (a, b))
                dve.tensor_tensor(dst, a, b, ALU.add).then_inc(*signal(*label))

            dve.wait_ge(*ready("consts"))
            for l in range(DEPTH):
                y, ay, e_, w, w2, p_, dneg, dpos = (lc[:, 2 * i:2 * i + 2] for i in range(8))
                if l > 0:
                    dve.wait_ge(*ready("lru_tanh", l - 1, LC - 1))
                link(dve.tensor_scalar(y, par(l, "lam", 0, LC), -1.0, None, ALU.mult))
                dve.tensor_tensor(ay, y, par(l, "lam", 0, LC), ALU.max).then_inc(*signal("lam_abs", l))
                dve.wait_ge(*ready("lam_exp", l))
                link(dve.tensor_scalar(w, e_, 2.0, None, ALU.add))
                link(dve.reciprocal(w, w))
                link(dve.tensor_tensor(w, w, e_, ALU.mult))
                link(dve.tensor_tensor(w2, w, w, ALU.mult))
                link(dve.tensor_scalar(p_, w2, 1.0 / 19, 1.0 / 17, ALU.mult, ALU.add))
                for n in range(15, 0, -2):
                    link(dve.tensor_tensor(p_, p_, w2, ALU.mult))
                    link(dve.tensor_scalar(p_, p_, 1.0 / n, None, ALU.add))
                link(dve.tensor_tensor(p_, p_, w, ALU.mult))
                link(dve.tensor_scalar(p_, p_, 16.0, None, ALU.mult))
                link(dve.tensor_scalar(y, y, 0.0, 8.0, ALU.max, ALU.mult))
                link(dve.tensor_tensor(dpos, y, p_, ALU.add))
                link(dve.tensor_scalar(lc[:, 10:12], dpos, -1.0, None, ALU.mult))
                dve.tensor_copy(lc[:, 12:14], dpos).then_inc(*signal("decay", l))

                normed((l, "mix"), [(hT[:, k, :], xT[:, k, :], par(l, "norm_mix", k), P) for k in range(KC)], "h")
                dve.wait_ge(*ready("feat", l, 1))
                link(dve.memset(xl[:, :, 0:CONV - 1], 0.0))
                for c in range(LC):
                    link(dve.tensor_scalar(tmp[:, c, :], xl[:, c, 0:T], par(l, "conv_w", c * CONV),
                                           par(l, "conv_b", c), ALU.mult, ALU.add))
                    for k in range(1, CONV):
                        ins = dve.scalar_tensor_tensor(out=tmp[:, c, :], in0=xl[:, c, k:k + T],
                                                       scalar=par(l, "conv_w", c * CONV + k), in1=tmp[:, c, :],
                                                       op0=ALU.mult, op1=ALU.add)
                        if k < CONV - 1:
                            link(ins)
                    ins.then_inc(*signal("conv", l, c))
                dve.wait_ge(*ready("tok", l, TT - 1))
                dve.tensor_tensor(vtok[:, :, 2 * P:], vtok[:, :, 2 * P:],
                                  par(l, "gate_b", 0, GATES).unsqueeze(1).broadcast_to([P, TT, GATES]),
                                  ALU.add).then_inc(*signal("gate_sum", l))
                for name, c, src, tab in rope_list(l):
                    dve.wait_ge(*ready("rot_mm", l, name, c))
                    b = bank[ring_of[("rot", l, name, c)]]
                    if name == "kpe":
                        rows = slice(NOPE, DQK)
                        rope(kh[rows, :, :], src, b[rows, :], cos32[rows, :], sin32[rows, :], tmp[rows, 2, :],
                             tmp[rows, 3, :], ("roped", l, name, c))
                    else:
                        rope(src, src, b[:, :], cos64[:, :], sin64[:, :], tmp[:, 2, :], tmp[:, 3, :],
                             ("roped", l, name, c))
                    dve.wait_ge(*ready("roped", l, name, c))
                normed((l, "q"), [(qdn[:, 0, :], qdn[:, 0, :], par(l, "q_norm", 0), P),
                                  (qdn[0:Q_RANK - P, 1, :], qdn[0:Q_RANK - P, 1, :],
                                   par(l, "q_norm", 1)[0:Q_RANK - P, :], Q_RANK - P)], "latent")
                dve.wait_ge(*ready("latent", l, "q", 1))
                normed((l, "kv"), [(kvdn, kvdn, par(l, "kv_norm"), P)], "latent")
                for h in range(HEADS):
                    rows = slice(NOPE, DQK)
                    dve.wait_ge(*ready("qrot_mm", l, h))
                    b = bank[ring_of[("qrot", l, h)]]
                    rope(qh[rows, h, :], qh[rows, h, :], b[rows, :], cos32[rows, :], sin32[rows, :],
                         tmp[rows, 2, :], tmp[rows, 3, :], ("qrope", l, h))
                    dve.wait_ge(*ready("qrope", l, h))
                for s in range(2):
                    dve.wait_ge(*ready("kcg", l, s))
                    if s == 1:
                        dve.wait_ge(*ready("hid_mm", l, 0))
                    for l1 in range(2):
                        v = kcg.rearrange("p g (n u) -> p g n u", u=CMP_STRIDE)[:, :, l1:l1 + NCMP, 0:CMP_STRIDE:2]
                        v = v.rearrange("p g n u -> p u g n")
                        pos = cpos[:, s, l1 * 8:l1 * 8 + 8].unsqueeze(2).unsqueeze(3).broadcast_to([P, 8, 2, NCMP])
                        ins = dve.tensor_tensor(win[:, l1 * 8:l1 * 8 + 8, :, :], v, pos, ALU.add)
                    ins.then_inc(*signal("win", l, s))
                for i in range(TT):
                    for g in range(2):
                        dve.wait_ge(*ready("sc_mm", l, i, g))
                        dve.tensor_tensor(Sc[:, i, 3 * g:3 * g + 3, :], bank[ring_of[("sc", l, i, g)]][:, 0:3 * NCMP]
                                          .rearrange("p (h n) -> p h n", h=3),
                                          cmask[:, i, :].unsqueeze(1).broadcast_to([P, 3, NCMP]),
                                          ALU.add).then_inc(*signal("sc", l, i, g))
                dve.wait_ge(*ready("sc", l, TT - 1, 1))
                link(dve.tensor_reduce(cmx, Sc, AX_X, ALU.max))
                dve.tensor_tensor(Sc, Sc, cmx.unsqueeze(3).broadcast_to([P, TT, HEADS, NCMP]),
                                  ALU.subtract).then_inc(*signal("sc_sub", l))
                for c in range(LC):
                    dve.wait_ge(*ready("lru_tanh", l, c))
                    link(dve.tensor_scalar(sq[:, c, :], tmp[:, 2 + c, :], 1.0, None, ALU.add))
                    link(dve.reciprocal(sq[:, c, :], sq[:, c, :]))
                    dve.tensor_tensor(tmp[:, 2 + c, :], tmp[:, 2 + c, :], sq[:, c, :],
                                      ALU.mult).then_inc(*signal("lru_quot", l, c))
                    ix = [rms, rstd][c]
                    link(dve.tensor_tensor(ix, ix, tmp[:, c, :], ALU.mult))
                dve.wait_ge(*ready("sc_exp", l))
                dve.wait_ge(*ready("gates", l))
                link(dve.tensor_reduce(csum, Sc, AX_X, ALU.add))
                link(dve.tensor_scalar(csum, csum, 1e-30, None, ALU.max))
                link(dve.reciprocal(csum, csum))
                gates = vtok[:, :, 2 * P:].rearrange("p i (h b) -> p i h b", b=3)
                link(dve.tensor_tensor(csum, csum, gates[:, :, :, 0], ALU.mult))
                link(dve.tensor_tensor(csum, csum, crow[:, :].unsqueeze(2).broadcast_to([P, TT, HEADS]), ALU.mult))
                dve.tensor_tensor(Sc, Sc, csum.unsqueeze(3).broadcast_to([P, TT, HEADS, NCMP]),
                                  ALU.mult).then_inc(*signal("pc", l))
                for c in range(LC):
                    dve.wait_ge(*ready("lru_root", l, c))
                    ix = [rms, rstd][c]
                    link(dve.tensor_tensor(ix, ix, tmp[:, 2 + c, :], ALU.mult))
                    link(dve.tensor_tensor_scan(tmp[:, c, :], xl[:, c, 0:T], ix, 0.0, ALU.mult, ALU.add))
                    dve.tensor_tensor(mixT[:, c, :], tmp[:, c, :], yl[:, c, :],
                                      ALU.mult).then_inc(*signal("lru_out", l, c))

                def maxima(u):
                    for i in range(TT):
                        n = u * TT + i
                        N = (i + 1) * P
                        dve.wait_ge(*ready("s_mm", l, n))
                        b = score_bank[n % 2]
                        link(dve.tensor_tensor(b[:, i * P:N], b[:, i * P:N], diag[:, :], ALU.add))
                        m = n % 8
                        link(dve.tensor_reduce(mx[:, m:m + 1], b[:, 0:N], AX_X, ALU.max))
                        dve.tensor_scalar(nmx[:, m:m + 1], mx[:, m:m + 1],
                                          -(SCALE_NSA if UNITS[u][0] == "nsa" else SCALE_MLA), None,
                                          ALU.mult).then_inc(*signal("nmx", l, n))

                def scales(u):
                    kind, h, br = UNITS[u]
                    dve.wait_ge(*ready("p", l, u * TT + TT - 1))
                    if u >= 2:
                        dve.wait_ge(*ready("pn", l, (u - 2) * TT + TT - 1))
                    r = rsum[:, u % 2, :]
                    link(dve.tensor_scalar(r, ssum[:, u % 2, :], 1e-30, None, ALU.max))
                    ins = dve.reciprocal(r, r)
                    if kind == "nsa":
                        link(ins)
                        ins = dve.tensor_tensor(r, r, gates[:, :, h, br], ALU.mult)
                    ins.then_inc(*signal("scale", l, u))

                def collect(u):
                    chunk, p0, opens, closes = unit_out(u)
                    if closes:
                        dve.wait_ge(*ready("pv", l, u))
                        dve.tensor_copy(mixT[:, chunk, :], out_bank[chunk % 2][:, :]).then_inc(*signal("mix", l, chunk))

                for u in range(NU):
                    maxima(u)
                    scales(u)
                    if u >= 1:
                        collect(u - 1)
                collect(NU - 1)
                for m in range(KC):
                    dve.wait_ge(*ready("w_used", NW * l + NF + m))
                    dve.tensor_tensor(xT[:, m, :], xT[:, m, :], bank[ring_of[("out", l, m)]][:, :],
                                      ALU.add).then_inc(*signal("x_mixed", l, m))
                dve.wait_ge(*ready("x_mixed", l, KC - 1))
                normed((l, "ffn"), [(hT[:, k, :], xT[:, k, :], par(l, "norm_ffn", k), P) for k in range(KC)], "h")
                if l == 1:
                    dve.wait_ge(*ready("router_mm", l))
                    dve.tensor_copy(lg, bank[ring_of[("router", l)]][:, 0:TT * NE]
                                    .rearrange("p (i e) -> p i e", i=TT)).then_inc(*signal("lg", l))
                    dve.wait_ge(*ready("lg", l))
                    full = [P, TT, NE, NE]
                    of_j, of_e = lg.unsqueeze(2).broadcast_to(full), lg.unsqueeze(3).broadcast_to(full)
                    link(dve.tensor_reduce(rmx, lg, AX_X, ALU.max))
                    link(dve.tensor_tensor(cmp1, of_j, of_e, ALU.is_gt))
                    link(dve.tensor_tensor(cmp2, of_j, of_e, ALU.is_equal))
                    link(dve.tensor_tensor(cmp2, cmp2, tri[:, :].rearrange("p (e j) -> p e j", e=NE).unsqueeze(1)
                                           .broadcast_to(full), ALU.mult))
                    link(dve.tensor_tensor(cmp1, cmp1, cmp2, ALU.add))
                    link(dve.tensor_reduce(gate, cmp1, AX_X, ALU.add))
                    link(dve.tensor_scalar(gate, gate, 1.5, None, ALU.is_lt))
                    dve.tensor_tensor(lg, lg, rmx.unsqueeze(2).broadcast_to([P, TT, NE]),
                                      ALU.subtract).then_inc(*signal("lg_sub", l))
                    dve.wait_ge(*ready("lg_exp", l))
                    link(dve.tensor_tensor(gate, gate, lg, ALU.mult))
                    link(dve.tensor_reduce(rsm, gate, AX_X, ALU.add))
                    link(dve.reciprocal(rsm, rsm))
                    dve.tensor_tensor(gate, gate, rsm.unsqueeze(2).broadcast_to([P, TT, NE]),
                                      ALU.mult).then_inc(*signal("gate", l))
                    dve.wait_ge(*ready("gateb", l, NE - 1))
                s = ffn_sems[l]
                gated = sem(f"gated_{l}")
                dve.sem_inc(s["act_ready"], FC)
                dve.sem_inc(s["y_added"], KC)
                with dve.Fori(0, EXPERTS[l]) as e:
                    dve.wait_ge(s["down_mm"], e * KC + KC)
                    for f in range(FC):
                        dve.wait_ge(s["silu"], e * FC + f + 1)
                        if l == 1:
                            dve.tensor_tensor(sg[:, f % 2, :], sg[:, f % 2, :],
                                              gateB_[:, bass.ts(e, T)], ALU.mult).then_inc(gated, 1)
                            dve.wait_ge(gated, e * FC + f + 1)
                        dve.wait_ge(s["up_mm"], e * FC + FC + f + 1)
                        dve.tensor_tensor(actT[:, f, :], sg[:, f % 2, :], bank[2 * (f % 2) + 1][:, :],
                                          ALU.mult).then_inc(s["act_ready"], 1)
                    dve.wait_ge(s["y_added"], e * KC + KC)
                    for m in range(KC):
                        dve.wait_ge(s["down_mm"], e * KC + KC + m + 1)
                        dve.tensor_tensor(xT[:, m, :], xT[:, m, :], bank[4 + m % 4][:, :],
                                          ALU.add).then_inc(s["y_added"], 1)
                dve.wait_ge(s["y_added"], KC * (EXPERTS[l] + 1))
            normed((DEPTH, "final"), [(hT[:, k, :], xT[:, k, :], gfin[:, k:k + 1], P) for k in range(KC)], "h")

        @block.gpsimd
        def _(pool):
            for l in range(DEPTH):
                for s, src in enumerate((kcT, vcT)):
                    if s == 0:
                        pool.wait_ge(*ready("roped", l, "kc", 0))
                    else:
                        pool.wait_ge(*ready("feat", l, feat_index("vc", 0)))
                        pool.wait_ge(*ready("win", l, 0))
                    for g in range(2):
                        rows = src[g * HD:(g + 1) * HD, :]
                        pool.dma_start(kcg[0:HD, g, :], rows).then_inc(*signal("kcg", l, s, by=16))
                        pool.dma_start(kcg[HD:P, g, 0:T - 1], rows[:, 1:T]).then_inc(*signal("kcg", l, s, by=16))
                for u in range(NU):
                    pool.wait_ge(*ready("scale", l, u))
                    for i in range(TT):
                        v = Pt[:, u % 2, OFF[i]:OFF[i] + (i + 1) * P]
                        pool.tensor_scalar(v, v, rsum[:, u % 2, i:i + 1], None,
                                           ALU.mult).then_inc(*signal("pn", l, u * TT + i))

        @block.sync
        def _(sp):
            for name, dst in (("ident", ident), ("rot64", rot64), ("rot32", rot32), ("ones", ones), ("diag", diag),
                              ("crow", crow), ("tri", tri), ("eps", eps), ("cos64", cos64), ("sin64", sin64),
                              ("cos32", cos32), ("sin32", sin32), ("pp", pp), ("gfin", gfin)):
                sp.dma_start(dst[:, :], io[name]).then_inc(*signal("consts", by=16))
            sp.dma_start(cmask, io["cmask"]).then_inc(*signal("consts", by=16))
            sp.dma_start(xT_[:, :], io["x"]).then_inc(*signal("x_loaded", 0, by=16))
            sp.dma_start(wrt, io["router"]).then_inc(*signal("router_w", by=16))

            def chunk(J):
                if J >= WR:
                    sp.wait_ge(*ready("w_used", J - WR))
                sp.dma_start(wring[:, J % WR, :, :], io["w_chunk"][J]).then_inc(*signal(f"wring{J % WR}", J, by=16))

            for J in range(WR):
                chunk(J)
            for l in range(DEPTH):
                if l > 0:
                    sp.wait_ge(*x_ready(l, 0))
                sp.dma_start(wtok, io["w_tok"][l]).then_inc(*signal("wtok", l, by=16))
                sp.dma_start(wuq, io["w_uq"][l]).then_inc(*signal("mla_w", l, by=16))
                sp.dma_start(wukv, io["w_ukv"][l]).then_inc(*signal("mla_w", l, by=16))
                sp.dma_start(cw1, io["cmp_w1"][l]).then_inc(*signal("cmp_w", l, by=16))
                sp.dma_start(cw2, io["cmp_w2"][l]).then_inc(*signal("cmp_w", l, by=16))
                sp.dma_start(cpos, io["cmp_pos"][l]).then_inc(*signal("cmp_w", l, by=16))
                sp.dma_start(lruw, io["lru_w"][l]).then_inc(*signal("lru_w", l, by=16))
                for J in range(NW * l + WR, NW * (l + 1)):
                    chunk(J)
                if l + 1 < DEPTH:
                    for J in range(NW * (l + 1), NW * (l + 1) + WR):
                        chunk(J)
                s = ffn_sems[l]
                sp.wait_ge(*ready("pv", l, NU - 1))
                sp.wait_ge(*ready("lru_out", l, LC - 1))
                w_gu, w_dn = io[f"gu{l}"], io[f"dn{l}"]
                with sp.Fori(0, EXPERTS[l]) as e:
                    for f in range(FC):
                        before = f - 4 if f >= 4 else (f + 8 if f < 3 else 7) - FC
                        sp.wait_ge(s["up_mm"], e * FC + FC + before + 1)
                        sp.dma_start(gu[:, f % 4, :, :, :], w_gu[bass.ds(e * FC + f, 1)]
                                     .rearrange("a p g k m -> p (a g) k m")).then_inc(gu_loaded[l][f % 4], 16)
                        if f == 3:
                            sp.wait_ge(s["down_mm"], e * KC + KC)
                            for n in range(FC):
                                sp.dma_start(wd[:, n, :], w_dn[bass.ds(e * FC + n, 1)]
                                             .rearrange("a p m -> p (a m)")).then_inc(s["wd_loaded"], 16)
            for k in range(KC):
                sp.wait_ge(*ready("h", DEPTH, "final", k))
                sp.dma_start(io["out"][:, k, :], hT[:, k, :]).then_inc(*signal("stored", by=16))
            sp.wait_ge(*ready("stored"))
        return raised_to


def tables(np):
    t = {}
    pos = np.arange(T, dtype=np.float32)

    def rope(d, rows, at):
        half = d // 2
        inv = (np.float32(10000.0) ** (-np.arange(half, dtype=np.float32) * np.float32(2.0) / np.float32(d)))
        ang = pos[:, None] * inv.astype(np.float32)[None, :]
        cos, sin = np.cos(ang).T, np.sin(ang).T
        c, s = np.zeros((P, T), np.float32), np.zeros((P, T), np.float32)
        for a in range(at, at + rows, d):
            c[a:a + half], c[a + half:a + d] = cos, cos
            s[a:a + half], s[a + half:a + d] = -sin, sin
        return c, s

    t["cos64"], t["sin64"] = rope(HD, P, 0)
    t["cos32"], t["sin32"] = rope(ROPE, ROPE, NOPE)
    t["ident"] = np.eye(P, dtype=np.float32)
    r = np.arange(P)
    t["rot64"] = (r[:, None] == (r ^ 32)[None, :]).astype(np.float32)
    t["rot32"] = ((r[:, None] % ROPE) == (np.arange(ROPE) ^ 16)[None, :]).astype(np.float32)
    t["ones"] = np.ones((P, P), np.float32)
    t["diag"] = np.where(r[None, :] <= r[:, None], 0.0, NEG).astype(np.float32)
    end = np.arange(NCMP) * CMP_STRIDE + CMP_LEN - 1
    q = np.arange(TT)[None, :] * P + r[:, None]
    t["cmask"] = np.where(end[None, None, :] <= q[:, :, None], 0.0, NEG).astype(np.float32)
    t["crow"] = (q >= CMP_LEN - 1).astype(np.float32)
    e = np.arange(NE)
    t["tri"] = np.tile((e[None, :] < e[:, None]).astype(np.float32).reshape(1, -1), (P, 1))
    t["eps"] = np.full((P, 1), EPS, np.float32)
    return t


def kernel(x, norm_mix, w_in, lru_conv_w, lru_conv_b, lru_wa, lru_ba, lru_wx, lru_bx, lru_lambda,
           mla_q_norm, mla_w_uq, mla_kv_norm, mla_w_ukv, nsa_cmp_pos, nsa_cmp_w1, nsa_cmp_w2, nsa_gate_b,
           w_out, norm_ffn, ffn_w_gate, ffn_w_up, ffn_w_down, router_w, moe_w_gate, moe_w_up,
           moe_w_down, norm_final):
    import numpy as np
    import concourse.bacc as bacc
    from concourse.bass_utils import run_bass_kernel_spmd

    A = np.asarray
    w_in, w_out = A(w_in), A(w_out)
    arrays = tables(np)

    def cols(v, rows=P):
        v = A(v)
        return np.moveaxis(v.reshape(v.shape[0], -1, rows), 2, 0)

    pp = np.zeros((P, DEPTH, NPP), np.float32)

    def put(name, v):
        pp[:v.shape[0], :, PC[name]:PC[name] + v.shape[2]] = v

    put("norm_mix", cols(norm_mix))
    put("norm_ffn", cols(norm_ffn))
    put("conv_w", A(lru_conv_w).reshape(DEPTH, CONV, LC, P).transpose(3, 0, 2, 1).reshape(P, DEPTH, LC * CONV))
    put("conv_b", cols(lru_conv_b))
    put("ba", cols(lru_ba))
    put("bx", cols(lru_bx))
    put("lam", cols(lru_lambda))
    put("q_norm", cols(A(mla_q_norm)[:, :P]))
    pp[:Q_RANK - P, :, PC["q_norm"] + 1] = A(mla_q_norm)[:, P:].T
    put("kv_norm", cols(mla_kv_norm))
    pp[:, :, PC["gate_b"]:PC["gate_b"] + GATES] = A(nsa_gate_b)[None]
    arrays["pp"] = pp.reshape(P, DEPTH * NPP)
    arrays["gfin"] = A(norm_final).reshape(KC, P).T
    arrays["x"] = A(x)[0].T.reshape(KC, P, T).transpose(1, 0, 2).reshape(P, KC * T)

    heads = [np.r_[c * HD:(c + 1) * HD, (c + 3) * HD:(c + 4) * HD] for c in range(3)]
    where = {"x": (0, P), "y": (LRU_W, P), "qdn": (512, P), "kvdn": (704, P), "kpe": (832, ROPE), "q": (864, P),
             "kc": (1248, P), "vc": (1376, P), "ks": (1504, P), "kw": (1760, P)}
    chunks = np.zeros((DEPTH * NW, P, KC, P), np.float32)
    for l in range(DEPTH):
        w = w_in[l].reshape(KC, P, -1).transpose(1, 0, 2)
        for j, (name, c, rows, p0) in enumerate(FEAT):
            at = where[name][0] + c * P
            idx = where["q"][0] + heads[c] if name == "q" else np.arange(at, at + rows)
            chunks[l * NW + j, :, :, :rows] = w[:, :, idx]
        order = np.concatenate([np.arange(5 * P)] + [5 * P + h for h in heads])
        wo = w_out[l][order].reshape(KC, P, KC, P).transpose(2, 1, 0, 3)
        chunks[l * NW + NF:(l + 1) * NW] = wo
    arrays["w_chunk"] = chunks
    tok = np.r_[1632:1760, 1888:2016, 2016:2034]
    arrays["w_tok"] = w_in[:, :, tok].reshape(DEPTH, KC, P, TOKW).transpose(0, 2, 1, 3)
    wuq = np.zeros((DEPTH, P, 2, HEADS * DQK), np.float32)
    wuq[:, :, 0] = A(mla_w_uq)[:, :P]
    wuq[:, :Q_RANK - P, 1] = A(mla_w_uq)[:, P:]
    arrays["w_uq"] = wuq
    arrays["w_ukv"] = A(mla_w_ukv).reshape(DEPTH, P, HEADS, 2, HD).transpose(0, 1, 3, 2, 4).reshape(DEPTH, P, 2, -1)
    arrays["cmp_w1"] = A(nsa_cmp_w1).reshape(DEPTH, 2, LP, P, P).transpose(0, 3, 1, 2, 4)
    arrays["cmp_w2"] = A(nsa_cmp_w2).transpose(0, 2, 1, 3)
    arrays["cmp_pos"] = A(nsa_cmp_pos).reshape(DEPTH, 2, LP, P).transpose(0, 3, 1, 2)
    lru = np.zeros((DEPTH, P, 2, LC, P), np.float32)
    for w, v in enumerate((A(lru_wa), A(lru_wx))):
        for n in range(4):
            a = 64 * (n % 2)
            lru[:, a:a + 64, w, n // 2, a:a + 64] = v[:, n]
    arrays["lru_w"] = lru
    arrays["router"] = A(router_w)[0].reshape(KC, P, NE).transpose(1, 0, 2)

    def gate_up(g, u):
        both = np.stack([A(g), A(u)], 0)
        both = both.reshape(2, -1, KC, P, FC, P)
        return both.transpose(1, 4, 3, 0, 2, 5).reshape(-1, P, 2, KC, P)

    dense = [A(v)[0].reshape(DM, 2, FE).transpose(1, 0, 2) for v in (ffn_w_gate, ffn_w_up)]
    arrays["gu0"] = gate_up(*dense)
    arrays["dn0"] = A(ffn_w_down)[0].reshape(-1, P, DM)
    arrays["gu1"] = gate_up(A(moe_w_gate)[0], A(moe_w_up)[0])
    arrays["dn1"] = A(moe_w_down)[0].reshape(-1, P, DM)

    def build(known):
        nc = bacc.Bacc("TRN2", target_bir_lowering=False, num_devices=1)
        io = {n: nc.dram_tensor(f"in_{n}", list(a.shape), F32, kind="ExternalInput").ap() for n, a in arrays.items()}
        io["out"] = nc.dram_tensor("out_x", [P, KC, T], F32, kind="ExternalOutput").ap()
        return nc, trunk(nc, io, known)

    _, counted = build({})
    nc, again = build(counted)
    assert again == counted
    r = run_bass_kernel_spmd(nc, [{f"in_{n}": np.ascontiguousarray(a, np.float32) for n, a in arrays.items()}],
                             core_ids=[0])
    out = r.results[0]["out_x"]
    return np.ascontiguousarray(out.transpose(1, 0, 2).reshape(DM, T).T[None])
```

```python
from contextlib import ExitStack

import concourse.bass as bass
from concourse import mybir

ALU = mybir.AluOpType
ACT = mybir.ActivationFunctionType
F32 = mybir.dt.float32
BF16 = mybir.dt.bfloat16
F16 = mybir.dt.float16
I32 = mybir.dt.int32
AX_X = mybir.AxisListType.X

P = 128
T = 512
TT = T // P
DM = 1024
KC = DM // P
DEPTH = 2
EPS = 1e-6
LRU_W = 256
LC = LRU_W // P
CONV = 4
HEADS = 6
NOPE, ROPE, HD = 64, 32, 64
DQK = NOPE + ROPE
Q_RANK, KV_RANK = 192, 128
CMP_LEN, CMP_STRIDE = 32, 16
NCMP = (T - CMP_LEN) // CMP_STRIDE + 1
LP = CMP_LEN // 2
GATES = 3 * HEADS
TOKW = 2 * P + GATES
FE = 1408
FC = FE // P
NE = 8
CAP = 192
ROUNDS = -(-T // CAP)
TAIL = CAP - P
ES, EP = 3, 4
LEAD = 2
NEG = -1.0e30
SCALE_MLA = float(DQK) ** -0.5
SCALE_NSA = float(HD) ** -0.5

FEAT = [("x", 0, P, 0), ("x", 1, P, 0), ("y", 0, P, 0), ("y", 1, P, 0),
        ("qdn", 0, P, 0), ("qdn", 1, Q_RANK - P, 0), ("kvdn", 0, P, 0), ("kpe", 0, ROPE, NOPE),
        ("q", 0, P, 0), ("q", 1, P, 0), ("q", 2, P, 0),
        ("kc", 0, P, 0), ("vc", 0, P, 0), ("ks", 0, P, 0), ("kw", 0, P, 0)]
NF = len(FEAT)
NW = NF + KC
WS, WR = 2, 3
SW, SX = 256.0, 16.0

PC = {}
_at = 0
for _n, _w in (("norm_mix", KC), ("norm_ffn", KC), ("conv_w", LC * CONV), ("conv_b", LC), ("ba", LC), ("bx", LC),
               ("lam", LC), ("q_norm", 2), ("kv_norm", 1), ("gate_b", GATES)):
    PC[_n] = _at
    _at += _w
NPP = _at

UNITS = []
for _c in range(3):
    for _h in (_c, _c + 3):
        UNITS += [("nsa", _h, 1), ("nsa", _h, 2)]
for _h in range(HEADS):
    UNITS.append(("mla", _h, 0))
NU = len(UNITS)


def unit_out(u):
    kind, h, br = UNITS[u]
    if kind == "nsa":
        return 5 + h % 3, 64 * (h // 3), br == 1, h >= 3 and br == 2
    return 2 + h // 2, 64 * (h % 2), True, h % 2 == 1


def trunk(nc, io, known):
    with ExitStack() as ctx:
        def sb(name, cols):
            return ctx.enter_context(nc.sbuf_tensor(name, [P, cols], F32))

        def sem(name):
            return ctx.enter_context(nc.semaphore(name))

        family_sem, raised, raised_to = {}, {}, {}

        def sem_of(family):
            if family not in family_sem:
                family_sem[family] = sem(family)
            return family_sem[family]

        def signal(family, *item, by=1):
            raised[family] = raised.get(family, 0) + by
            raised_to[(family,) + item] = raised[family]
            return sem_of(family), by

        def ready(family, *item):
            return sem_of(family), known[(family,) + item] if known else 1

        xT_ = sb("xT", KC * T)
        hh = sb("hh", KC * T // 2)[:, :].bitcast(BF16).rearrange("p (k t) -> p k t", k=KC)
        hl = sb("hl", KC * T // 2)[:, :].bitcast(F16).rearrange("p (k t) -> p k t", k=KC)
        hf = sb("hf", 2 * T)[:, :].rearrange("p (s t) -> p s t", s=2)
        xT = xT_[:, :].rearrange("p (k t) -> p k t", k=KC)
        mixh, mixl = hh, hl
        ident = sb("ident", P)
        identb = sb("identb", P // 2)[:, :].bitcast(BF16)
        identh = sb("identh", P // 2)[:, :].bitcast(F16)
        lower = sb("lower", P)
        rot64 = sb("rot64", P)
        rot32 = sb("rot32", ROPE)
        ones = sb("ones", P)
        diagb = sb("diagb", P // 2)[:, :].bitcast(BF16)
        cmask = sb("cmask", TT * NCMP)[:, :].rearrange("p (i n) -> p i n", i=TT)
        crow = sb("crow", TT)
        tri = sb("tri", NE * NE)
        eps = sb("eps", 1)
        cos64, sin64 = sb("cos64", T), sb("sin64", T)
        cos32, sin32 = sb("cos32", T), sb("sin32", T)
        pp = sb("pp", DEPTH * NPP)
        gfin = sb("gfin", KC)
        small = sb("small", 256)
        wrt_ = sb("wrt", KC * NE)[:, :]
        wrt_hi, wrt_lo = (sb(f"wrt_{n}", KC * NE // 2)[:, :].bitcast(F16)
                          .rearrange("p (k e) -> p k e", k=KC) for n in ("hi", "lo"))
        iota = sb("iota", ROUNDS * CAP)
        flag = ctx.enter_context(nc.sbuf_tensor("flag", [P, 1], I32))
        wstage = sb("wstage", WS * KC * P)[:, :].rearrange("p (s k m) -> p s k m", s=WS, k=KC)
        wring_hi, wring_lo = (sb(f"wring_{n}", WR * KC * P // 2)[:, :].bitcast(F16)
                              .rearrange("p (s k m) -> p s k m", s=WR, k=KC) for n in ("hi", "lo"))

        ARENA = 34720
        arena = sb("arena", ARENA)
        used = [0]

        def room(cols):
            a = used[0]
            used[0] += cols
            assert used[0] <= ARENA, used[0]
            return arena[:, a:a + cols]

        def room16(cols, dtype=F16):
            return room((cols + 1) // 2).bitcast(dtype)

        wtok_ = room(KC * TOKW)
        wtok = wtok_.rearrange("p (k m) -> p k m", k=KC)
        vm = wtok_[:, 0:TT * HEADS * HD].rearrange("p (i m) -> p i m", i=TT)
        xl = room(LC * (T + CONV - 1)).rearrange("p (c t) -> p c t", c=LC)
        yl = room(LC * T).rearrange("p (c t) -> p c t", c=LC)
        qdn = room(2 * T).rearrange("p (c t) -> p c t", c=2)
        latent_ = room(2 * T)
        kvdn, kpe = latent_[:, 0:T], latent_[:, T:2 * T]
        Sc = latent_[:, 0:TT * HEADS * NCMP].rearrange("p (i h n) -> p i h n", i=TT, h=HEADS)
        qn = room(3 * T).rearrange("p (c t) -> p c t", c=3)
        kcT, vcT, ksT, kwT = room(T), room(T), room(T), room(T)
        vtok = room(TT * TOKW).rearrange("p (i m) -> p i m", i=TT)
        wuq = room(2 * HEADS * DQK).rearrange("p (c m) -> p c m", c=2)
        wukv = room(2 * HEADS * HD).rearrange("p (v m) -> p v m", v=2)
        cw1_ = room(2 * LP * P)
        cw1 = cw1_.rearrange("p (s l m) -> p s l m", s=2, l=LP)
        PT = cw1_.rearrange("p (s k t) -> p s k t", s=2, k=TT)
        cw2 = room(2 * HD).rearrange("p (s m) -> p s m", s=2)
        cpos = room(2 * LP).rearrange("p (s l) -> p s l", s=2)
        lruw = room(2 * LC * P).rearrange("p (w c m) -> p w c m", w=2, c=LC)
        qh = room(HEADS * T).rearrange("p (h t) -> p h t", h=HEADS)
        kh_ = room(HEADS * T)
        kh = kh_.rearrange("p (h t) -> p h t", h=HEADS)
        wtok_hi, wtok_lo = (kh_[:, n * KC * TOKW // 2:(n + 1) * KC * TOKW // 2].bitcast(F16)
                            .rearrange("p (k m) -> p k m", k=KC) for n in range(2))
        NP_ = sum((i + 1) * P for i in range(TT))
        Pt = room(2 * NP_).rearrange("p (s n) -> p s n", s=2)
        diag = Pt[:, 0, 0:P]
        OFF = [sum((j + 1) * P for j in range(i)) for i in range(TT)]
        shared_ = room(HEADS * T)
        PTc = shared_.rearrange("p (h t) -> p h t", h=HEADS)
        kcg = shared_[:, 0:2 * T].rearrange("p (g t) -> p g t", g=2)
        win = shared_[:, 2 * T:2 * T + LP * 2 * NCMP].rearrange("p (l g n) -> p l g n", l=LP, g=2)
        hid = room(2 * NCMP)
        kcs = room(NCMP)
        vcs = room(2 * HD)
        tmp = room(4 * T).rearrange("p (s t) -> p s t", s=4)
        sq = room(2 * T).rearrange("p (s t) -> p s t", s=2)
        rms, rstd = room(T), room(T)
        sq_at = used[0] - 4 * T
        used[0] = 0
        GS = 3
        dw = room(WS * 3 * DM).rearrange("p (s n) -> p s n", s=WS)
        gu_hi_, gu_lo_ = (room16(GS * 2 * DM).rearrange("p (s n) -> p s n", s=GS) for _ in range(2))
        gu_hi, gu_lo = (v.rearrange("p s (g k m) -> p s g k m", g=2, k=KC) for v in (gu_hi_, gu_lo_))
        wd_hi, wd_lo = (room16(FC * DM).rearrange("p (f m) -> p f m", f=FC) for _ in range(2))
        act_hi = room16(FC * T, BF16).rearrange("p (f t) -> p f t", f=FC)
        act_lo = room16(FC * T).rearrange("p (f t) -> p f t", f=FC)
        sg = room(2 * T).rearrange("p (s t) -> p s t", s=2)
        af = hf
        assert used[0] <= sq_at, (used[0], sq_at)
        used[0] = 0
        ew = room(ES * 3 * DM).rearrange("p (s n) -> p s n", s=ES)
        ew_hi_, ew_lo_ = (room16(EP * 3 * DM).rearrange("p (s n) -> p s n", s=EP) for _ in range(2))
        ew_hi, ew_lo = (v.rearrange("p s (g k m) -> p s g k m", g=3, k=KC) for v in (ew_hi_, ew_lo_))
        posm_ = room(TT * NE)
        posm = posm_.rearrange("p (i e) -> p i e", i=TT)
        g3_ = room16(TT * NE * 4, BF16)
        g3 = g3_.rearrange("p (i e c) -> p i e c", i=TT, e=NE)
        lg = room(TT * NE).rearrange("p (i e) -> p i e", i=TT)
        gate = room(TT * NE).rearrange("p (i e) -> p i e", i=TT)
        sel = room(TT * NE).rearrange("p (i e) -> p i e", i=TT)
        cmp1 = room(TT * NE * NE).rearrange("p (i e j) -> p i e j", i=TT, e=NE)
        cmp2 = room(TT * NE * NE).rearrange("p (i e j) -> p i e j", i=TT, e=NE)
        tok_h = room16(TT * DM, BF16).rearrange("p (i d) -> p i d", i=TT)
        tok_l = room16(TT * DM).rearrange("p (i d) -> p i d", i=TT)
        assert used[0] <= sq_at, (used[0], sq_at)
        xg_h = room16(KC * CAP, BF16).rearrange("p (k n) -> p k n", k=KC)
        xg_l = room16(KC * CAP).rearrange("p (k n) -> p k n", k=KC)
        eact_h = room16(3 * CAP, BF16).rearrange("p (s n) -> p s n", s=3)
        eact_l = room16(3 * CAP).rearrange("p (s n) -> p s n", s=3)
        esg = room(2 * CAP).rearrange("p (s n) -> p s n", s=2)
        eaf = room(2 * CAP).rearrange("p (s n) -> p s n", s=2)
        hot = room16(TT * 2 * P, BF16).rearrange("p (i n) -> p i n", i=TT)
        hotT = room16(2 * T, BF16).rearrange("p (h t) -> p h t", h=2)
        yT_ = room(KC * CAP + 2 * P - CAP)
        yT = yT_[:, 0:KC * CAP].rearrange("p (m n) -> p m n", m=KC)
        y_hi = room16(2 * DM, BF16).rearrange("p (h d) -> p h d", h=2)
        y_lo = room16(2 * DM).rearrange("p (h d) -> p h d", h=2)
        gslot = room(2)
        outf = arena[:, 0:KC * T].rearrange("p (k t) -> p k t", k=KC)

        nmx = small[:, 8:16]
        ssum = small[:, 16:24].rearrange("p (s i) -> p s i", s=2)
        rsum = small[:, 24:32].rearrange("p (s i) -> p s i", s=2)
        cmx = small[:, 32:56].rearrange("p (i h) -> p i h", i=TT)
        csum = small[:, 56:80].rearrange("p (i h) -> p i h", i=TT)
        lc = small[:, 80:100]
        rmx = small[:, 100:104]
        rsm = small[:, 104:108]
        cmax = small[:, 108:109]

        bank = [ctx.enter_context(nc.psum_tensor(f"bank{i}", [P, T], F32)) for i in range(8)]
        RING = 2
        score_bank = [bank[2], bank[3], bank[0], bank[1]]
        turn_bank = [bank[4], bank[5]]
        out_bank = [bank[6], bank[7]]
        ring_of = {}
        jobs = []

        dense_sems = ("gate_mm", "up_mm", "silu", "product", "act_ready", "down_mm", "y_added", "hi_ready", "lo_ready",
                      "wd_hi_ready", "wd_lo_ready")
        D = {n: sem(f"dense_{n}") for n in dense_sems}
        dw_loaded = [sem(f"dense_w_loaded{i}") for i in range(WS)]
        HALVES = 2
        moe_sems = ("hi_ready", "lo_ready", "up_mm", "down_mm", "silu", "product", "act_ready", "y_out", "y_hi", "y_lo",
                    "turned_mm", "scatter_mm", "x_added", "hot", "gather_mm", "gathered", "hotT_mm", "hotT", "gslot_mm",
                    "gslot", "split")
        M = {n: sem(f"moe_{n}") for n in moe_sems}
        ew_loaded = [sem(f"moe_w_loaded{i}") for i in range(ES)]

        def x_ready(l, stage):
            if stage == 1:
                return ready("x_mixed", l, KC - 1)
            return (D["y_added"], KC * (HALVES + 1)) if l == 1 else ready("moe_added")

        def par(l, name, i=0, n=1):
            a = l * NPP + PC[name] + i
            return pp[:, a:a + n]

        def rope_list(l):
            return ([("q", c, qn[:, c, :], 64) for c in range(3)] + [("kc", 0, kcT, 64), ("ks", 0, ksT, 64),
                    ("kw", 0, kwT, 64), ("kpe", 0, kpe[NOPE:DQK, :], 32)])

        def feat_index(name, c):
            return [(f[0], f[1]) for f in FEAT].index((name, c))

        def mla_rot(pe, take, l, h):
            b = take(("qrot", l, h), ("qrope", l, h))
            pe.wait_ge(*ready("uq", l, h))
            pe.matmul(b[NOPE:DQK, :], rot32[NOPE:DQK, :], qh[NOPE:DQK, h, :], start=True,
                      stop=True).then_inc(*signal("qrot_mm", l, h))

        def dense(pe, product):
            for job in jobs[-RING:]:
                pe.wait_ge(*ready(*job))
            pe.sem_inc(D["up_mm"], FC)
            pe.sem_inc(D["down_mm"], KC)
            with pe.Fori(0, HALVES) as e:
                for f in range(FC):
                    slot = f % GS
                    pe.wait_ge(D["lo_ready"], e * FC + f + 1)
                    pe.wait_ge(D["product"], e * FC + FC + last_in(2, f) + 1)
                    for g, done in ((0, "gate_mm"), (1, "up_mm")):
                        for k in range(KC):
                            mm = product(bank[2 * (f % 2) + g][:, :], gu_hi[:, slot, g, k, :], gu_lo[:, slot, g, k, :],
                                         hh[:, k, :], hl[:, k, :], k == 0, k == KC - 1)
                        mm.then_inc(D[done], 1)
                pe.wait_ge(D["act_ready"], e * FC + FC)
                pe.wait_ge(D["wd_lo_ready"], e * FC + 2 * FC)
                for m in range(KC):
                    pe.wait_ge(D["y_added"], e * KC + KC + m - 4 + 1)
                    for f in range(FC):
                        mm = product(bank[4 + m % 4][:, :], wd_hi[:, f, m * P:(m + 1) * P],
                                     wd_lo[:, f, m * P:(m + 1) * P], act_hi[:, f, :], act_lo[:, f, :],
                                     f == 0, f == FC - 1)
                    mm.then_inc(D["down_mm"], 1)
            pe.wait_ge(D["y_added"], KC * (HALVES + 1))

        def route(pe, take, product):
            b = take(("router",), ("lg",))
            pe.wait_ge(*ready("router_lo"))
            for i in range(TT):
                t = slice(i * P, (i + 1) * P)
                for k in range(KC):
                    mm = product(b[:, i * NE:(i + 1) * NE], hh[:, k, t], hl[:, k, t], wrt_hi[:, k, :], wrt_lo[:, k, :],
                                 k == 0, k == KC - 1)
            mm.then_inc(*signal("router_mm"))
            for i in range(TT):
                for src, family, unit, dtype in ((hh, "tok_h", identb, BF16), (hl, "tok_l", identh, F16)):
                    b = take((family, i), (family, i))[:, :].bitcast(dtype)
                    for k in range(KC):
                        mm = pe.transpose(b[:, k * P:(k + 1) * P], src[:, k, i * P:(i + 1) * P], unit)
                    mm.then_inc(*signal(family + "_mm", i))
            b = take(("count",), ("places",))
            pe.wait_ge(*ready("sel"))
            for i in range(TT):
                for j in range(i + 1):
                    pe.matmul(b[:, i * NE:(i + 1) * NE], (lower if j == i else ones)[:, :], sel[:, j, :],
                              start=(j == 0), stop=(j == i))
            for j in range(TT):
                mm = pe.matmul(b[:, TT * NE:(TT + 1) * NE], ones[:, :], sel[:, j, :], start=(j == 0),
                               stop=(j == TT - 1))
            mm.then_inc(*signal("count_mm"))

        def last_in(slots, f):
            return f - slots if f >= slots else max(g for g in range(FC) if g % slots == f % slots) - FC

        def loaded(sems, n, f):
            slots = len(sems)
            per = (FC - f % slots + slots - 1) // slots
            return sems[f % slots], n * (16 * per) + 16 * (f // slots + 1)

        def experts_pe(pe, product):
            def other(j, reader, value):
                pe.wait_ge(M[reader], value)
                return bank[6 + j % 2]

            def gather(n, waits):
                pe.wait_ge(M["hot"], n * TT + TT)
                for j in range(KC):
                    b = other(j, *(waits[j] if j < 2 else ("gathered", n * KC + j - 1)))
                    for h in range(2):
                        k = 2 * (j // 2) + h
                        for i in range(TT):
                            mm = pe.matmul(b[:, h * CAP:(h + 1) * CAP], (tok_h, tok_l)[j % 2][:, i, k * P:(k + 1) * P],
                                           hot[:, i, 0:CAP], start=(i == 0), stop=(i == TT - 1))
                    mm.then_inc(M["gather_mm"], 1)

            def turn_hot(n, e, waits):
                for h in range(2):
                    b = other(h, *waits[h])[:, :].bitcast(BF16)
                    for i in range(TT):
                        mm = pe.transpose(b[:, i * P:(i + 1) * P], hot[:, i, h * P:(h + 1) * P], identb)
                    mm.then_inc(M["hotT_mm"], 1)
                for h in range(2):
                    b = other(h, "hotT", n * 2 + h + 1)
                    for i in range(TT):
                        mm = pe.matmul(b[:, 0:4], hot[:, i, h * P:(h + 1) * P], g3_of(i, e), start=(i == 0),
                                       stop=(i == TT - 1))
                    mm.then_inc(M["gslot_mm"], 1)

            def chunks(n):
                def down(f):
                    pe.wait_ge(M["act_ready"], n * FC + f + 1)
                    if f == 0:
                        pe.wait_ge(M["y_out"], n * 4 + 4)
                    for m in range(KC):
                        out = bank[2 + m // 2][:, (m % 2) * CAP:(m % 2 + 1) * CAP]
                        w = ew_hi[:, f % EP, 2, m, :], ew_lo[:, f % EP, 2, m, :]
                        x = eact_h[:, f % 3, :], eact_l[:, f % 3, :]
                        pe.matmul(out, w[0], x[0], start=(f == 0 and m % 2 == 0), stop=False, skip_group_check=True)
                        pe.matmul(out, w[0], x[1], start=False, stop=False, skip_group_check=True)
                        mm = pe.matmul(out, w[1], x[0], start=False, stop=(f == FC - 1), skip_group_check=True)
                    mm.then_inc(M["down_mm"], 1)

                for f in range(FC):
                    pe.wait_ge(M["lo_ready"], n * FC + FC + f + 1)
                    pe.wait_ge(M["product"], n * FC + FC + last_in(2, f) + 1)
                    for g in range(2):
                        for k in range(KC):
                            mm = product(bank[f % 2][:, g * CAP:(g + 1) * CAP], ew_hi[:, f % EP, g, k, :],
                                         ew_lo[:, f % EP, g, k, :], xg_h[:, k, :], xg_l[:, k, :], k == 0,
                                         k == KC - 1)
                    mm.then_inc(M["up_mm"], 1)
                    if f >= 1:
                        down(f - 1)
                down(FC - 1)

            def tail(n, waits):
                pe.wait_ge(M["y_out"], n * 4 + 8)
                j = 0
                for h in range(2):
                    for half in range(2):
                        b = other(j, *(waits[j] if j < 2 else ("y_lo", n * 4 + j - 1)))
                        for m in range(4):
                            a = (half * 4 + m) * CAP + h * P
                            mm = pe.transpose(b[:, m * P:(m + 1) * P], yT_[:, a:a + P], ident[:, :])
                        mm.then_inc(M["turned_mm"], 1)
                        j += 1
                pe.wait_ge(M["y_lo"], n * 4 + 4)
                pe.wait_ge(M["hotT"], n * 2 + 2)
                for m in range(KC):
                    b = other(m, *(("y_lo", n * 4 + 3 + m) if m < 2 else ("x_added", n * KC + m - 1)))
                    for h, w in ((0, P), (1, TAIL)):
                        for src in (y_hi, y_lo):
                            mm = pe.matmul(b[:, :], src[0:w, h, m * P:(m + 1) * P], hotT[0:w, h, :],
                                           start=(h == 0 and src is y_hi), stop=(h == 1 and src is y_lo))
                    mm.then_inc(M["scatter_mm"], 1)

            pe.sem_inc(M["down_mm"], FC)
            pe.wait_ge(*ready("routed"))
            gather(0, [("product", FC)] * 2)
            turn_hot(0, 0, [("gathered", KC - 1), ("gathered", KC)])
            with pe.Fori(0, NE - 1) as e:
                chunks(e)
                gather(e + 1, [("gslot", e * 2 + 1), ("gslot", e * 2 + 2)])
                tail(e, [("gathered", e * KC + 2 * KC - 1), ("gathered", e * KC + 2 * KC)])
                turn_hot(e + 1, e + 1, [("x_added", e * KC + KC - 1), ("x_added", e * KC + KC)])
            chunks(NE - 1)
            tail(NE - 1, [("gslot", 2 * NE - 1), ("gslot", 2 * NE)])
            over = pe.value_load(flag[0:1, 0:1])
            with pe.If(over > CAP):
                with pe.Fori(1, ROUNDS) as r:
                    with pe.Fori(0, NE) as e:
                        n = r * NE + e
                        gather(n, [("x_added", n * KC - 1), ("x_added", n * KC)])
                        turn_hot(n, e, [("gathered", n * KC + KC - 1), ("gathered", n * KC + KC)])
                        chunks(n)
                        tail(n, [("gslot", n * 2 + 1), ("gslot", n * 2 + 2)])

        def g3_of(i, e):
            a = (i * NE + e) * 4
            return g3_[:, bass.ds(a, 4)]

        def experts_act(act):
            def hi(n, f):
                act.wait_ge(*loaded(ew_loaded, n, f))
                act.wait_ge(M["down_mm"], n * FC + FC + last_in(EP, f) + 1)
                act.activation(ew_hi_[:, f % EP, :], ew[:, f % ES, :], ACT.Copy, scale=SW).then_inc(M["hi_ready"], 1)

            def gathered(n):
                for j in range(KC):
                    k = 2 * (j // 2)
                    act.wait_ge(M["gather_mm"], n * KC + j + 1)
                    act.copy((xg_h, xg_l)[j % 2][:, k:k + 2, :].rearrange("p k n -> p (k n)"),
                             bank[6 + j % 2][:, 0:2 * CAP]).then_inc(M["gathered"], 1)

            def hot_turned(n):
                for h, w in ((0, P), (1, TAIL)):
                    act.wait_ge(M["hotT_mm"], n * 2 + h + 1)
                    act.copy(hotT[0:w, h, :], bank[6 + h][:, :].bitcast(BF16)[0:w, 0:T]).then_inc(M["hotT"], 1)

            def silus(n, ahead):
                for f in range(FC):
                    act.wait_ge(M["up_mm"], n * FC + f + 1)
                    act.wait_ge(M["product"], n * FC + FC + last_in(2, f) + 1)
                    act.activation(esg[:, f % 2, :], bank[f % 2][:, 0:CAP], ACT.Silu,
                                   scale=1.0 / (SW * SX)).then_inc(M["silu"], 1)
                    if f + LEAD < FC:
                        hi(n, f + LEAD)
                    elif ahead:
                        hi(n + 1, f + LEAD - FC)

            def results(n):
                act.wait_ge(M["down_mm"], n * FC + 2 * FC)
                for j in range(4):
                    act.activation(yT[:, 2 * j:2 * j + 2, :].rearrange("p m n -> p (m n)"), bank[2 + j][:, 0:2 * CAP],
                                   ACT.Copy, scale=1.0 / SW).then_inc(M["y_out"], 1)

            def gated(n):
                act.wait_ge(M["gslot"], n * 2 + 2)
                for j in range(4):
                    h, half, w = j // 2, j % 2, (P, TAIL)[j // 2]
                    act.wait_ge(M["turned_mm"], n * 4 + j + 1)
                    act.activation(y_hi[0:w, h, half * T:(half + 1) * T], bank[6 + j % 2][0:w, :], ACT.Copy,
                                   scale=gslot[0:w, h:h + 1]).then_inc(M["y_hi"], 1)

            act.sem_inc(M["y_out"], 4)
            gathered(0)
            for f in range(LEAD):
                hi(0, f)
            hot_turned(0)
            with act.Fori(0, NE - 1) as e:
                silus(e, True)
                results(e)
                gathered(e + 1)
                gated(e)
                hot_turned(e + 1)
            silus(NE - 1, False)
            results(NE - 1)
            gated(NE - 1)
            over = act.value_load(flag[0:1, 0:1])
            with act.If(over > CAP):
                with act.Fori(1, ROUNDS) as r:
                    with act.Fori(0, NE) as e:
                        n = r * NE + e
                        gathered(n)
                        hot_turned(n)
                        for f in range(LEAD):
                            hi(n, f)
                        silus(n, False)
                        results(n)
                        gated(n)

        def experts_dve(dve):
            def remainder(n, f):
                dve.wait_ge(M["hi_ready"], n * FC + f + 1)
                dve.scalar_tensor_tensor(out=ew_lo_[:, f % EP, :], in0=ew[:, f % ES, :], scalar=SW,
                                         in1=ew_hi_[:, f % EP, :], op0=ALU.mult,
                                         op1=ALU.subtract).then_inc(M["lo_ready"], 1)

            def one_hot(n, e, r):
                for i in range(TT):
                    dve.tensor_scalar(hot[:, i, 0:CAP], iota[:, bass.ds(r * CAP, CAP)], posm_[:, bass.ds(i * NE + e, 1)],
                                      None, ALU.is_equal).then_inc(M["hot"], 1)

            def slot_gates(n):
                for h, w in ((0, P), (1, TAIL)):
                    dve.wait_ge(M["gslot_mm"], n * 2 + h + 1)
                    dve.tensor_reduce(gslot[0:w, h:h + 1], bank[6 + h][0:w, 0:3], AX_X, ALU.add).then_inc(M["gslot"], 1)

            def products(n, ahead):
                for f in range(FC):
                    dve.wait_ge(M["silu"], n * FC + f + 1)
                    if f >= 2:
                        dve.wait_ge(M["act_ready"], n * FC + f - 1)
                    dve.scalar_tensor_tensor(out=eaf[:, f % 2, :], in0=bank[f % 2][:, CAP:2 * CAP], scalar=1.0 / SW,
                                             in1=esg[:, f % 2, :], op0=ALU.mult,
                                             op1=ALU.mult).then_inc(M["product"], 1)
                    dve.wait_ge(M["product"], n * FC + FC + f + 1)
                    dve.tensor_copy(eact_h[:, f % 3, :], eaf[:, f % 2, :]).then_inc(M["split"], 1)
                    dve.wait_ge(M["split"], n * FC + f + 1)
                    dve.tensor_tensor(eact_l[:, f % 3, :], eaf[:, f % 2, :], eact_h[:, f % 3, :],
                                      ALU.subtract).then_inc(M["act_ready"], 1)
                    if f + LEAD < FC:
                        remainder(n, f + LEAD)
                    elif ahead:
                        remainder(n + 1, f + LEAD - FC)

            def y_remainders(n):
                for j in range(4):
                    h, half, w = j // 2, j % 2, (P, TAIL)[j // 2]
                    cols = slice(half * T, (half + 1) * T)
                    dve.wait_ge(M["y_hi"], n * 4 + j + 1)
                    dve.scalar_tensor_tensor(out=y_lo[0:w, h, cols], in0=bank[6 + j % 2][0:w, :],
                                             scalar=gslot[0:w, h:h + 1], in1=y_hi[0:w, h, cols], op0=ALU.mult,
                                             op1=ALU.subtract).then_inc(M["y_lo"], 1)

            def sums(n):
                for m in range(KC):
                    dve.wait_ge(M["scatter_mm"], n * KC + m + 1)
                    dve.scalar_tensor_tensor(out=xT[:, m, :], in0=bank[6 + m % 2][:, :], scalar=1.0 / SX,
                                             in1=xT[:, m, :], op0=ALU.mult, op1=ALU.add).then_inc(M["x_added"], 1)

            dve.sem_inc(M["product"], FC)
            dve.sem_inc(M["lo_ready"], FC)
            one_hot(0, 0, 0)
            remainder(0, 0)
            remainder(0, 1)
            slot_gates(0)
            with dve.Fori(0, NE - 1) as e:
                dve.wait_ge(M["gslot_mm"], e * 2 + 2)
                one_hot(e + 1, e + 1, 0)
                products(e, True)
                y_remainders(e)
                sums(e)
                dve.wait_ge(M["x_added"], e * KC + KC)
                slot_gates(e + 1)
            products(NE - 1, False)
            y_remainders(NE - 1)
            sums(NE - 1)
            dve.wait_ge(M["x_added"], NE * KC)
            over = dve.value_load(flag[0:1, 0:1])
            with dve.If(over > CAP):
                with dve.Fori(1, ROUNDS) as r:
                    with dve.Fori(0, NE) as e:
                        n = r * NE + e
                        dve.wait_ge(M["x_added"], n * KC)
                        one_hot(n, e, r)
                        remainder(n, 0)
                        remainder(n, 1)
                        slot_gates(n)
                        products(n, False)
                        y_remainders(n)
                        sums(n)
                dve.wait_ge(M["x_added"], ROUNDS * NE * KC)

        def experts_sp(sp):
            def load(n, e, f):
                sp.wait_ge(M["lo_ready"], n * FC + FC + last_in(ES, f) + 1)
                sp.dma_start(ew[:, f % ES, :], io["ew"][bass.ds(e * FC + f, 1)]
                             .rearrange("a p n -> p (a n)")).then_inc(ew_loaded[f % ES], 16)

            with sp.Fori(0, NE) as e:
                for f in range(FC):
                    load(e, e, f)
            sp.wait_ge(*ready("flag"))
            over = sp.value_load(flag[0:1, 0:1])
            with sp.If(over > CAP):
                with sp.Fori(1, ROUNDS) as r:
                    with sp.Fori(0, NE) as e:
                        for f in range(FC):
                            load(r * NE + e, e, f)

        block = ctx.enter_context(nc.Block())

        @block.tensor
        def _(pe):
            def take(job, reader):
                n = len(jobs)
                if n >= RING:
                    pe.wait_ge(*ready(*jobs[n - RING]))
                jobs.append(reader)
                ring_of[job] = n % RING
                return bank[n % RING]

            def norm_sum(tag, chunks, rows):
                b = take(("ssq",) + tag, ("rms",) + tag)
                for k in range(chunks):
                    pe.wait_ge(*ready("sq", *tag, k))
                    r = rows[k]
                    pe.matmul(b[:, :], ones[0:r, :], sq[0:r, k % 2, :], start=(k == 0),
                              stop=(k == chunks - 1)).then_inc(*signal("ssq", *tag, k))

            def product(out, w_hi, w_lo, x_hi, x_lo, first, last):
                pe.matmul(out, w_hi, x_hi, start=first, stop=False)
                pe.matmul(out, w_hi, x_lo, start=False, stop=False)
                return pe.matmul(out, w_lo, x_hi, start=False, stop=last)

            pe.wait_ge(*ready("first_consts"))
            for l in range(DEPTH):
                norm_sum((l, "mix"), KC, [P] * KC)
                for j, (name, c, rows, p0) in enumerate(FEAT):
                    b = take(("feat", l, j), ("feat", l, j))
                    J = NW * l + j
                    pe.wait_ge(*ready("w_lo", J))
                    for k in range(KC):
                        if j == 0:
                            pe.wait_ge(*ready("hl", l, "mix", k))
                        mm = product(b[p0:p0 + rows, :], wring_hi[:, J % WR, k, 0:rows],
                                     wring_lo[:, J % WR, k, 0:rows], hh[:, k, :], hl[:, k, :], k == 0, k == KC - 1)
                    mm.then_inc(*signal("w_used", J))
                pe.wait_ge(*ready("wtok_lo", l))
                for i in range(TT):
                    b = take(("tok", l, i), ("tok", l, i))
                    for k in range(KC):
                        t = slice(i * P, (i + 1) * P)
                        mm = product(b[:, 0:TOKW], hh[:, k, t], hl[:, k, t], wtok_hi[:, k, :], wtok_lo[:, k, :],
                                     k == 0, k == KC - 1)
                    mm.then_inc(*signal("tok_mm", l, i))
                if l == 0:
                    pe.wait_ge(*ready("consts"))
                    pe.wait_ge(*ready("identb"))
                for name, c, src, tab in rope_list(l):
                    b = take(("rot", l, name, c), ("roped", l, name, c))
                    pe.wait_ge(*ready("feat", l, feat_index(name, c)))
                    if name == "kpe":
                        mm = pe.matmul(b[NOPE:DQK, :], rot32[NOPE:DQK, :], src, start=True, stop=True)
                    else:
                        mm = pe.matmul(b[:, :], rot64[:, :], src, start=True, stop=True)
                    mm.then_inc(*signal("rot_mm", l, name, c))
                norm_sum((l, "q"), 2, [P, Q_RANK - P])
                norm_sum((l, "kv"), 1, [P])
                pe.wait_ge(*ready("mla_w", l))
                pe.wait_ge(*ready("latent", l, "q", 1))
                for h in range(HEADS):
                    b = take(("uq", l, h), ("uq", l, h))
                    pe.matmul(b[0:DQK, :], wuq[:, 0, h * DQK:(h + 1) * DQK], qdn[:, 0, :], start=True, stop=False)
                    pe.matmul(b[0:DQK, :], wuq[0:Q_RANK - P, 1, h * DQK:(h + 1) * DQK], qdn[0:Q_RANK - P, 1, :],
                              start=False, stop=True).then_inc(*signal("uq_mm", l, h))
                    if h >= 1:
                        mla_rot(pe, take, l, h - 1)
                mla_rot(pe, take, l, HEADS - 1)
                pe.wait_ge(*ready("latent", l, "kv", 0))
                for h in range(HEADS):
                    b = take(("uk", l, h), ("uk", l, h))
                    pe.matmul(b[0:NOPE, :], wukv[:, 0, h * HD:(h + 1) * HD], kvdn, start=True,
                              stop=True).then_inc(*signal("uk_mm", l, h))
                for i in range(TT):
                    b = take(("uv", l, i), ("uv", l, i))
                    pe.matmul(b[:, 0:HEADS * HD], kvdn[:, i * P:(i + 1) * P], wukv[:, 1, :], start=True,
                              stop=True).then_inc(*signal("uv_mm", l, i))
                pe.wait_ge(*ready("cmp_w", l))
                for s in range(2):
                    b = take(("hid", l, s), ("hid", l, s))
                    pe.wait_ge(*ready("win", l, s))
                    for lp in range(LP):
                        mm = pe.matmul(b[:, 0:2 * NCMP], cw1[:, s, lp, :], win[:, lp, :, :],
                                       start=(lp == 0), stop=(lp == LP - 1))
                    mm.then_inc(*signal("hid_mm", l, s))
                    b = take(("cmp", l, s), ("cmp", l, s))
                    pe.wait_ge(*ready("hid", l, s))
                    for g in range(2):
                        if s == 0:
                            mm = pe.matmul(b[g * HD:(g + 1) * HD, 0:NCMP], cw2[:, 0, :],
                                           hid[:, g * NCMP:(g + 1) * NCMP], start=True, stop=True)
                        else:
                            mm = pe.matmul(b[0:NCMP, g * HD:(g + 1) * HD], hid[:, g * NCMP:(g + 1) * NCMP],
                                           cw2[:, 1, :], start=True, stop=True)
                    mm.then_inc(*signal("cmp_mm", l, s))
                pe.wait_ge(*ready("cmp", l, 0))
                pe.wait_ge(*ready("roped", l, "q", 2))
                for i in range(TT):
                    for g in range(2):
                        b = take(("sc", l, i, g), ("sc", l, i, g))
                        for c in range(3):
                            mm = pe.matmul(b[:, c * NCMP:(c + 1) * NCMP], qn[g * HD:(g + 1) * HD, c, i * P:(i + 1) * P],
                                           kcs[g * HD:(g + 1) * HD, :], start=True, stop=True)
                        mm.then_inc(*signal("sc_mm", l, i, g))
                pe.wait_ge(*ready("lru_w", l))
                for c in range(LC):
                    pe.wait_ge(*ready("conv", l, c))
                    for w in range(2):
                        b = take(("lru", l, c, w), ("lru", l, c, w))
                        pe.matmul(b[:, :], lruw[:, w, c, :], tmp[:, c, :], start=True,
                                  stop=True).then_inc(*signal("lru_mm", l, c, w))
                pe.wait_ge(*ready("pc", l))
                for h in range(HEADS):
                    b = take(("pct", l, h), ("pct", l, h))
                    for i in range(TT):
                        mm = pe.transpose(b[0:NCMP, i * P:(i + 1) * P], Sc[:, i, h, :], ident[:, :])
                    mm.then_inc(*signal("pct_mm", l, h))

                def scores(u):
                    kind, h, br = UNITS[u]
                    if u == 0:
                        pe.wait_ge(*ready("roped", l, "ks", 0))
                        pe.wait_ge(*ready("roped", l, "kw", 0))
                    if kind == "mla" and h == 0:
                        pe.wait_ge(*ready("roped", l, "kpe", 0))
                        pe.wait_ge(*ready("uk", l, HEADS - 1))
                        pe.wait_ge(*ready("qrope", l, HEADS - 1))
                    for i in range(TT):
                        n = u * TT + i
                        if n >= 4:
                            pe.wait_ge(*ready("p", l, n - 4))
                        elif n >= 2:
                            pe.wait_ge(*ready("pct", l, HEADS - 1))
                        N = (i + 1) * P
                        if kind == "nsa":
                            g = h // 3
                            lo, hi = g * HD, (g + 1) * HD
                            q, k = qn[lo:hi, h % 3, i * P:N], (ksT if br == 1 else kwT)[lo:hi, 0:N]
                        else:
                            q, k = qh[0:DQK, h, i * P:N], kh[0:DQK, h, 0:N]
                        pe.matmul(score_bank[n % 4][:, 0:N], q, k, start=True, stop=False)
                        pe.matmul(score_bank[n % 4][:, i * P:N], identb, diagb, start=False,
                                  stop=True).then_inc(*signal("s_mm", l, n))

                def turn(u):
                    for i in range(TT):
                        n = u * TT + i
                        pe.wait_ge(*ready("pn", l, n))
                        if n >= 2:
                            pe.wait_ge(*ready("pt", l, n - 2))
                        for kb in range(i + 1):
                            mm = pe.transpose(turn_bank[n % 2][:, kb * P:(kb + 1) * P],
                                              Pt[:, u % 2, OFF[i] + kb * P:OFF[i] + (kb + 1) * P], ident[:, :])
                        mm.then_inc(*signal("pt_mm", l, n))

                def values(u):
                    kind, h, br = UNITS[u]
                    chunk, p0, opens, closes = unit_out(u)
                    ob = out_bank[chunk % 2]
                    if opens and p0 == 0:
                        before = {5: None, 6: None, 7: 5, 2: 6, 3: 7, 4: 2}[chunk]
                        if before is not None:
                            pe.wait_ge(*ready("mix", l, before))
                    if opens and kind == "nsa":
                        pe.wait_ge(*ready("pct", l, h))
                        g = h // 3
                        pe.matmul(ob[p0:p0 + HD, :], vcs[0:NCMP, g * HD:(g + 1) * HD], PTc[0:NCMP, h, :],
                                  start=True, stop=False)
                    pe.wait_ge(*ready("pt", l, u * TT + TT - 1))
                    last = kind == "mla" or br == 2
                    for kb in range(TT):
                        if kind == "nsa":
                            g = h // 3
                            a = (br - 1) * P + g * HD
                            v = vtok[:, kb, a:a + HD]
                        else:
                            v = vm[:, kb, h * HD:(h + 1) * HD]
                        mm = pe.matmul(ob[p0:p0 + HD, kb * P:T], v, PT[:, u % 2, kb, kb * P:T],
                                       start=(kb == 0 and kind == "mla"), stop=(last and kb == TT - 1))
                    mm.then_inc(*signal("pv", l, u))

                for u in range(NU):
                    scores(u)
                    if u >= 2:
                        values(u - 2)
                    if u >= 1:
                        turn(u - 1)
                values(NU - 2)
                turn(NU - 1)
                values(NU - 1)
                for m in range(KC):
                    J = NW * l + NF + m
                    b = take(("out", l, m), ("x_mixed", l, m))
                    pe.wait_ge(*ready("w_lo", J))
                    if m == 0:
                        pe.wait_ge(*ready("mix", l, 4))
                        pe.wait_ge(*ready("lru_out", l, LC - 1))
                    for k in range(KC):
                        mm = product(b[:, :], wring_hi[:, J % WR, k, :], wring_lo[:, J % WR, k, :], mixh[:, k, :],
                                     mixl[:, k, :], k == 0, k == KC - 1)
                    mm.then_inc(*signal("w_used", J))
                norm_sum((l, "ffn"), KC, [P] * KC)
                pe.wait_ge(*ready("hl", l, "ffn", KC - 1))
                if l == 0:
                    dense(pe, product)
                else:
                    route(pe, take, product)
                    for job in jobs[-RING:]:
                        pe.wait_ge(*ready(*job))
                    experts_pe(pe, product)
                    pe.wait_ge(*ready("moe_added"))
            norm_sum((DEPTH, "final"), KC, [P] * KC)

        @block.scalar
        def _(act):
            norms = []

            def norm_rms(tag, parts, width):
                for k, (src, r, wait) in enumerate(parts):
                    if wait is not None:
                        act.wait_ge(*wait)
                    if k >= 2:
                        act.wait_ge(*ready("ssq", *tag, k - 2))
                    act.activation(sq[0:r, k % 2, :], src, ACT.Square).then_inc(*signal("sq", *tag, k))
                act.wait_ge(*ready("ssq", *tag, len(parts) - 1))
                if norms:
                    act.wait_ge(*ready("rstd", *norms[-1]))
                norms.append(tag)
                act.activation(rms[:, :], bank[ring_of[("ssq",) + tag]][:, :], ACT.Sqrt, bias=eps[:, 0:1],
                               scale=1.0 / width).then_inc(*signal("rms", *tag))

            def halves(tag):
                for k in range(KC):
                    act.wait_ge(*ready("hf", *tag, k))
                    act.activation(hh[:, k, :], hf[:, k % 2, :], ACT.Copy,
                                   scale=SX).then_inc(*signal("hh", *tag, k))

            def w_hi(J):
                act.wait_ge(*ready(f"wstage{J % WS}", J))
                if J >= WR:
                    act.wait_ge(*ready("w_used", J - WR))
                act.activation(wring_hi[:, J % WR, :, :], wstage[:, J % WS, :, :], ACT.Copy,
                               scale=SW).then_inc(*signal("w_hi", J))

            act.wait_ge(*ready("first_consts"))
            for l in range(DEPTH):
                act.wait_ge(*ready("lam_abs", l))
                act.activation(lc[:, 4:6], lc[:, 2:4], ACT.Exp, scale=-1.0).then_inc(*signal("lam_exp", l))
                for J in range(NW * l, NW * l + WR):
                    w_hi(J)
                x_wait = {0: x_ready(l, 0)} if l > 0 else {k: ready(f"x_loaded{k // 2}") for k in range(0, KC, 2)}
                norm_rms((l, "mix"), [(xT[:, k, :], P, x_wait.get(k)) for k in range(KC)], DM)
                halves((l, "mix"))
                home = {"x": lambda c: xl[:, c, CONV - 1:], "y": lambda c: yl[:, c, :], "qdn": lambda c: qdn[:, c, :],
                        "kvdn": lambda c: kvdn, "kpe": lambda c: kpe, "q": lambda c: qn[:, c, :], "kc": lambda c: kcT,
                        "vc": lambda c: vcT, "ks": lambda c: ksT, "kw": lambda c: kwT}
                for j, (name, c, rows, p0) in enumerate(FEAT):
                    act.wait_ge(*ready("w_used", NW * l + j))
                    act.activation(home[name](c)[p0:p0 + rows, :], bank[ring_of[("feat", l, j)]][p0:p0 + rows, :],
                                   ACT.Copy, scale=(SCALE_NSA if name == "q" else 1.0) / (SW * SX)
                                   ).then_inc(*signal("feat", l, j))
                    if j + WR < NF:
                        w_hi(NW * l + j + WR)
                act.wait_ge(*ready("wtok", l))
                act.activation(wtok_hi, wtok, ACT.Copy, scale=SW).then_inc(*signal("wtok_hi", l))
                for i in range(TT):
                    act.wait_ge(*ready("tok_mm", l, i))
                    act.activation(vtok[:, i, :], bank[ring_of[("tok", l, i)]][:, 0:TOKW], ACT.Copy,
                                   scale=1.0 / (SW * SX)).then_inc(*signal("tok", l, i))
                norm_rms((l, "q"), [(qdn[:, 0, :], P, ready("feat", l, NF - 1)),
                                    (qdn[0:Q_RANK - P, 1, :], Q_RANK - P, None)], Q_RANK)
                norm_rms((l, "kv"), [(kvdn, P, None)], KV_RANK)
                for h in range(HEADS):
                    act.wait_ge(*ready("uq_mm", l, h))
                    act.activation(qh[0:DQK, h, :], bank[ring_of[("uq", l, h)]][0:DQK, :], ACT.Copy,
                                   scale=SCALE_MLA).then_inc(*signal("uq", l, h))
                for h in range(HEADS):
                    act.wait_ge(*ready("uk_mm", l, h))
                    act.copy(kh[0:NOPE, h, :], bank[ring_of[("uk", l, h)]][0:NOPE, :]).then_inc(*signal("uk", l, h))
                for i in range(TT):
                    act.wait_ge(*ready("uv_mm", l, i))
                    act.copy(vm[:, i, :], bank[ring_of[("uv", l, i)]][:, 0:HEADS * HD]).then_inc(*signal("uv", l, i))
                for s in range(2):
                    act.wait_ge(*ready("hid_mm", l, s))
                    if s == 1:
                        act.wait_ge(*ready("cmp_mm", l, 0))
                    act.activation(hid, bank[ring_of[("hid", l, s)]][:, 0:2 * NCMP],
                                   ACT.Gelu_apprx_tanh).then_inc(*signal("hid", l, s))
                    act.wait_ge(*ready("cmp_mm", l, s))
                    b = bank[ring_of[("cmp", l, s)]]
                    if s == 0:
                        act.copy(kcs, b[:, 0:NCMP]).then_inc(*signal("cmp", l, s))
                    else:
                        act.copy(vcs[0:NCMP, :], b[0:NCMP, 0:2 * HD]).then_inc(*signal("cmp", l, s))
                for c in range(LC):
                    ins = act.activation(yl[:, c, :], yl[:, c, :], ACT.Gelu_apprx_tanh)
                ins.then_inc(*signal("gelu_y", l))
                act.wait_ge(*ready("gate_sum", l))
                act.activation(vtok[:, :, 2 * P:], vtok[:, :, 2 * P:], ACT.Sigmoid).then_inc(*signal("gates", l))
                for c in range(LC):
                    act.wait_ge(*ready("lru_mm", l, c, 0))
                    if c == 0:
                        act.wait_ge(*ready("latent", l, "kv", 0))
                    act.activation(sq[:, c, :], bank[ring_of[("lru", l, c, 0)]][:, :], ACT.Sigmoid,
                                   bias=par(l, "ba", c)).then_inc(*signal("lru", l, c, 0))
                    act.wait_ge(*ready("lru_mm", l, c, 1))
                    act.activation([rms, rstd][c], bank[ring_of[("lru", l, c, 1)]][:, :], ACT.Sigmoid,
                                   bias=par(l, "bx", c)).then_inc(*signal("lru", l, c, 1))
                act.wait_ge(*ready("decay", l))
                act.wait_ge(*ready("lru", l, LC - 1, 1))
                for c in range(LC):
                    act.activation(xl[:, c, 0:T], sq[:, c, :], ACT.Exp, scale=lc[:, 10 + c:11 + c])
                    act.activation(tmp[:, 2 + c, :], sq[:, c, :], ACT.Tanh,
                                   scale=lc[:, 12 + c:13 + c]).then_inc(*signal("lru_tanh", l, c))
                act.wait_ge(*ready("sc_sub", l))
                act.activation(Sc, Sc, ACT.Exp).then_inc(*signal("sc_exp", l))
                for c in range(LC):
                    act.wait_ge(*ready("lru_quot", l, c))
                    act.activation(tmp[:, 2 + c, :], tmp[:, 2 + c, :], ACT.Sqrt,
                                   scale=2.0).then_inc(*signal("lru_root", l, c))
                for J in range(NW * l + NF, NW * l + NF + WR):
                    w_hi(J)
                for h in range(HEADS):
                    act.wait_ge(*ready("pct_mm", l, h))
                    act.copy(PTc[0:NCMP, h, :], bank[ring_of[("pct", l, h)]][0:NCMP, :]).then_inc(*signal("pct", l, h))

                def exps(u):
                    if u >= 2:
                        act.wait_ge(*ready("pt_mm", l, (u - 2) * TT + TT - 1))
                        act.wait_ge(*ready("scale", l, u - 2))
                    for i in range(TT):
                        n = u * TT + i
                        N = (i + 1) * P
                        act.wait_ge(*ready("nmx", l, n))
                        act.activation(Pt[:, u % 2, OFF[i]:OFF[i] + N], score_bank[n % 4][:, 0:N], ACT.Exp,
                                       bias=nmx[:, n % 8:n % 8 + 1],
                                       accum_out=ssum[:, u % 2, i:i + 1]).then_inc(*signal("p", l, n))

                def turned(u):
                    if u >= 2:
                        act.wait_ge(*ready("pv", l, u - 2))
                    for i in range(TT):
                        n = u * TT + i
                        act.wait_ge(*ready("pt_mm", l, n))
                        act.copy(PT[:, u % 2, 0:i + 1, i * P:(i + 1) * P],
                                 turn_bank[n % 2][:, 0:(i + 1) * P].rearrange("p (k q) -> p k q", q=P)
                                 ).then_inc(*signal("pt", l, n))

                for u in range(NU):
                    exps(u)
                    if u >= 1:
                        turned(u - 1)
                turned(NU - 1)
                for m in range(WR, KC):
                    w_hi(NW * l + NF + m)
                norm_rms((l, "ffn"), [(xT[:, k, :], P, ready("x_mixed", l, k)) for k in range(KC)], DM)
                halves((l, "ffn"))
                if l == 0:
                    def gu_hi_part(e, f):
                        act.wait_ge(*loaded(dw_loaded, e, f))
                        act.wait_ge(D["up_mm"], e * FC + FC + last_in(GS, f) + 1)
                        act.activation(gu_hi_[:, f % GS, :], dw[:, f % WS, 0:2 * DM], ACT.Copy,
                                       scale=SW).then_inc(D["hi_ready"], 1)

                    def wd_hi_part(e, f):
                        act.activation(wd_hi[:, f, :], dw[:, f % WS, 2 * DM:], ACT.Copy,
                                       scale=SW).then_inc(D["wd_hi_ready"], 1)

                    with act.Fori(0, HALVES) as e:
                        for f in range(LEAD):
                            gu_hi_part(e, f)
                        act.wait_ge(D["down_mm"], e * KC + KC)
                        for f in range(LEAD):
                            wd_hi_part(e, f)
                        for f in range(FC):
                            act.wait_ge(D["gate_mm"], e * FC + f + 1)
                            act.wait_ge(D["product"], e * FC + FC + last_in(2, f) + 1)
                            act.activation(sg[:, f % 2, :], bank[2 * (f % 2)][:, :], ACT.Silu,
                                           scale=1.0 / (SW * SX)).then_inc(D["silu"], 1)
                            if f + LEAD < FC:
                                gu_hi_part(e, f + LEAD)
                                wd_hi_part(e, f + LEAD)
                else:
                    act.wait_ge(*ready("late_consts"))
                    act.activation(wrt_hi, wrt_.rearrange("p (k e) -> p k e", k=KC), ACT.Copy,
                                   scale=SW).then_inc(*signal("router_hi"))
                    for i in range(TT):
                        act.wait_ge(*ready("tok_h_mm", i))
                        act.copy(tok_h[:, i, :], bank[ring_of[("tok_h", i)]][:, :].bitcast(BF16)
                                 ).then_inc(*signal("tok_h", i))
                    act.wait_ge(*ready("lg_sub"))
                    act.activation(lg, lg, ACT.Exp).then_inc(*signal("lg_exp"))
                    act.wait_ge(*ready("flag"))
                    experts_act(act)
            norm_rms((DEPTH, "final"), [(xT[:, k, :], P, x_ready(DEPTH, 0) if k == 0 else None)
                                        for k in range(KC)], DM)

        @block.vector
        def _(dve):
            chained = sem("dve_chained")
            chain = [0]

            def link(ins):
                chain[0] += 1
                ins.then_inc(chained, 1)
                dve.wait_ge(chained, chain[0])

            def normed(tag, parts, name):
                dve.wait_ge(*ready("rms", *tag))
                dve.reciprocal(rstd, rms).then_inc(*signal("rstd", *tag))
                dve.wait_ge(*ready("rstd", *tag))
                for k, (dst, src, gain, r) in enumerate(parts):
                    if name == "hf" and k >= 2:
                        dve.wait_ge(*ready("hl", *tag, k - 2))
                    dve.scalar_tensor_tensor(out=dst, in0=src, scalar=gain, in1=rstd[0:r, :], op0=ALU.mult,
                                             op1=ALU.mult).then_inc(*signal(name, *tag, k))
                    if name == "hf" and k >= 1:
                        lower_half(tag, k - 1)
                if name == "hf":
                    lower_half(tag, KC - 1)

            def lower_half(tag, k):
                dve.wait_ge(*ready("hh", *tag, k))
                dve.scalar_tensor_tensor(out=hl[:, k, :], in0=hf[:, k % 2, :], scalar=SX, in1=hh[:, k, :],
                                         op0=ALU.mult, op1=ALU.subtract).then_inc(*signal("hl", *tag, k))

            def w_remainder(J):
                dve.wait_ge(*ready("w_hi", J))
                dve.scalar_tensor_tensor(out=wring_lo[:, J % WR, :, :], in0=wstage[:, J % WS, :, :], scalar=SW,
                                         in1=wring_hi[:, J % WR, :, :], op0=ALU.mult,
                                         op1=ALU.subtract).then_inc(*signal("w_lo", J))

            def keep(chunk, src, label):
                link(dve.tensor_scalar(mixh[:, chunk, :], src, SX, None, ALU.mult))
                dve.scalar_tensor_tensor(out=mixl[:, chunk, :], in0=src, scalar=SX, in1=mixh[:, chunk, :],
                                         op0=ALU.mult, op1=ALU.subtract).then_inc(*signal(*label))

            def rope(dst, src, rotated, cos, sin, a, b, label):
                link(dve.tensor_tensor(a, src, cos, ALU.mult))
                link(dve.tensor_tensor(b, rotated, sin, ALU.mult))
                if dst.shape != a.shape:
                    a, b = (v.unsqueeze(1).broadcast_to(list(dst.shape)) for v in (a, b))
                dve.tensor_tensor(dst, a, b, ALU.add).then_inc(*signal(*label))

            dve.wait_ge(*ready("first_consts"))
            for l in range(DEPTH):
                y, ay, e_, w, w2, p_, dneg, dpos = (lc[:, 2 * i:2 * i + 2] for i in range(8))
                if l > 0:
                    dve.wait_ge(*ready("lru_tanh", l - 1, LC - 1))
                link(dve.tensor_scalar(y, par(l, "lam", 0, LC), -1.0, None, ALU.mult))
                dve.tensor_tensor(ay, y, par(l, "lam", 0, LC), ALU.max).then_inc(*signal("lam_abs", l))
                dve.wait_ge(*ready("lam_exp", l))
                link(dve.tensor_scalar(w, e_, 2.0, None, ALU.add))
                link(dve.reciprocal(w, w))
                link(dve.tensor_tensor(w, w, e_, ALU.mult))
                link(dve.tensor_tensor(w2, w, w, ALU.mult))
                link(dve.tensor_scalar(p_, w2, 1.0 / 19, 1.0 / 17, ALU.mult, ALU.add))
                for n in range(15, 0, -2):
                    link(dve.tensor_tensor(p_, p_, w2, ALU.mult))
                    link(dve.tensor_scalar(p_, p_, 1.0 / n, None, ALU.add))
                link(dve.tensor_tensor(p_, p_, w, ALU.mult))
                link(dve.tensor_scalar(p_, p_, 16.0, None, ALU.mult))
                link(dve.tensor_scalar(y, y, 0.0, 8.0, ALU.max, ALU.mult))
                link(dve.tensor_tensor(dpos, y, p_, ALU.add))
                link(dve.tensor_scalar(lc[:, 10:12], dpos, -1.0, None, ALU.mult))
                dve.tensor_copy(lc[:, 12:14], dpos).then_inc(*signal("decay", l))

                for J in range(NW * l, NW * l + WR):
                    w_remainder(J)
                normed((l, "mix"), [(hf[:, k % 2, :], xT[:, k, :], par(l, "norm_mix", k), P) for k in range(KC)], "hf")
                for J in range(NW * l + WR, NW * l + NF):
                    w_remainder(J)
                dve.wait_ge(*ready("wtok_hi", l))
                dve.scalar_tensor_tensor(out=wtok_lo, in0=wtok, scalar=SW, in1=wtok_hi, op0=ALU.mult,
                                         op1=ALU.subtract).then_inc(*signal("wtok_lo", l))
                dve.wait_ge(*ready("feat", l, 1))
                link(dve.memset(xl[:, :, 0:CONV - 1], 0.0))
                for c in range(LC):
                    link(dve.tensor_scalar(tmp[:, c, :], xl[:, c, 0:T], par(l, "conv_w", c * CONV),
                                           par(l, "conv_b", c), ALU.mult, ALU.add))
                    for k in range(1, CONV):
                        ins = dve.scalar_tensor_tensor(out=tmp[:, c, :], in0=xl[:, c, k:k + T],
                                                       scalar=par(l, "conv_w", c * CONV + k), in1=tmp[:, c, :],
                                                       op0=ALU.mult, op1=ALU.add)
                        if k < CONV - 1:
                            link(ins)
                    ins.then_inc(*signal("conv", l, c))
                dve.wait_ge(*ready("tok", l, TT - 1))
                dve.tensor_tensor(vtok[:, :, 2 * P:], vtok[:, :, 2 * P:],
                                  par(l, "gate_b", 0, GATES).unsqueeze(1).broadcast_to([P, TT, GATES]),
                                  ALU.add).then_inc(*signal("gate_sum", l))
                if l == 0:
                    dve.wait_ge(*ready("consts"))
                for name, c, src, tab in rope_list(l):
                    dve.wait_ge(*ready("rot_mm", l, name, c))
                    b = bank[ring_of[("rot", l, name, c)]]
                    if name == "kpe":
                        rows = slice(NOPE, DQK)
                        rope(kh[rows, :, :], src, b[rows, :], cos32[rows, :], sin32[rows, :], tmp[rows, 2, :],
                             tmp[rows, 3, :], ("roped", l, name, c))
                    else:
                        rope(src, src, b[:, :], cos64[:, :], sin64[:, :], tmp[:, 2, :], tmp[:, 3, :],
                             ("roped", l, name, c))
                    dve.wait_ge(*ready("roped", l, name, c))
                normed((l, "q"), [(qdn[:, 0, :], qdn[:, 0, :], par(l, "q_norm", 0), P),
                                  (qdn[0:Q_RANK - P, 1, :], qdn[0:Q_RANK - P, 1, :],
                                   par(l, "q_norm", 1)[0:Q_RANK - P, :], Q_RANK - P)], "latent")
                dve.wait_ge(*ready("latent", l, "q", 1))
                normed((l, "kv"), [(kvdn, kvdn, par(l, "kv_norm"), P)], "latent")
                for h in range(HEADS):
                    rows = slice(NOPE, DQK)
                    dve.wait_ge(*ready("qrot_mm", l, h))
                    b = bank[ring_of[("qrot", l, h)]]
                    rope(qh[rows, h, :], qh[rows, h, :], b[rows, :], cos32[rows, :], sin32[rows, :],
                         tmp[rows, 2, :], tmp[rows, 3, :], ("qrope", l, h))
                    dve.wait_ge(*ready("qrope", l, h))
                for s in range(2):
                    dve.wait_ge(*ready("kcg", l, s))
                    if s == 1:
                        dve.wait_ge(*ready("hid_mm", l, 0))
                    for l1 in range(2):
                        v = kcg.rearrange("p g (n u) -> p g n u", u=CMP_STRIDE)[:, :, l1:l1 + NCMP, 0:CMP_STRIDE:2]
                        v = v.rearrange("p g n u -> p u g n")
                        pos = cpos[:, s, l1 * 8:l1 * 8 + 8].unsqueeze(2).unsqueeze(3).broadcast_to([P, 8, 2, NCMP])
                        ins = dve.tensor_tensor(win[:, l1 * 8:l1 * 8 + 8, :, :], v, pos, ALU.add)
                    ins.then_inc(*signal("win", l, s))
                for i in range(TT):
                    for g in range(2):
                        dve.wait_ge(*ready("sc_mm", l, i, g))
                        dve.tensor_tensor(Sc[:, i, 3 * g:3 * g + 3, :], bank[ring_of[("sc", l, i, g)]][:, 0:3 * NCMP]
                                          .rearrange("p (h n) -> p h n", h=3),
                                          cmask[:, i, :].unsqueeze(1).broadcast_to([P, 3, NCMP]),
                                          ALU.add).then_inc(*signal("sc", l, i, g))
                dve.wait_ge(*ready("sc", l, TT - 1, 1))
                link(dve.tensor_reduce(cmx, Sc, AX_X, ALU.max))
                dve.tensor_tensor(Sc, Sc, cmx.unsqueeze(3).broadcast_to([P, TT, HEADS, NCMP]),
                                  ALU.subtract).then_inc(*signal("sc_sub", l))
                for c in range(LC):
                    dve.wait_ge(*ready("lru_tanh", l, c))
                    link(dve.tensor_scalar(sq[:, c, :], tmp[:, 2 + c, :], 1.0, None, ALU.add))
                    link(dve.reciprocal(sq[:, c, :], sq[:, c, :]))
                    dve.tensor_tensor(tmp[:, 2 + c, :], tmp[:, 2 + c, :], sq[:, c, :],
                                      ALU.mult).then_inc(*signal("lru_quot", l, c))
                    ix = [rms, rstd][c]
                    link(dve.tensor_tensor(ix, ix, tmp[:, c, :], ALU.mult))
                dve.wait_ge(*ready("sc_exp", l))
                dve.wait_ge(*ready("gates", l))
                link(dve.tensor_reduce(csum, Sc, AX_X, ALU.add))
                link(dve.tensor_scalar(csum, csum, 1e-30, None, ALU.max))
                link(dve.reciprocal(csum, csum))
                gates = vtok[:, :, 2 * P:].rearrange("p i (h b) -> p i h b", b=3)
                link(dve.tensor_tensor(csum, csum, gates[:, :, :, 0], ALU.mult))
                link(dve.tensor_tensor(csum, csum, crow[:, :].unsqueeze(2).broadcast_to([P, TT, HEADS]), ALU.mult))
                dve.tensor_tensor(Sc, Sc, csum.unsqueeze(3).broadcast_to([P, TT, HEADS, NCMP]),
                                  ALU.mult).then_inc(*signal("pc", l))
                for c in range(LC):
                    dve.wait_ge(*ready("lru_root", l, c))
                    ix = [rms, rstd][c]
                    link(dve.tensor_tensor(ix, ix, tmp[:, 2 + c, :], ALU.mult))
                    link(dve.tensor_tensor_scan(tmp[:, c, :], xl[:, c, 0:T], ix, 0.0, ALU.mult, ALU.add))
                    link(dve.tensor_tensor(tmp[:, c, :], tmp[:, c, :], yl[:, c, :], ALU.mult))
                    keep(c, tmp[:, c, :], ("lru_out", l, c))
                for J in range(NW * l + NF, NW * l + NF + WR):
                    w_remainder(J)

                def maxima(u):
                    for i in range(TT):
                        n = u * TT + i
                        N = (i + 1) * P
                        dve.wait_ge(*ready("s_mm", l, n))
                        m = n % 8
                        dve.tensor_reduce(nmx[:, m:m + 1], score_bank[n % 4][:, 0:N], AX_X, ALU.max,
                                          negate=True).then_inc(*signal("nmx", l, n))

                def scales(u):
                    kind, h, br = UNITS[u]
                    dve.wait_ge(*ready("p", l, u * TT + TT - 1))
                    r = rsum[:, u % 2, :]
                    link(dve.tensor_scalar(r, ssum[:, u % 2, :], 1e-30, None, ALU.max))
                    ins = dve.reciprocal(r, r)
                    if kind == "nsa":
                        link(ins)
                        ins = dve.tensor_tensor(r, r, gates[:, :, h, br], ALU.mult)
                    ins.then_inc(*signal("scale", l, u))
                    dve.wait_ge(*ready("scale", l, u))
                    for i in range(TT):
                        v = Pt[:, u % 2, OFF[i]:OFF[i] + (i + 1) * P]
                        dve.tensor_scalar(v, v, r[:, i:i + 1], None, ALU.mult).then_inc(*signal("pn", l, u * TT + i))

                def collect(u):
                    chunk, p0, opens, closes = unit_out(u)
                    if closes:
                        dve.wait_ge(*ready("pv", l, u))
                        keep(chunk, out_bank[chunk % 2][:, :], ("mix", l, chunk))

                for u in range(NU):
                    maxima(u)
                    if u >= 1:
                        scales(u - 1)
                    if u >= 2:
                        collect(u - 2)
                scales(NU - 1)
                collect(NU - 2)
                collect(NU - 1)
                for m in range(KC):
                    dve.wait_ge(*ready("w_used", NW * l + NF + m))
                    dve.scalar_tensor_tensor(out=xT[:, m, :], in0=bank[ring_of[("out", l, m)]][:, :],
                                             scalar=1.0 / (SW * SX), in1=xT[:, m, :], op0=ALU.mult,
                                             op1=ALU.add).then_inc(*signal("x_mixed", l, m))
                    if m + WR < KC:
                        w_remainder(NW * l + NF + m + WR)
                dve.wait_ge(*ready("x_mixed", l, KC - 1))
                normed((l, "ffn"), [(hf[:, k % 2, :], xT[:, k, :], par(l, "norm_ffn", k), P) for k in range(KC)], "hf")
                if l == 0:
                    def gu_remainder(e, f):
                        dve.wait_ge(D["hi_ready"], e * FC + f + 1)
                        dve.scalar_tensor_tensor(out=gu_lo_[:, f % GS, :], in0=dw[:, f % WS, 0:2 * DM], scalar=SW,
                                                 in1=gu_hi_[:, f % GS, :], op0=ALU.mult,
                                                 op1=ALU.subtract).then_inc(D["lo_ready"], 1)

                    def wd_remainder(e, f):
                        dve.wait_ge(D["wd_hi_ready"], e * FC + f + 1)
                        dve.scalar_tensor_tensor(out=wd_lo[:, f, :], in0=dw[:, f % WS, 2 * DM:], scalar=SW,
                                                 in1=wd_hi[:, f, :], op0=ALU.mult,
                                                 op1=ALU.subtract).then_inc(D["wd_lo_ready"], 1)

                    parted = sem("dense_parted")
                    dve.sem_inc(D["product"], FC)
                    dve.sem_inc(D["y_added"], KC)
                    dve.sem_inc(D["wd_lo_ready"], FC)
                    with dve.Fori(0, HALVES) as e:
                        for f in range(LEAD):
                            gu_remainder(e, f)
                        for f in range(LEAD):
                            wd_remainder(e, f)
                        for f in range(FC):
                            dve.wait_ge(D["silu"], e * FC + f + 1)
                            dve.wait_ge(D["up_mm"], e * FC + FC + f + 1)
                            if f >= 2:
                                dve.wait_ge(D["act_ready"], e * FC + f - 1)
                            dve.scalar_tensor_tensor(out=af[:, f % 2, :], in0=bank[2 * (f % 2) + 1][:, :],
                                                     scalar=1.0 / SW, in1=sg[:, f % 2, :], op0=ALU.mult,
                                                     op1=ALU.mult).then_inc(D["product"], 1)
                            dve.wait_ge(D["product"], e * FC + FC + f + 1)
                            dve.tensor_copy(act_hi[:, f, :], af[:, f % 2, :]).then_inc(parted, 1)
                            dve.wait_ge(parted, e * FC + f + 1)
                            dve.tensor_tensor(act_lo[:, f, :], af[:, f % 2, :], act_hi[:, f, :],
                                              ALU.subtract).then_inc(D["act_ready"], 1)
                            if f + LEAD < FC:
                                gu_remainder(e, f + LEAD)
                                wd_remainder(e, f + LEAD)
                        dve.wait_ge(D["y_added"], e * KC + KC)
                        for m in range(KC):
                            dve.wait_ge(D["down_mm"], e * KC + KC + m + 1)
                            dve.scalar_tensor_tensor(out=xT[:, m, :], in0=bank[4 + m % 4][:, :],
                                                     scalar=1.0 / (SW * SX), in1=xT[:, m, :], op0=ALU.mult,
                                                     op1=ALU.add).then_inc(D["y_added"], 1)
                    dve.wait_ge(D["y_added"], KC * (HALVES + 1))
                else:
                    dve.wait_ge(*ready("router_hi"))
                    dve.scalar_tensor_tensor(out=wrt_lo, in0=wrt_.rearrange("p (k e) -> p k e", k=KC), scalar=SW,
                                             in1=wrt_hi, op0=ALU.mult, op1=ALU.subtract).then_inc(*signal("router_lo"))
                    dve.wait_ge(*ready("router_mm"))
                    dve.tensor_scalar(lg, bank[ring_of[("router",)]][:, 0:TT * NE].rearrange("p (i e) -> p i e", i=TT),
                                      1.0 / (SW * SX), None, ALU.mult).then_inc(*signal("lg"))
                    dve.wait_ge(*ready("lg"))
                    for i in range(TT):
                        dve.wait_ge(*ready("tok_l_mm", i))
                        dve.tensor_copy(tok_l[:, i, :], bank[ring_of[("tok_l", i)]][:, :].bitcast(F16)
                                        ).then_inc(*signal("tok_l", i))
                    full = [P, TT, NE, NE]
                    of_j, of_e = lg.unsqueeze(2).broadcast_to(full), lg.unsqueeze(3).broadcast_to(full)
                    link(dve.tensor_reduce(rmx, lg, AX_X, ALU.max))
                    link(dve.tensor_tensor(cmp1, of_j, of_e, ALU.is_gt))
                    link(dve.tensor_tensor(cmp2, of_j, of_e, ALU.is_equal))
                    link(dve.tensor_tensor(cmp2, cmp2, tri[:, :].rearrange("p (e j) -> p e j", e=NE).unsqueeze(1)
                                           .broadcast_to(full), ALU.mult))
                    link(dve.tensor_tensor(cmp1, cmp1, cmp2, ALU.add))
                    link(dve.tensor_reduce(sel, cmp1, AX_X, ALU.add))
                    dve.tensor_scalar(sel, sel, 1.5, None, ALU.is_lt).then_inc(*signal("sel"))
                    dve.tensor_tensor(lg, lg, rmx.unsqueeze(2).broadcast_to([P, TT, NE]),
                                      ALU.subtract).then_inc(*signal("lg_sub"))
                    dve.wait_ge(*ready("lg_exp"))
                    dve.wait_ge(*ready("sel"))
                    link(dve.tensor_tensor(gate, sel, lg, ALU.mult))
                    link(dve.tensor_reduce(rsm, gate, AX_X, ALU.add))
                    link(dve.reciprocal(rsm, rsm))
                    link(dve.tensor_tensor(gate, gate, rsm.unsqueeze(2).broadcast_to([P, TT, NE]), ALU.mult))
                    link(dve.memset(yT_[:, KC * CAP:], 0.0))
                    link(dve.memset(hot[:, :, CAP:], 0.0))
                    link(dve.memset(g3_, 0.0))
                    for c in range(3):
                        link(dve.tensor_copy(g3[:, :, :, c], gate))
                        if c < 2:
                            link(dve.tensor_tensor(gate, gate, g3[:, :, :, c], ALU.subtract))
                    dve.wait_ge(*ready("count_mm"))
                    b = bank[ring_of[("count",)]]
                    link(dve.scalar_tensor_tensor(out=posm, in0=b[:, 0:TT * NE].rearrange("p (i e) -> p i e", i=TT),
                                                  scalar=1.0, in1=sel, op0=ALU.add, op1=ALU.mult))
                    link(dve.tensor_scalar(posm_, posm_, -1.0, None, ALU.add))
                    dve.tensor_reduce(cmax, b[:, TT * NE:(TT + 1) * NE], AX_X, ALU.max).then_inc(*signal("places"))
                    dve.wait_ge(*ready("places"))
                    dve.tensor_copy(flag[:, :], cmax).then_inc(*signal("flag"))
                    dve.wait_ge(*ready("flag"))
                    dve.sem_inc(*signal("routed"))
                    experts_dve(dve)
                    dve.memset(cmax, 0.0).then_inc(*signal("moe_added"))
            normed((DEPTH, "final"), [(outf[:, k, :], xT[:, k, :], gfin[:, k:k + 1], P) for k in range(KC)], "h")

        @block.gpsimd
        def _(pool):
            pool.wait_ge(*ready("consts"))
            pool.tensor_copy(identb, ident[:, :]).then_inc(*signal("identb"))
            pool.tensor_copy(identh, ident[:, :]).then_inc(*signal("identb"))
            pool.tensor_copy(diagb, diag).then_inc(*signal("identb"))
            for l in range(DEPTH):
                for s, src in enumerate((kcT, vcT)):
                    if s == 0:
                        pool.wait_ge(*ready("roped", l, "kc", 0))
                    else:
                        pool.wait_ge(*ready("feat", l, feat_index("vc", 0)))
                        pool.wait_ge(*ready("win", l, 0))
                    for g in range(2):
                        rows = src[g * HD:(g + 1) * HD, :]
                        pool.dma_start(kcg[0:HD, g, :], rows).then_inc(*signal("kcg", l, s, by=16))
                        pool.dma_start(kcg[HD:P, g, 0:T - 1], rows[:, 1:T]).then_inc(*signal("kcg", l, s, by=16))

        @block.sync
        def _(sp):
            for k in range(0, KC, 2):
                sp.dma_start(xT[:, k:k + 2, :], io["x"][:, k * T:(k + 2) * T].rearrange("p (k t) -> p k t", k=2)
                             ).then_inc(*signal(f"x_loaded{k // 2}", by=16))
            for name, dst in (("ones", ones), ("eps", eps), ("pp", pp)):
                sp.dma_start(dst[:, :], io[name]).then_inc(*signal("first_consts", by=16))

            def chunk(J):
                if J >= WS:
                    sp.wait_ge(*ready("w_lo", J - WS))
                sp.dma_start(wstage[:, J % WS, :, :], io["w_chunk"][J]).then_inc(*signal(f"wstage{J % WS}", J, by=16))

            for J in range(WS):
                chunk(J)
            for name, dst in (("ident", ident), ("diag", diag), ("rot64", rot64), ("rot32", rot32), ("cos64", cos64),
                              ("sin64", sin64), ("cos32", cos32), ("sin32", sin32), ("crow", crow)):
                sp.dma_start(dst[:, :], io[name]).then_inc(*signal("consts", by=16))
            sp.dma_start(cmask, io["cmask"]).then_inc(*signal("consts", by=16))
            for l in range(DEPTH):
                if l > 0:
                    sp.wait_ge(*x_ready(l, 0))
                sp.dma_start(wtok, io["w_tok"][l]).then_inc(*signal("wtok", l, by=16))
                sp.dma_start(wuq, io["w_uq"][l]).then_inc(*signal("mla_w", l, by=16))
                sp.dma_start(wukv, io["w_ukv"][l]).then_inc(*signal("mla_w", l, by=16))
                sp.dma_start(cw1, io["cmp_w1"][l]).then_inc(*signal("cmp_w", l, by=16))
                sp.dma_start(cw2, io["cmp_w2"][l]).then_inc(*signal("cmp_w", l, by=16))
                sp.dma_start(cpos, io["cmp_pos"][l]).then_inc(*signal("cmp_w", l, by=16))
                sp.dma_start(lruw, io["lru_w"][l]).then_inc(*signal("lru_w", l, by=16))
                if l == 0:
                    for name, dst in (("lower", lower), ("iota", iota), ("tri", tri), ("gfin", gfin)):
                        sp.dma_start(dst[:, :], io[name]).then_inc(*signal("late_consts", by=16))
                    sp.dma_start(wrt_, io["router"]).then_inc(*signal("late_consts", by=16))
                for J in range(NW * l + WS, NW * (l + 1)):
                    chunk(J)
                if l + 1 < DEPTH:
                    for J in range(NW * (l + 1), NW * (l + 1) + WS):
                        chunk(J)
                sp.wait_ge(*ready("pv", l, NU - 1))
                sp.wait_ge(*ready("lru_out", l, LC - 1))
                if l == 1:
                    experts_sp(sp)
                    continue
                with sp.Fori(0, HALVES) as e:
                    for f in range(FC):
                        sp.wait_ge(D["wd_lo_ready"], e * FC + FC + last_in(WS, f) + 1)
                        sp.dma_start(dw[:, f % WS, :], io["dw"][bass.ds(e * FC + f, 1)]
                                     .rearrange("a p n -> p (a n)")).then_inc(dw_loaded[f % WS], 16)
            for k in range(KC):
                sp.wait_ge(*ready("h", DEPTH, "final", k))
                sp.dma_start(io["out"][:, k, :], outf[:, k, :]).then_inc(*signal("stored", by=16))
            sp.wait_ge(*ready("stored"))
        return raised_to


def tables(np):
    t = {}
    pos = np.arange(T, dtype=np.float32)

    def rope(d, rows, at):
        half = d // 2
        inv = (np.float32(10000.0) ** (-np.arange(half, dtype=np.float32) * np.float32(2.0) / np.float32(d)))
        ang = pos[:, None] * inv.astype(np.float32)[None, :]
        cos, sin = np.cos(ang).T, np.sin(ang).T
        c, s = np.zeros((P, T), np.float32), np.zeros((P, T), np.float32)
        for a in range(at, at + rows, d):
            c[a:a + half], c[a + half:a + d] = cos, cos
            s[a:a + half], s[a + half:a + d] = -sin, sin
        return c, s

    t["cos64"], t["sin64"] = rope(HD, P, 0)
    t["cos32"], t["sin32"] = rope(ROPE, ROPE, NOPE)
    t["ident"] = np.eye(P, dtype=np.float32)
    r = np.arange(P)
    t["rot64"] = (r[:, None] == (r ^ 32)[None, :]).astype(np.float32)
    t["rot32"] = ((r[:, None] % ROPE) == (np.arange(ROPE) ^ 16)[None, :]).astype(np.float32)
    t["ones"] = np.ones((P, P), np.float32)
    t["lower"] = (r[:, None] < r[None, :]).astype(np.float32)
    t["iota"] = np.tile(np.arange(ROUNDS * CAP, dtype=np.float32), (P, 1))
    t["diag"] = np.where(r[None, :] <= r[:, None], 0.0, NEG).astype(np.float32)
    end = np.arange(NCMP) * CMP_STRIDE + CMP_LEN - 1
    q = np.arange(TT)[None, :] * P + r[:, None]
    t["cmask"] = np.where(end[None, None, :] <= q[:, :, None], 0.0, NEG).astype(np.float32)
    t["crow"] = (q >= CMP_LEN - 1).astype(np.float32)
    e = np.arange(NE)
    t["tri"] = np.tile((e[None, :] < e[:, None]).astype(np.float32).reshape(1, -1), (P, 1))
    t["eps"] = np.full((P, 1), EPS, np.float32)
    return t


def kernel(x, norm_mix, w_in, lru_conv_w, lru_conv_b, lru_wa, lru_ba, lru_wx, lru_bx, lru_lambda,
           mla_q_norm, mla_w_uq, mla_kv_norm, mla_w_ukv, nsa_cmp_pos, nsa_cmp_w1, nsa_cmp_w2, nsa_gate_b,
           w_out, norm_ffn, ffn_w_gate, ffn_w_up, ffn_w_down, router_w, moe_w_gate, moe_w_up,
           moe_w_down, norm_final):
    import numpy as np
    import concourse.bacc as bacc
    from concourse.bass_utils import run_bass_kernel_spmd

    A = np.asarray
    w_in, w_out = A(w_in), A(w_out)
    arrays = tables(np)

    def cols(v, rows=P):
        v = A(v)
        return np.moveaxis(v.reshape(v.shape[0], -1, rows), 2, 0)

    pp = np.zeros((P, DEPTH, NPP), np.float32)

    def put(name, v):
        pp[:v.shape[0], :, PC[name]:PC[name] + v.shape[2]] = v

    put("norm_mix", cols(norm_mix))
    put("norm_ffn", cols(norm_ffn))
    put("conv_w", A(lru_conv_w).reshape(DEPTH, CONV, LC, P).transpose(3, 0, 2, 1).reshape(P, DEPTH, LC * CONV))
    put("conv_b", cols(lru_conv_b))
    put("ba", cols(lru_ba))
    put("bx", cols(lru_bx))
    put("lam", cols(lru_lambda))
    put("q_norm", cols(A(mla_q_norm)[:, :P]))
    pp[:Q_RANK - P, :, PC["q_norm"] + 1] = A(mla_q_norm)[:, P:].T
    put("kv_norm", cols(mla_kv_norm))
    pp[:, :, PC["gate_b"]:PC["gate_b"] + GATES] = A(nsa_gate_b)[None]
    arrays["pp"] = pp.reshape(P, DEPTH * NPP)
    arrays["gfin"] = A(norm_final).reshape(KC, P).T
    arrays["x"] = A(x)[0].T.reshape(KC, P, T).transpose(1, 0, 2).reshape(P, KC * T)

    heads = [np.r_[c * HD:(c + 1) * HD, (c + 3) * HD:(c + 4) * HD] for c in range(3)]
    where = {"x": (0, P), "y": (LRU_W, P), "qdn": (512, P), "kvdn": (704, P), "kpe": (832, ROPE), "q": (864, P),
             "kc": (1248, P), "vc": (1376, P), "ks": (1504, P), "kw": (1760, P)}
    chunks = np.zeros((DEPTH * NW, P, KC, P), np.float32)
    for l in range(DEPTH):
        w = w_in[l].reshape(KC, P, -1).transpose(1, 0, 2)
        for j, (name, c, rows, p0) in enumerate(FEAT):
            at = where[name][0] + c * P
            idx = where["q"][0] + heads[c] if name == "q" else np.arange(at, at + rows)
            chunks[l * NW + j, :, :, :rows] = w[:, :, idx]
        order = np.concatenate([np.arange(5 * P)] + [5 * P + h for h in heads])
        wo = w_out[l][order].reshape(KC, P, KC, P).transpose(2, 1, 0, 3)
        chunks[l * NW + NF:(l + 1) * NW] = wo
    arrays["w_chunk"] = chunks
    tok = np.r_[1632:1760, 1888:2016, 2016:2034]
    arrays["w_tok"] = w_in[:, :, tok].reshape(DEPTH, KC, P, TOKW).transpose(0, 2, 1, 3)
    wuq = np.zeros((DEPTH, P, 2, HEADS * DQK), np.float32)
    wuq[:, :, 0] = A(mla_w_uq)[:, :P]
    wuq[:, :Q_RANK - P, 1] = A(mla_w_uq)[:, P:]
    arrays["w_uq"] = wuq
    arrays["w_ukv"] = A(mla_w_ukv).reshape(DEPTH, P, HEADS, 2, HD).transpose(0, 1, 3, 2, 4).reshape(DEPTH, P, 2, -1)
    arrays["cmp_w1"] = A(nsa_cmp_w1).reshape(DEPTH, 2, LP, P, P).transpose(0, 3, 1, 2, 4)
    arrays["cmp_w2"] = A(nsa_cmp_w2).transpose(0, 2, 1, 3)
    arrays["cmp_pos"] = A(nsa_cmp_pos).reshape(DEPTH, 2, LP, P).transpose(0, 3, 1, 2)
    lru = np.zeros((DEPTH, P, 2, LC, P), np.float32)
    for w, v in enumerate((A(lru_wa), A(lru_wx))):
        for n in range(4):
            a = 64 * (n % 2)
            lru[:, a:a + 64, w, n // 2, a:a + 64] = v[:, n]
    arrays["lru_w"] = lru
    arrays["router"] = A(router_w)[0].reshape(KC, P, NE).transpose(1, 0, 2).reshape(P, KC * NE)

    def gate_up(g, u):
        both = np.stack([A(g), A(u)], 0)
        both = both.reshape(2, -1, KC, P, FC, P)
        return both.transpose(1, 4, 3, 0, 2, 5).reshape(-1, P, 2, KC, P)

    dense = [A(v)[0].reshape(DM, 2, FE).transpose(1, 0, 2) for v in (ffn_w_gate, ffn_w_up)]

    def chunked(g, u, d):
        w = np.empty((g.shape[0] * FC, P, 3, DM), np.float32)
        w[:, :, 0:2] = gate_up(g, u).reshape(-1, P, 2, DM)
        w[:, :, 2] = d.reshape(-1, P, DM)
        return w.reshape(-1, P, 3 * DM)

    arrays["dw"] = chunked(*dense, A(ffn_w_down)[0])
    arrays["ew"] = chunked(A(moe_w_gate)[0], A(moe_w_up)[0], A(moe_w_down)[0])

    def build(known):
        nc = bacc.Bacc("TRN2", target_bir_lowering=False, num_devices=1)
        io = {n: nc.dram_tensor(f"in_{n}", list(a.shape), F32, kind="ExternalInput").ap() for n, a in arrays.items()}
        io["out"] = nc.dram_tensor("out_x", [P, KC, T], F32, kind="ExternalOutput").ap()
        return nc, trunk(nc, io, known)

    _, counted = build({})
    nc, again = build(counted)
    assert again == counted
    r = run_bass_kernel_spmd(nc, [{f"in_{n}": np.ascontiguousarray(a, np.float32) for n, a in arrays.items()}],
                             core_ids=[0])
    out = r.results[0]["out_x"]
    return np.ascontiguousarray(out.transpose(1, 0, 2).reshape(DM, T).T[None])
```

```python
from contextlib import ExitStack

import concourse.bass as bass
from concourse import mybir

ALU = mybir.AluOpType
ACT = mybir.ActivationFunctionType
F32 = mybir.dt.float32
BF16 = mybir.dt.bfloat16
F16 = mybir.dt.float16
I32 = mybir.dt.int32
AX_X = mybir.AxisListType.X

P = 128
T = 512
TT = T // P
DM = 1024
KC = DM // P
DEPTH = 2
EPS = 1e-6
LRU_W = 256
LC = LRU_W // P
CONV = 4
HEADS = 6
NOPE, ROPE, HD = 64, 32, 64
DQK = NOPE + ROPE
Q_RANK, KV_RANK = 192, 128
CMP_LEN, CMP_STRIDE = 32, 16
NCMP = (T - CMP_LEN) // CMP_STRIDE + 1
LP = CMP_LEN // 2
GATES = 3 * HEADS
TOKW = 2 * P + GATES
FE = 1408
FC = FE // P
NE = 8
CAP = 192
ROUNDS = -(-T // CAP)
TAIL = CAP - P
ES, EP = 3, 4
LEAD = 2
NEG = -1.0e30
SCALE_MLA = float(DQK) ** -0.5
SCALE_NSA = float(HD) ** -0.5

FEAT = [("qdn", 0, P, 0), ("qdn", 1, Q_RANK - P, 0), ("kvdn", 0, P, 0), ("kpe", 0, ROPE, NOPE),
        ("x", 0, P, 0), ("x", 1, P, 0), ("kc", 0, P, 0), ("vc", 0, P, 0), ("ks", 0, P, 0), ("kw", 0, P, 0),
        ("q", 0, P, 0), ("q", 1, P, 0), ("q", 2, P, 0), ("y", 0, P, 0), ("y", 1, P, 0)]
NF = len(FEAT)

PREPARE = [
    ("feat", 0), ("feat", 1), ("squares", "q"),
    ("feat", 2), ("norm", "q"), ("squares", "kv"),
    ("feat", 3), ("norm", "kv"),
    ("feat", 4), ("rope", ("kpe", 0)),
    ("feat", 5), ("conv", 0), ("uq", 0), ("uq", 1),
    ("feat", 6), ("conv", 1), ("uq", 2), ("uq", 3), ("qrot", 0),
    ("feat", 7), ("rope", ("kc", 0)), ("uq", 4), ("uq", 5), ("qrot", 1),
    ("feat", 8), ("uk", 0), ("uk", 1), ("qrot", 2), ("rope", ("ks", 0)),
    ("feat", 9), ("win", 0), ("uk", 2), ("uk", 3), ("qrot", 3),
    ("feat", 10), ("rope", ("kw", 0)), ("hid", 0), ("wtok", 0), ("uk", 4), ("uk", 5),
    ("feat", 11), ("rope", ("q", 0)), ("cmp", 0), ("lru_gates", 0), ("lru_gates", 1), ("qrot", 4),
    ("feat", 12), ("rope", ("q", 1)), ("win", 1), ("uv", 0), ("uv", 1),
    ("tok", 0), ("rope", ("q", 2)), ("hid", 1), ("uv", 2), ("uv", 3),
    ("tok", 1), ("cmp", 1), ("cmp_scores", 0), ("cmp_max", 0),
    ("tok", 2), ("lru_decay", 0),
    ("tok", 3), ("gates", 0), ("cmp_probs", 0), ("lru_root", 0),
    ("feat", 13), ("turn_cmp", 0), ("qrot", 5),
    ("feat", 14), ("gelu_y", 0),
]
NW = NF + KC
WS, WR = 2, 3
SW, SX = 256.0, 16.0

PC = {}
_at = 0
for _n, _w in (("norm_mix", KC), ("norm_ffn", KC), ("conv_w", LC * CONV), ("conv_b", LC), ("ba", LC), ("bx", LC),
               ("lam", LC), ("q_norm", 2), ("kv_norm", 1), ("gate_b", GATES)):
    PC[_n] = _at
    _at += _w
NPP = _at

UNITS = []
for _c in range(3):
    for _h in (_c, _c + 3):
        UNITS += [("nsa", _h, 1), ("nsa", _h, 2)]
for _h in range(HEADS):
    UNITS.append(("mla", _h, 0))
NU = len(UNITS)


def unit_out(u):
    kind, h, br = UNITS[u]
    if kind == "nsa":
        return 5 + h % 3, 64 * (h // 3), br == 1, h >= 3 and br == 2
    return 2 + h // 2, 64 * (h % 2), True, h % 2 == 1


def trunk(nc, io, known):
    with ExitStack() as ctx:
        def sb(name, cols):
            return ctx.enter_context(nc.sbuf_tensor(name, [P, cols], F32))

        def sem(name):
            return ctx.enter_context(nc.semaphore(name))

        family_sem, raised, raised_to = {}, {}, {}

        def sem_of(family):
            if family not in family_sem:
                family_sem[family] = sem(family)
            return family_sem[family]

        def signal(family, *item, by=1):
            raised[family] = raised.get(family, 0) + by
            raised_to[(family,) + item] = raised[family]
            return sem_of(family), by

        def ready(family, *item):
            return sem_of(family), known[(family,) + item] if known else 1

        xT_ = sb("xT", KC * T)
        hh = sb("hh", KC * T // 2)[:, :].bitcast(BF16).rearrange("p (k t) -> p k t", k=KC)
        hl = sb("hl", KC * T // 2)[:, :].bitcast(F16).rearrange("p (k t) -> p k t", k=KC)
        hf = sb("hf", 2 * T)[:, :].rearrange("p (s t) -> p s t", s=2)
        xT = xT_[:, :].rearrange("p (k t) -> p k t", k=KC)
        mixh, mixl = hh, hl
        ident = sb("ident", P)
        identb = sb("identb", P // 2)[:, :].bitcast(BF16)
        identh = sb("identh", P // 2)[:, :].bitcast(F16)
        lower = sb("lower", P)
        rot64 = sb("rot64", P)
        rot32 = sb("rot32", ROPE)
        ones = sb("ones", P)
        diagb = sb("diagb", P // 2)[:, :].bitcast(BF16)
        cmask = sb("cmask", TT * NCMP)[:, :].rearrange("p (i n) -> p i n", i=TT)
        crow = sb("crow", TT)
        tri = sb("tri", NE * NE)
        eps = sb("eps", 1)
        cos64, sin64 = sb("cos64", T), sb("sin64", T)
        cos32, sin32 = sb("cos32", T), sb("sin32", T)
        pp = sb("pp", DEPTH * NPP)
        gfin = sb("gfin", KC)
        small = sb("small", 256)
        wrt_ = sb("wrt", KC * NE)[:, :]
        wrt_hi, wrt_lo = (sb(f"wrt_{n}", KC * NE // 2)[:, :].bitcast(F16)
                          .rearrange("p (k e) -> p k e", k=KC) for n in ("hi", "lo"))
        iota = sb("iota", ROUNDS * CAP)
        flag = ctx.enter_context(nc.sbuf_tensor("flag", [P, 1], I32))
        wstage = sb("wstage", WS * KC * P)[:, :].rearrange("p (s k m) -> p s k m", s=WS, k=KC)
        wring_hi, wring_lo = (sb(f"wring_{n}", WR * KC * P // 2)[:, :].bitcast(F16)
                              .rearrange("p (s k m) -> p s k m", s=WR, k=KC) for n in ("hi", "lo"))

        ARENA = 34720
        arena = sb("arena", ARENA)
        used = [0]

        def room(cols):
            a = used[0]
            used[0] += cols
            assert used[0] <= ARENA, used[0]
            return arena[:, a:a + cols]

        def room16(cols, dtype=F16):
            return room((cols + 1) // 2).bitcast(dtype)

        wtok_ = room(KC * TOKW)
        wtok = wtok_.rearrange("p (k m) -> p k m", k=KC)
        vm = wtok_[:, 0:TT * HEADS * HD].rearrange("p (i m) -> p i m", i=TT)
        xl = room(LC * (T + CONV - 1)).rearrange("p (c t) -> p c t", c=LC)
        yl = room(LC * T).rearrange("p (c t) -> p c t", c=LC)
        qdn = room(2 * T).rearrange("p (c t) -> p c t", c=2)
        latent_ = room(2 * T)
        kvdn, kpe = latent_[:, 0:T], latent_[:, T:2 * T]
        Sc = latent_[:, 0:TT * HEADS * NCMP].rearrange("p (i h n) -> p i h n", i=TT, h=HEADS)
        qn = room(3 * T).rearrange("p (c t) -> p c t", c=3)
        kcT, vcT, ksT, kwT = room(T), room(T), room(T), room(T)
        vtok = room(TT * TOKW).rearrange("p (i m) -> p i m", i=TT)
        wuq = room(2 * HEADS * DQK).rearrange("p (c m) -> p c m", c=2)
        wukv = room(2 * HEADS * HD).rearrange("p (v m) -> p v m", v=2)
        cw1_ = room(2 * LP * P)
        cw1 = cw1_.rearrange("p (s l m) -> p s l m", s=2, l=LP)
        PT = cw1_.rearrange("p (s k t) -> p s k t", s=2, k=TT)
        cw2 = room(2 * HD).rearrange("p (s m) -> p s m", s=2)
        cpos = room(2 * LP).rearrange("p (s l) -> p s l", s=2)
        lruw = room(2 * LC * P).rearrange("p (w c m) -> p w c m", w=2, c=LC)
        qh = room(HEADS * T).rearrange("p (h t) -> p h t", h=HEADS)
        kh_ = room(HEADS * T)
        kh = kh_.rearrange("p (h t) -> p h t", h=HEADS)
        NP_ = sum((i + 1) * P for i in range(TT))
        Pt_ = room(2 * NP_)
        Pt = Pt_.rearrange("p (s n) -> p s n", s=2)
        wtok_hi, wtok_lo = (Pt_[:, n * KC * TOKW // 2:(n + 1) * KC * TOKW // 2].bitcast(F16)
                            .rearrange("p (k m) -> p k m", k=KC) for n in range(2))
        diag = Pt_[:, 2 * NP_ - P:]
        assert KC * TOKW <= 2 * NP_ - P
        OFF = [sum((j + 1) * P for j in range(i)) for i in range(TT)]
        shared_ = room(HEADS * T)
        PTc = shared_.rearrange("p (h t) -> p h t", h=HEADS)
        kcg = shared_[:, 0:2 * T].rearrange("p (g t) -> p g t", g=2)
        win = shared_[:, 2 * T:2 * T + LP * 2 * NCMP].rearrange("p (l g n) -> p l g n", l=LP, g=2)
        hid = room(2 * NCMP)
        kcs = room(NCMP)
        vcs = room(2 * HD)
        tmp = room(4 * T).rearrange("p (s t) -> p s t", s=4)
        sq = room(2 * T).rearrange("p (s t) -> p s t", s=2)
        rms, rstd = room(T), room(T)
        sq_at = used[0] - 4 * T
        used[0] = 0
        GS = 3
        dw = room(WS * 3 * DM).rearrange("p (s n) -> p s n", s=WS)
        gu_hi_, gu_lo_ = (room16(GS * 2 * DM).rearrange("p (s n) -> p s n", s=GS) for _ in range(2))
        gu_hi, gu_lo = (v.rearrange("p s (g k m) -> p s g k m", g=2, k=KC) for v in (gu_hi_, gu_lo_))
        wd_hi, wd_lo = (room16(FC * DM).rearrange("p (f m) -> p f m", f=FC) for _ in range(2))
        act_hi = room16(FC * T, BF16).rearrange("p (f t) -> p f t", f=FC)
        act_lo = room16(FC * T).rearrange("p (f t) -> p f t", f=FC)
        sg = room(2 * T).rearrange("p (s t) -> p s t", s=2)
        af = hf
        assert used[0] <= sq_at, (used[0], sq_at)
        used[0] = 0
        ew = room(ES * 3 * DM).rearrange("p (s n) -> p s n", s=ES)
        ew_hi_, ew_lo_ = (room16(EP * 3 * DM).rearrange("p (s n) -> p s n", s=EP) for _ in range(2))
        ew_hi, ew_lo = (v.rearrange("p s (g k m) -> p s g k m", g=3, k=KC) for v in (ew_hi_, ew_lo_))
        posm_ = room(TT * NE)
        posm = posm_.rearrange("p (i e) -> p i e", i=TT)
        g3_ = room16(TT * NE * 4, BF16)
        g3 = g3_.rearrange("p (i e c) -> p i e c", i=TT, e=NE)
        lg = room(TT * NE).rearrange("p (i e) -> p i e", i=TT)
        gate = room(TT * NE).rearrange("p (i e) -> p i e", i=TT)
        sel = room(TT * NE).rearrange("p (i e) -> p i e", i=TT)
        cmp1 = room(TT * NE * NE).rearrange("p (i e j) -> p i e j", i=TT, e=NE)
        cmp2 = room(TT * NE * NE).rearrange("p (i e j) -> p i e j", i=TT, e=NE)
        tok_h = room16(TT * DM, BF16).rearrange("p (i d) -> p i d", i=TT)
        tok_l = room16(TT * DM).rearrange("p (i d) -> p i d", i=TT)
        assert used[0] <= sq_at, (used[0], sq_at)
        xg_h = room16(KC * CAP, BF16).rearrange("p (k n) -> p k n", k=KC)
        xg_l = room16(KC * CAP).rearrange("p (k n) -> p k n", k=KC)
        eact_h = room16(3 * CAP, BF16).rearrange("p (s n) -> p s n", s=3)
        eact_l = room16(3 * CAP).rearrange("p (s n) -> p s n", s=3)
        esg = room(2 * CAP).rearrange("p (s n) -> p s n", s=2)
        eaf = room(2 * CAP).rearrange("p (s n) -> p s n", s=2)
        hot = room16(TT * 2 * P, BF16).rearrange("p (i n) -> p i n", i=TT)
        hotT = room16(2 * T, BF16).rearrange("p (h t) -> p h t", h=2)
        yT_ = room(KC * CAP + 2 * P - CAP)
        yT = yT_[:, 0:KC * CAP].rearrange("p (m n) -> p m n", m=KC)
        y_hi = room16(2 * DM, BF16).rearrange("p (h d) -> p h d", h=2)
        y_lo = room16(2 * DM).rearrange("p (h d) -> p h d", h=2)
        gslot = room(2)
        outf = arena[:, 0:KC * T].rearrange("p (k t) -> p k t", k=KC)

        nmx = small[:, 8:16]
        ssum = small[:, 16:24].rearrange("p (s i) -> p s i", s=2)
        rsum = small[:, 24:32].rearrange("p (s i) -> p s i", s=2)
        cmx = small[:, 32:56].rearrange("p (i h) -> p i h", i=TT)
        csum = small[:, 56:80].rearrange("p (i h) -> p i h", i=TT)
        lc = small[:, 80:100]
        rmx = small[:, 100:104]
        rsm = small[:, 104:108]
        cmax = small[:, 108:109]

        bank = [ctx.enter_context(nc.psum_tensor(f"bank{i}", [P, T], F32)) for i in range(8)]
        RING = 4
        score_bank = [bank[2], bank[3], bank[0], bank[1]]
        turn_bank = [bank[4], bank[5]]
        out_bank = [bank[6], bank[7]]
        ring_of = {}
        jobs = []

        dense_sems = ("gate_mm", "up_mm", "silu", "product", "act_ready", "down_mm", "y_added", "hi_ready", "lo_ready",
                      "wd_hi_ready", "wd_lo_ready")
        D = {n: sem(f"dense_{n}") for n in dense_sems}
        dw_loaded = [sem(f"dense_w_loaded{i}") for i in range(WS)]
        HALVES = 2
        moe_sems = ("hi_ready", "lo_ready", "up_mm", "down_mm", "silu", "product", "act_ready", "y_out", "y_hi", "y_lo",
                    "turned_mm", "scatter_mm", "x_added", "hot", "gather_mm", "gathered", "hotT_mm", "hotT", "gslot_mm",
                    "gslot", "split")
        M = {n: sem(f"moe_{n}") for n in moe_sems}
        ew_loaded = [sem(f"moe_w_loaded{i}") for i in range(ES)]

        def x_ready(l, stage):
            if stage == 1:
                return ready("x_mixed", l, KC - 1)
            return (D["y_added"], KC * (HALVES + 1)) if l == 1 else ready("moe_added")

        def par(l, name, i=0, n=1):
            a = l * NPP + PC[name] + i
            return pp[:, a:a + n]

        def roped_tensor(name, c):
            return {"q": qn[:, c, :], "kc": kcT, "ks": ksT, "kw": kwT, "kpe": kpe[NOPE:DQK, :]}[name]

        def feat_index(name, c):
            return [(f[0], f[1]) for f in FEAT].index((name, c))

        def dense(pe, product):
            for job in jobs[-RING:]:
                pe.wait_ge(*ready(*job))
            with pe.Fori(0, HALVES) as e:
                for f in range(FC):
                    slot = f % GS
                    pe.wait_ge(D["lo_ready"], e * FC + f + 1)
                    pe.wait_ge(D["product"], e * FC + FC + last_in(2, f) + 1)
                    for g, done in ((0, "gate_mm"), (1, "up_mm")):
                        for k in range(KC):
                            if f == 0 and g == 0:
                                pe.wait_ge(*ready("hl", 0, "ffn", k))
                            mm = product(bank[2 * (f % 2) + g][:, :], gu_hi[:, slot, g, k, :], gu_lo[:, slot, g, k, :],
                                         hh[:, k, :], hl[:, k, :], k == 0, k == KC - 1)
                        mm.then_inc(D[done], 1)
                pe.wait_ge(D["act_ready"], e * FC + FC)
                pe.wait_ge(D["wd_lo_ready"], e * FC + 2 * FC)
                for m in range(KC):
                    pe.wait_ge(D["y_added"], e * KC + KC + m - 4 + 1)
                    for f in range(FC):
                        mm = product(bank[4 + m % 4][:, :], wd_hi[:, f, m * P:(m + 1) * P],
                                     wd_lo[:, f, m * P:(m + 1) * P], act_hi[:, f, :], act_lo[:, f, :],
                                     f == 0, f == FC - 1)
                    mm.then_inc(D["down_mm"], 1)
            pe.wait_ge(D["y_added"], KC * (HALVES + 1))

        def route(pe, take, product):
            b = take(("router",), ("lg",))
            pe.wait_ge(*ready("router_lo"))
            for i in range(TT):
                t = slice(i * P, (i + 1) * P)
                for k in range(KC):
                    mm = product(b[:, i * NE:(i + 1) * NE], hh[:, k, t], hl[:, k, t], wrt_hi[:, k, :], wrt_lo[:, k, :],
                                 k == 0, k == KC - 1)
            mm.then_inc(*signal("router_mm"))
            for i in range(TT):
                for src, family, unit, dtype in ((hh, "tok_h", identb, BF16), (hl, "tok_l", identh, F16)):
                    b = take((family, i), (family, i))[:, :].bitcast(dtype)
                    for k in range(KC):
                        mm = pe.transpose(b[:, k * P:(k + 1) * P], src[:, k, i * P:(i + 1) * P], unit)
                    mm.then_inc(*signal(family + "_mm", i))
            b = take(("count",), ("places",))
            pe.wait_ge(*ready("sel"))
            for i in range(TT):
                for j in range(i + 1):
                    pe.matmul(b[:, i * NE:(i + 1) * NE], (lower if j == i else ones)[:, :], sel[:, j, :],
                              start=(j == 0), stop=(j == i))
            for j in range(TT):
                mm = pe.matmul(b[:, TT * NE:(TT + 1) * NE], ones[:, :], sel[:, j, :], start=(j == 0),
                               stop=(j == TT - 1))
            mm.then_inc(*signal("count_mm"))

        SCATTER_BANK = [0, 1, 6, 7, 6, 7, 0, 1]

        def turned_bank(j):
            return bank[(6, 7, 0, 1)[j]]

        def last_in(slots, f):
            return f - slots if f >= slots else max(g for g in range(FC) if g % slots == f % slots) - FC

        def loaded(sems, n, f):
            slots = len(sems)
            per = (FC - f % slots + slots - 1) // slots
            return sems[f % slots], n * (16 * per) + 16 * (f // slots + 1)

        def experts_pe(pe, product):
            def other(j, reader, value):
                pe.wait_ge(M[reader], value)
                return bank[6 + j % 2]

            def gather(n, waits, first=0, end=KC):
                pe.wait_ge(M["hot"], n * TT + TT)
                for j in range(first, end):
                    b = other(j, *(waits[j - first] if j < first + 2 else ("gathered", n * KC + j - 1)))
                    for h in range(2):
                        k = 2 * (j // 2) + h
                        for i in range(TT):
                            mm = pe.matmul(b[:, h * CAP:(h + 1) * CAP], (tok_h, tok_l)[j % 2][:, i, k * P:(k + 1) * P],
                                           hot[:, i, 0:CAP], start=(i == 0), stop=(i == TT - 1))
                    mm.then_inc(M["gather_mm"], 1)

            def turn_hot(n, e, waits):
                for h in range(2):
                    b = other(h, *waits[h])[:, :].bitcast(BF16)
                    for i in range(TT):
                        mm = pe.transpose(b[:, i * P:(i + 1) * P], hot[:, i, h * P:(h + 1) * P], identb)
                    mm.then_inc(M["hotT_mm"], 1)
                for h in range(2):
                    b = other(h, "hotT", n * 2 + h + 1)
                    for i in range(TT):
                        mm = pe.matmul(b[:, 0:4], hot[:, i, h * P:(h + 1) * P], g3_of(i, e), start=(i == 0),
                                       stop=(i == TT - 1))
                    mm.then_inc(M["gslot_mm"], 1)

            def chunks(n, ahead):
                def down(f):
                    pe.wait_ge(M["act_ready"], n * FC + f + 1)
                    if f == 0:
                        pe.wait_ge(M["y_out"], n * 4 + 4)
                    for m in range(KC):
                        out = bank[2 + m // 2][:, (m % 2) * CAP:(m % 2 + 1) * CAP]
                        w = ew_hi[:, f % EP, 2, m, :], ew_lo[:, f % EP, 2, m, :]
                        x = eact_h[:, f % 3, :], eact_l[:, f % 3, :]
                        pe.matmul(out, w[0], x[0], start=(f == 0 and m % 2 == 0), stop=False, skip_group_check=True)
                        pe.matmul(out, w[0], x[1], start=False, stop=False, skip_group_check=True)
                        mm = pe.matmul(out, w[1], x[0], start=False, stop=(f == FC - 1), skip_group_check=True)
                    mm.then_inc(M["down_mm"], 1)

                for f in range(FC):
                    pe.wait_ge(M["lo_ready"], n * FC + FC + f + 1)
                    pe.wait_ge(M["product"], n * FC + FC + last_in(2, f) + 1)
                    for g in range(2):
                        for k in range(KC):
                            mm = product(bank[f % 2][:, g * CAP:(g + 1) * CAP], ew_hi[:, f % EP, g, k, :],
                                         ew_lo[:, f % EP, g, k, :], xg_h[:, k, :], xg_l[:, k, :], k == 0,
                                         k == KC - 1)
                    mm.then_inc(M["up_mm"], 1)
                    if f >= 1:
                        down(f - 1)
                if ahead:
                    gather(n + 1, [("gslot", n * 2 + 1), ("gslot", n * 2 + 2)], 0, 2)
                down(FC - 1)

            def tail(n, waits, ahead):
                pe.wait_ge(M["y_out"], n * 4 + 8)
                j = 0
                for h in range(2):
                    for half in range(2):
                        b = other(j, *waits[j]) if j < 2 else bank[j - 2]
                        for m in range(4):
                            a = (half * 4 + m) * CAP + h * P
                            mm = pe.transpose(b[:, m * P:(m + 1) * P], yT_[:, a:a + P], ident[:, :])
                        mm.then_inc(M["turned_mm"], 1)
                        j += 1
                if ahead:
                    gather(n + 1, [("y_lo", n * 4 + 1), ("y_lo", n * 4 + 2)], KC - 2, KC)
                pe.wait_ge(M["y_lo"], n * 4 + 4)
                pe.wait_ge(M["hotT"], n * 2 + 2)
                for m in range(KC):
                    b = bank[SCATTER_BANK[m]]
                    if m in (2, 3) and ahead:
                        pe.wait_ge(M["gathered"], (n + 1) * KC + KC - 3 + m)
                    elif m >= 4:
                        pe.wait_ge(M["x_added"], n * KC + SCATTER_BANK.index(SCATTER_BANK[m]) + 1)
                    for h, w in ((0, P), (1, TAIL)):
                        for src in (y_hi, y_lo):
                            mm = pe.matmul(b[:, :], src[0:w, h, m * P:(m + 1) * P], hotT[0:w, h, :],
                                           start=(h == 0 and src is y_hi), stop=(h == 1 and src is y_lo))
                    mm.then_inc(M["scatter_mm"], 1)

            pe.wait_ge(*ready("routed"))
            gather(0, [("product", FC)] * 2)
            turn_hot(0, 0, [("gathered", KC - 1), ("gathered", KC)])
            with pe.Fori(0, NE - 1) as e:
                chunks(e, True)
                gather(e + 1, [("gathered", e * KC + KC + 1), ("gathered", e * KC + KC + 2)], 2, KC - 2)
                tail(e, [("gathered", e * KC + 2 * KC - 3), ("gathered", e * KC + 2 * KC - 2)], True)
                turn_hot(e + 1, e + 1, [("x_added", e * KC + 5), ("x_added", e * KC + 6)])
                pe.wait_ge(M["x_added"], e * KC + KC)
            chunks(NE - 1, False)
            tail(NE - 1, [("gslot", 2 * NE - 1), ("gslot", 2 * NE)], False)
            over = pe.value_load(flag[0:1, 0:1])
            with pe.If(over > CAP):
                with pe.Fori(1, ROUNDS) as r:
                    with pe.Fori(0, NE) as e:
                        n = r * NE + e
                        gather(n, [("x_added", n * KC - 1), ("x_added", n * KC)])
                        turn_hot(n, e, [("gathered", n * KC + KC - 1), ("gathered", n * KC + KC)])
                        chunks(n, False)
                        tail(n, [("gslot", n * 2 + 1), ("gslot", n * 2 + 2)], False)

        def g3_of(i, e):
            a = (i * NE + e) * 4
            return g3_[:, bass.ds(a, 4)]

        def expert_hi(act, n, f):
            act.wait_ge(*loaded(ew_loaded, n, f))
            act.wait_ge(M["down_mm"], n * FC + FC + last_in(EP, f) + 1)
            act.activation(ew_hi_[:, f % EP, :], ew[:, f % ES, :], ACT.Copy, scale=SW).then_inc(M["hi_ready"], 1)

        def experts_act(act):
            def hi(n, f):
                expert_hi(act, n, f)

            def gathered(n, first=0, end=KC):
                for j in range(first, end):
                    k = 2 * (j // 2)
                    act.wait_ge(M["gather_mm"], n * KC + j + 1)
                    act.copy((xg_h, xg_l)[j % 2][:, k:k + 2, :].rearrange("p k n -> p (k n)"),
                             bank[6 + j % 2][:, 0:2 * CAP]).then_inc(M["gathered"], 1)

            def hot_turned(n):
                for h, w in ((0, P), (1, TAIL)):
                    act.wait_ge(M["hotT_mm"], n * 2 + h + 1)
                    act.copy(hotT[0:w, h, :], bank[6 + h][:, :].bitcast(BF16)[0:w, 0:T]).then_inc(M["hotT"], 1)

            def silus(n, ahead):
                for f in range(FC):
                    act.wait_ge(M["up_mm"], n * FC + f + 1)
                    act.wait_ge(M["product"], n * FC + FC + last_in(2, f) + 1)
                    act.activation(esg[:, f % 2, :], bank[f % 2][:, 0:CAP], ACT.Silu,
                                   scale=1.0 / (SW * SX)).then_inc(M["silu"], 1)
                    if 0 < f < FC - LEAD:
                        hi(n, f + LEAD)
                    elif f > 0 and ahead:
                        hi(n + 1, f + LEAD - FC)

            def results(n):
                act.wait_ge(M["down_mm"], n * FC + 2 * FC)
                for j in range(4):
                    act.activation(yT[:, 2 * j:2 * j + 2, :].rearrange("p m n -> p (m n)"), bank[2 + j][:, 0:2 * CAP],
                                   ACT.Copy, scale=1.0 / SW).then_inc(M["y_out"], 1)

            def gated(n):
                act.wait_ge(M["gslot"], n * 2 + 2)
                for j in range(4):
                    h, half, w = j // 2, j % 2, (P, TAIL)[j // 2]
                    act.wait_ge(M["turned_mm"], n * 4 + j + 1)
                    act.activation(y_hi[0:w, h, half * T:(half + 1) * T], turned_bank(j)[0:w, :], ACT.Copy,
                                   scale=gslot[0:w, h:h + 1]).then_inc(M["y_hi"], 1)

            act.sem_inc(M["y_out"], 4)
            gathered(0)
            hot_turned(0)
            hi(0, LEAD)
            with act.Fori(0, NE - 1) as e:
                silus(e, True)
                gathered(e + 1, 0, 2)
                results(e)
                gathered(e + 1, 2, KC - 2)
                gated(e)
                gathered(e + 1, KC - 2, KC)
                hi(e + 1, LEAD)
                hot_turned(e + 1)
            silus(NE - 1, False)
            results(NE - 1)
            gated(NE - 1)
            over = act.value_load(flag[0:1, 0:1])
            with act.If(over > CAP):
                with act.Fori(1, ROUNDS) as r:
                    with act.Fori(0, NE) as e:
                        n = r * NE + e
                        gathered(n)
                        hot_turned(n)
                        for f in range(LEAD + 1):
                            hi(n, f)
                        silus(n, False)
                        results(n)
                        gated(n)

        def expert_remainder(dve, n, f):
            dve.wait_ge(M["hi_ready"], n * FC + f + 1)
            dve.scalar_tensor_tensor(out=ew_lo_[:, f % EP, :], in0=ew[:, f % ES, :], scalar=SW,
                                     in1=ew_hi_[:, f % EP, :], op0=ALU.mult,
                                     op1=ALU.subtract).then_inc(M["lo_ready"], 1)

        def experts_dve(dve):
            def remainder(n, f):
                expert_remainder(dve, n, f)

            def one_hot(n, e, r):
                for i in range(TT):
                    dve.tensor_scalar(hot[:, i, 0:CAP], iota[:, bass.ds(r * CAP, CAP)], posm_[:, bass.ds(i * NE + e, 1)],
                                      None, ALU.is_equal).then_inc(M["hot"], 1)

            def slot_gates(n):
                for h, w in ((0, P), (1, TAIL)):
                    dve.wait_ge(M["gslot_mm"], n * 2 + h + 1)
                    dve.tensor_reduce(gslot[0:w, h:h + 1], bank[6 + h][0:w, 0:3], AX_X, ALU.add).then_inc(M["gslot"], 1)

            def products(n, ahead):
                for f in range(FC):
                    dve.wait_ge(M["silu"], n * FC + f + 1)
                    if f >= 2:
                        dve.wait_ge(M["act_ready"], n * FC + f - 1)
                    dve.scalar_tensor_tensor(out=eaf[:, f % 2, :], in0=bank[f % 2][:, CAP:2 * CAP], scalar=1.0 / SW,
                                             in1=esg[:, f % 2, :], op0=ALU.mult,
                                             op1=ALU.mult).then_inc(M["product"], 1)
                    dve.wait_ge(M["product"], n * FC + FC + f + 1)
                    dve.tensor_copy(eact_h[:, f % 3, :], eaf[:, f % 2, :]).then_inc(M["split"], 1)
                    dve.wait_ge(M["split"], n * FC + f + 1)
                    dve.tensor_tensor(eact_l[:, f % 3, :], eaf[:, f % 2, :], eact_h[:, f % 3, :],
                                      ALU.subtract).then_inc(M["act_ready"], 1)
                    if 0 < f < FC - LEAD:
                        remainder(n, f + LEAD)
                    elif f > 0 and ahead:
                        remainder(n + 1, f + LEAD - FC)

            def y_remainders(n):
                for j in range(4):
                    h, half, w = j // 2, j % 2, (P, TAIL)[j // 2]
                    cols = slice(half * T, (half + 1) * T)
                    dve.wait_ge(M["y_hi"], n * 4 + j + 1)
                    dve.scalar_tensor_tensor(out=y_lo[0:w, h, cols], in0=turned_bank(j)[0:w, :],
                                             scalar=gslot[0:w, h:h + 1], in1=y_hi[0:w, h, cols], op0=ALU.mult,
                                             op1=ALU.subtract).then_inc(M["y_lo"], 1)

            def sums(n):
                for m in range(KC):
                    dve.wait_ge(M["scatter_mm"], n * KC + m + 1)
                    dve.scalar_tensor_tensor(out=xT[:, m, :], in0=bank[SCATTER_BANK[m]][:, :], scalar=1.0 / SX,
                                             in1=xT[:, m, :], op0=ALU.mult, op1=ALU.add).then_inc(M["x_added"], 1)

            one_hot(0, 0, 0)
            slot_gates(0)
            remainder(0, LEAD)
            with dve.Fori(0, NE - 1) as e:
                dve.wait_ge(M["gslot_mm"], e * 2 + 2)
                one_hot(e + 1, e + 1, 0)
                products(e, True)
                y_remainders(e)
                sums(e)
                dve.wait_ge(M["x_added"], e * KC + KC)
                slot_gates(e + 1)
                remainder(e + 1, LEAD)
            products(NE - 1, False)
            y_remainders(NE - 1)
            sums(NE - 1)
            dve.wait_ge(M["x_added"], NE * KC)
            over = dve.value_load(flag[0:1, 0:1])
            with dve.If(over > CAP):
                with dve.Fori(1, ROUNDS) as r:
                    with dve.Fori(0, NE) as e:
                        n = r * NE + e
                        dve.wait_ge(M["x_added"], n * KC)
                        one_hot(n, e, r)
                        for f in range(LEAD + 1):
                            remainder(n, f)
                        slot_gates(n)
                        products(n, False)
                        y_remainders(n)
                        sums(n)
                dve.wait_ge(M["x_added"], ROUNDS * NE * KC)

        def experts_sp(sp):
            def load(n, e, f):
                sp.wait_ge(M["lo_ready"], n * FC + FC + last_in(ES, f) + 1)
                sp.dma_start(ew[:, f % ES, :], io["ew"][bass.ds(e * FC + f, 1)]
                             .rearrange("a p n -> p (a n)")).then_inc(ew_loaded[f % ES], 16)

            with sp.Fori(0, NE) as e:
                for f in range(FC):
                    load(e, e, f)
            sp.wait_ge(*ready("flag"))
            over = sp.value_load(flag[0:1, 0:1])
            with sp.If(over > CAP):
                with sp.Fori(1, ROUNDS) as r:
                    with sp.Fori(0, NE) as e:
                        for f in range(FC):
                            load(r * NE + e, e, f)

        block = ctx.enter_context(nc.Block())

        @block.tensor
        def _(pe):
            def take(job, reader):
                n = len(jobs)
                if n >= RING:
                    pe.wait_ge(*ready(*jobs[n - RING]))
                jobs.append(reader)
                ring_of[job] = n % RING
                return bank[n % RING]

            def norm_sum(tag, chunks, rows):
                b = take(("ssq",) + tag, ("rms",) + tag)
                for k in range(chunks):
                    pe.wait_ge(*ready("sq", *tag, k))
                    r = rows[k]
                    pe.matmul(b[:, :], ones[0:r, :], sq[0:r, k % 2, :], start=(k == 0),
                              stop=(k == chunks - 1)).then_inc(*signal("ssq", *tag, k))

            def product(out, w_hi, w_lo, x_hi, x_lo, first, last):
                pe.matmul(out, w_hi, x_hi, start=first, stop=False)
                pe.matmul(out, w_hi, x_lo, start=False, stop=False)
                return pe.matmul(out, w_lo, x_hi, start=False, stop=last)

            pe.sem_inc(D["up_mm"], FC)
            pe.sem_inc(D["down_mm"], KC)
            pe.sem_inc(M["down_mm"], FC)
            pe.wait_ge(*ready("first_consts"))
            for l in range(DEPTH):
                norm_sum((l, "mix"), KC, [P] * KC)

                def feat(j):
                    name, c, rows, p0 = FEAT[j]
                    b = take(("feat", l, j), ("feat", l, j))
                    J = NW * l + j
                    pe.wait_ge(*ready("w_lo", J))
                    for k in range(KC):
                        if j == 0:
                            pe.wait_ge(*ready("hl", l, "mix", k))
                        mm = product(b[p0:p0 + rows, :], wring_hi[:, J % WR, k, 0:rows],
                                     wring_lo[:, J % WR, k, 0:rows], hh[:, k, :], hl[:, k, :], k == 0, k == KC - 1)
                    mm.then_inc(*signal("w_used", J))

                def tok(i):
                    if i == 0:
                        pe.wait_ge(*ready("wtok_lo", l))
                    b = take(("tok", l, i), ("tok", l, i))
                    t = slice(i * P, (i + 1) * P)
                    for k in range(KC):
                        mm = product(b[:, 0:TOKW], hh[:, k, t], hl[:, k, t], wtok_hi[:, k, :], wtok_lo[:, k, :],
                                     k == 0, k == KC - 1)
                    mm.then_inc(*signal("tok_mm", l, i))

                def rope_turn(which):
                    name, c = which
                    src = roped_tensor(name, c)
                    if l == 0 and name == "kpe":
                        pe.wait_ge(*ready("consts"))
                        pe.wait_ge(*ready("identb"))
                    b = take(("rot", l, name, c), ("roped", l, name, c))
                    pe.wait_ge(*ready("feat", l, feat_index(name, c)))
                    if name == "kpe":
                        mm = pe.matmul(b[NOPE:DQK, :], rot32[NOPE:DQK, :], src, start=True, stop=True)
                    else:
                        mm = pe.matmul(b[:, :], rot64[:, :], src, start=True, stop=True)
                    mm.then_inc(*signal("rot_mm", l, name, c))

                def latent_sum(which):
                    norm_sum((l, which), *((2, [P, Q_RANK - P]) if which == "q" else (1, [P])))

                def uq(h):
                    if h == 0:
                        pe.wait_ge(*ready("mla_w", l))
                        pe.wait_ge(*ready("latent", l, "q", 1))
                    b = take(("uq", l, h), ("uq", l, h))
                    pe.matmul(b[0:DQK, :], wuq[:, 0, h * DQK:(h + 1) * DQK], qdn[:, 0, :], start=True, stop=False)
                    pe.matmul(b[0:DQK, :], wuq[0:Q_RANK - P, 1, h * DQK:(h + 1) * DQK], qdn[0:Q_RANK - P, 1, :],
                              start=False, stop=True).then_inc(*signal("uq_mm", l, h))

                def qrot(h):
                    b = take(("qrot", l, h), ("qrope", l, h))
                    pe.wait_ge(*ready("uq", l, h))
                    pe.matmul(b[NOPE:DQK, :], rot32[NOPE:DQK, :], qh[NOPE:DQK, h, :], start=True,
                              stop=True).then_inc(*signal("qrot_mm", l, h))

                def uk(h):
                    if h == 0:
                        pe.wait_ge(*ready("latent", l, "kv", 0))
                    b = take(("uk", l, h), ("uk", l, h))
                    pe.matmul(b[0:NOPE, :], wukv[:, 0, h * HD:(h + 1) * HD], kvdn, start=True,
                              stop=True).then_inc(*signal("uk_mm", l, h))

                def uv(i):
                    b = take(("uv", l, i), ("uv", l, i))
                    pe.matmul(b[:, 0:HEADS * HD], kvdn[:, i * P:(i + 1) * P], wukv[:, 1, :], start=True,
                              stop=True).then_inc(*signal("uv_mm", l, i))

                def compress_hidden(s):
                    b = take(("hid", l, s), ("hid", l, s))
                    pe.wait_ge(*ready("cmp_w", l))
                    pe.wait_ge(*ready("win", l, s))
                    for lp in range(LP):
                        mm = pe.matmul(b[:, 0:2 * NCMP], cw1[:, s, lp, :], win[:, lp, :, :],
                                       start=(lp == 0), stop=(lp == LP - 1))
                    mm.then_inc(*signal("hid_mm", l, s))

                def compress_out(s):
                    b = take(("cmp", l, s), ("cmp", l, s))
                    pe.wait_ge(*ready("hid", l, s))
                    for g in range(2):
                        if s == 0:
                            mm = pe.matmul(b[g * HD:(g + 1) * HD, 0:NCMP], cw2[:, 0, :],
                                           hid[:, g * NCMP:(g + 1) * NCMP], start=True, stop=True)
                        else:
                            mm = pe.matmul(b[0:NCMP, g * HD:(g + 1) * HD], hid[:, g * NCMP:(g + 1) * NCMP],
                                           cw2[:, 1, :], start=True, stop=True)
                    mm.then_inc(*signal("cmp_mm", l, s))

                def cmp_scores(_):
                    pe.wait_ge(*ready("cmp", l, 0))
                    pe.wait_ge(*ready("roped", l, "q", 2))
                    for i in range(TT):
                        for g in range(2):
                            b = take(("sc", l, i, g), ("sc", l, i, g))
                            for c in range(3):
                                mm = pe.matmul(b[:, c * NCMP:(c + 1) * NCMP],
                                               qn[g * HD:(g + 1) * HD, c, i * P:(i + 1) * P],
                                               kcs[g * HD:(g + 1) * HD, :], start=True, stop=True)
                            mm.then_inc(*signal("sc_mm", l, i, g))

                def lru_gates(c):
                    if c == 0:
                        pe.wait_ge(*ready("lru_w", l))
                    pe.wait_ge(*ready("conv", l, c))
                    for w in range(2):
                        b = take(("lru", l, c, w), ("lru", l, c, w))
                        pe.matmul(b[:, :], lruw[:, w, c, :], tmp[:, c, :], start=True,
                                  stop=True).then_inc(*signal("lru_mm", l, c, w))

                def turn_cmp(_):
                    pe.wait_ge(*ready("pc", l))
                    for h in range(HEADS):
                        b = take(("pct", l, h), ("pct", l, h))
                        for i in range(TT):
                            mm = pe.transpose(b[0:NCMP, i * P:(i + 1) * P], Sc[:, i, h, :], ident[:, :])
                        mm.then_inc(*signal("pct_mm", l, h))

                part = {"feat": feat, "tok": tok, "rope": rope_turn, "norm": latent_sum, "uq": uq, "qrot": qrot,
                        "uk": uk, "uv": uv, "hid": compress_hidden, "cmp": compress_out, "cmp_scores": cmp_scores,
                        "lru_gates": lru_gates, "turn_cmp": turn_cmp}
                for step, which in PREPARE:
                    if step in part:
                        part[step](which)
                for job in jobs[-RING:]:
                    pe.wait_ge(*ready(*job))

                def scores(u):
                    kind, h, br = UNITS[u]
                    if u == 0:
                        pe.wait_ge(*ready("roped", l, "ks", 0))
                        pe.wait_ge(*ready("roped", l, "kw", 0))
                    if kind == "mla" and h == 0:
                        pe.wait_ge(*ready("roped", l, "kpe", 0))
                        pe.wait_ge(*ready("uk", l, HEADS - 1))
                        pe.wait_ge(*ready("qrope", l, HEADS - 1))
                    for i in range(TT):
                        n = u * TT + i
                        if n >= 4:
                            pe.wait_ge(*ready("p", l, n - 4))
                        N = (i + 1) * P
                        if kind == "nsa":
                            g = h // 3
                            lo, hi = g * HD, (g + 1) * HD
                            q, k = qn[lo:hi, h % 3, i * P:N], (ksT if br == 1 else kwT)[lo:hi, 0:N]
                        else:
                            q, k = qh[0:DQK, h, i * P:N], kh[0:DQK, h, 0:N]
                        pe.matmul(score_bank[n % 4][:, 0:N], q, k, start=True, stop=False)
                        pe.matmul(score_bank[n % 4][:, i * P:N], identb, diagb, start=False,
                                  stop=True).then_inc(*signal("s_mm", l, n))

                def turn(u):
                    for i in range(TT):
                        n = u * TT + i
                        pe.wait_ge(*ready("pn", l, n))
                        if n >= 2:
                            pe.wait_ge(*ready("pt", l, n - 2))
                        for kb in range(i + 1):
                            mm = pe.transpose(turn_bank[n % 2][:, kb * P:(kb + 1) * P],
                                              Pt[:, u % 2, OFF[i] + kb * P:OFF[i] + (kb + 1) * P], ident[:, :])
                        mm.then_inc(*signal("pt_mm", l, n))

                def values(u):
                    kind, h, br = UNITS[u]
                    chunk, p0, opens, closes = unit_out(u)
                    ob = out_bank[chunk % 2]
                    if opens and p0 == 0:
                        before = {5: None, 6: None, 7: 5, 2: 6, 3: 7, 4: 2}[chunk]
                        if before is not None:
                            pe.wait_ge(*ready("mix", l, before))
                    if opens and kind == "nsa":
                        pe.wait_ge(*ready("pct", l, h))
                        g = h // 3
                        pe.matmul(ob[p0:p0 + HD, :], vcs[0:NCMP, g * HD:(g + 1) * HD], PTc[0:NCMP, h, :],
                                  start=True, stop=False)
                    pe.wait_ge(*ready("pt", l, u * TT + TT - 1))
                    last = kind == "mla" or br == 2
                    for kb in range(TT):
                        if kind == "nsa":
                            g = h // 3
                            a = (br - 1) * P + g * HD
                            v = vtok[:, kb, a:a + HD]
                        else:
                            v = vm[:, kb, h * HD:(h + 1) * HD]
                        mm = pe.matmul(ob[p0:p0 + HD, kb * P:T], v, PT[:, u % 2, kb, kb * P:T],
                                       start=(kb == 0 and kind == "mla"), stop=(last and kb == TT - 1))
                    mm.then_inc(*signal("pv", l, u))

                for u in range(NU):
                    scores(u)
                    if u >= 2:
                        values(u - 2)
                    if u >= 1:
                        turn(u - 1)
                values(NU - 2)
                turn(NU - 1)
                values(NU - 1)
                for m in range(KC):
                    J = NW * l + NF + m
                    b = take(("out", l, m), ("x_mixed", l, m))
                    pe.wait_ge(*ready("w_lo", J))
                    if m == 0:
                        pe.wait_ge(*ready("mix", l, 4))
                        pe.wait_ge(*ready("lru_out", l, LC - 1))
                    for k in range(KC):
                        mm = product(b[:, :], wring_hi[:, J % WR, k, :], wring_lo[:, J % WR, k, :], mixh[:, k, :],
                                     mixl[:, k, :], k == 0, k == KC - 1)
                    mm.then_inc(*signal("w_used", J))
                norm_sum((l, "ffn"), KC, [P] * KC)
                if l == 0:
                    dense(pe, product)
                else:
                    pe.wait_ge(*ready("hl", l, "ffn", KC - 1))
                    route(pe, take, product)
                    for job in jobs[-RING:]:
                        pe.wait_ge(*ready(*job))
                    experts_pe(pe, product)
                    pe.wait_ge(*ready("moe_added"))
            norm_sum((DEPTH, "final"), KC, [P] * KC)

        @block.scalar
        def _(act):
            norms = []

            def squares(tag, parts):
                for k, (src, r, wait) in enumerate(parts):
                    if wait is not None:
                        act.wait_ge(*wait)
                    if k >= 2:
                        act.wait_ge(*ready("ssq", *tag, k - 2))
                    act.activation(sq[0:r, k % 2, :], src, ACT.Square).then_inc(*signal("sq", *tag, k))

            def root(tag, parts, width):
                act.wait_ge(*ready("ssq", *tag, parts - 1))
                if norms:
                    act.wait_ge(*ready("rstd", *norms[-1]))
                norms.append(tag)
                act.activation(rms[:, :], bank[ring_of[("ssq",) + tag]][:, :], ACT.Sqrt, bias=eps[:, 0:1],
                               scale=1.0 / width).then_inc(*signal("rms", *tag))

            def norm_rms(tag, parts, width):
                squares(tag, parts)
                root(tag, len(parts), width)

            def halves(tag):
                for k in range(KC):
                    act.wait_ge(*ready("hf", *tag, k))
                    act.activation(hh[:, k, :], hf[:, k % 2, :], ACT.Copy,
                                   scale=SX).then_inc(*signal("hh", *tag, k))

            def w_hi(J):
                act.wait_ge(*ready(f"wstage{J % WS}", J))
                if J >= WR:
                    act.wait_ge(*ready("w_used", J - WR))
                act.activation(wring_hi[:, J % WR, :, :], wstage[:, J % WS, :, :], ACT.Copy,
                               scale=SW).then_inc(*signal("w_hi", J))

            def gu_hi_part(e, f):
                act.wait_ge(*loaded(dw_loaded, e, f))
                act.wait_ge(D["up_mm"], e * FC + FC + last_in(GS, f) + 1)
                act.activation(gu_hi_[:, f % GS, :], dw[:, f % WS, 0:2 * DM], ACT.Copy,
                               scale=SW).then_inc(D["hi_ready"], 1)

            def wd_hi_part(e, f):
                act.activation(wd_hi[:, f, :], dw[:, f % WS, 2 * DM:], ACT.Copy,
                               scale=SW).then_inc(D["wd_hi_ready"], 1)

            def dense_half(e, ahead):
                for f in range(FC):
                    act.wait_ge(D["gate_mm"], e * FC + f + 1)
                    act.wait_ge(D["product"], e * FC + FC + last_in(2, f) + 1)
                    act.activation(sg[:, f % 2, :], bank[2 * (f % 2)][:, :], ACT.Silu,
                                   scale=1.0 / (SW * SX)).then_inc(D["silu"], 1)
                    if f + LEAD < FC:
                        gu_hi_part(e, f + LEAD)
                        wd_hi_part(e, f + LEAD)
                    elif ahead:
                        gu_hi_part(e + 1, f + LEAD - FC)

            act.wait_ge(*ready("first_consts"))
            for l in range(DEPTH):
                act.wait_ge(*ready("lam_abs", l))
                act.activation(lc[:, 4:6], lc[:, 2:4], ACT.Exp, scale=-1.0).then_inc(*signal("lam_exp", l))
                x_wait = {0: x_ready(l, 0)} if l > 0 else {k: ready(f"x_loaded{k // 2}") for k in range(0, KC, 2)}
                squares((l, "mix"), [(xT[:, k, :], P, x_wait.get(k)) for k in range(KC)])
                for J in range(NW * l, NW * l + WS):
                    w_hi(J)
                root((l, "mix"), KC, DM)
                halves((l, "mix"))
                for J in range(NW * l + WS, NW * l + WR):
                    w_hi(J)
                home = {"x": lambda c: xl[:, c, CONV - 1:], "y": lambda c: yl[:, c, :], "qdn": lambda c: qdn[:, c, :],
                        "kvdn": lambda c: kvdn, "kpe": lambda c: kpe, "q": lambda c: qn[:, c, :], "kc": lambda c: kcT,
                        "vc": lambda c: vcT, "ks": lambda c: ksT, "kw": lambda c: kwT}

                def feat(j):
                    name, c, rows, p0 = FEAT[j]
                    act.wait_ge(*ready("w_used", NW * l + j))
                    act.activation(home[name](c)[p0:p0 + rows, :], bank[ring_of[("feat", l, j)]][p0:p0 + rows, :],
                                   ACT.Copy, scale=(SCALE_NSA if name == "q" else 1.0) / (SW * SX)
                                   ).then_inc(*signal("feat", l, j))
                    w_hi(NW * l + j + WR)

                def wtok_upper(_):
                    act.wait_ge(*ready("wtok", l))
                    act.activation(wtok_hi, wtok, ACT.Copy, scale=SW).then_inc(*signal("wtok_hi", l))

                def tok(i):
                    act.wait_ge(*ready("tok_mm", l, i))
                    act.activation(vtok[:, i, :], bank[ring_of[("tok", l, i)]][:, 0:TOKW], ACT.Copy,
                                   scale=1.0 / (SW * SX)).then_inc(*signal("tok", l, i))

                def latent_squares(which):
                    if which == "q":
                        act.wait_ge(*ready("feat", l, feat_index("qdn", 1)))
                        squares((l, "q"), [(qdn[:, 0, :], P, None), (qdn[0:Q_RANK - P, 1, :], Q_RANK - P, None)])
                    else:
                        act.wait_ge(*ready("feat", l, feat_index("kvdn", 0)))
                        act.wait_ge(*ready("ssq", l, "q", 0))
                        squares((l, "kv"), [(kvdn, P, None)])

                def latent_root(which):
                    root((l, which), (2 if which == "q" else 1), (Q_RANK if which == "q" else KV_RANK))

                def uq(h):
                    act.wait_ge(*ready("uq_mm", l, h))
                    act.activation(qh[0:DQK, h, :], bank[ring_of[("uq", l, h)]][0:DQK, :], ACT.Copy,
                                   scale=SCALE_MLA).then_inc(*signal("uq", l, h))

                def uk(h):
                    act.wait_ge(*ready("uk_mm", l, h))
                    act.copy(kh[0:NOPE, h, :], bank[ring_of[("uk", l, h)]][0:NOPE, :]).then_inc(*signal("uk", l, h))

                def uv(i):
                    if i == 0:
                        act.wait_ge(*ready("wtok_lo", l))
                    act.wait_ge(*ready("uv_mm", l, i))
                    act.copy(vm[:, i, :], bank[ring_of[("uv", l, i)]][:, 0:HEADS * HD]).then_inc(*signal("uv", l, i))

                def compress_hidden(s):
                    act.wait_ge(*ready("hid_mm", l, s))
                    if s == 1:
                        act.wait_ge(*ready("cmp_mm", l, 0))
                    act.activation(hid, bank[ring_of[("hid", l, s)]][:, 0:2 * NCMP],
                                   ACT.Gelu_apprx_tanh).then_inc(*signal("hid", l, s))

                def compress_out(s):
                    act.wait_ge(*ready("cmp_mm", l, s))
                    b = bank[ring_of[("cmp", l, s)]]
                    if s == 0:
                        act.copy(kcs, b[:, 0:NCMP]).then_inc(*signal("cmp", l, s))
                    else:
                        act.copy(vcs[0:NCMP, :], b[0:NCMP, 0:2 * HD]).then_inc(*signal("cmp", l, s))

                def gelu_y(_):
                    for c in range(LC):
                        act.wait_ge(*ready("feat", l, feat_index("y", c)))
                        ins = act.activation(yl[:, c, :], yl[:, c, :], ACT.Gelu_apprx_tanh)
                    ins.then_inc(*signal("gelu_y", l))

                def gates_sigmoid(_):
                    act.wait_ge(*ready("gate_sum", l))
                    act.activation(vtok[:, :, 2 * P:], vtok[:, :, 2 * P:], ACT.Sigmoid).then_inc(*signal("gates", l))

                def lru_gates(c):
                    act.wait_ge(*ready("lru_mm", l, c, 0))
                    if c == 0:
                        act.wait_ge(*ready("latent", l, "kv", 0))
                    act.activation(sq[:, c, :], bank[ring_of[("lru", l, c, 0)]][:, :], ACT.Sigmoid,
                                   bias=par(l, "ba", c)).then_inc(*signal("lru", l, c, 0))
                    act.wait_ge(*ready("lru_mm", l, c, 1))
                    act.activation([rms, rstd][c], bank[ring_of[("lru", l, c, 1)]][:, :], ACT.Sigmoid,
                                   bias=par(l, "bx", c)).then_inc(*signal("lru", l, c, 1))

                def lru_decay(_):
                    act.wait_ge(*ready("decay", l))
                    act.wait_ge(*ready("lru", l, LC - 1, 1))
                    act.wait_ge(*ready("roped", l, "q", 2))
                    for c in range(LC):
                        act.activation(xl[:, c, 0:T], sq[:, c, :], ACT.Exp, scale=lc[:, 10 + c:11 + c])
                        act.activation(tmp[:, 2 + c, :], sq[:, c, :], ACT.Tanh,
                                       scale=lc[:, 12 + c:13 + c]).then_inc(*signal("lru_tanh", l, c))

                def cmp_max(_):
                    act.wait_ge(*ready("sc_sub", l))
                    act.activation(Sc, Sc, ACT.Exp).then_inc(*signal("sc_exp", l))

                def lru_root(_):
                    for c in range(LC):
                        act.wait_ge(*ready("lru_square", l, c))
                        act.activation(tmp[:, 2 + c, :], tmp[:, 2 + c, :],
                                       ACT.Sqrt).then_inc(*signal("lru_root", l, c))

                def turn_cmp(_):
                    for h in range(HEADS):
                        act.wait_ge(*ready("pct_mm", l, h))
                        act.copy(PTc[0:NCMP, h, :],
                                 bank[ring_of[("pct", l, h)]][0:NCMP, :]).then_inc(*signal("pct", l, h))

                part = {"feat": feat, "tok": tok, "wtok": wtok_upper, "squares": latent_squares, "norm": latent_root,
                        "uq": uq, "uk": uk, "uv": uv, "hid": compress_hidden, "cmp": compress_out, "gelu_y": gelu_y,
                        "gates": gates_sigmoid, "lru_gates": lru_gates, "lru_decay": lru_decay, "cmp_max": cmp_max,
                        "lru_root": lru_root, "turn_cmp": turn_cmp}
                for step, which in PREPARE:
                    if step in part:
                        part[step](which)

                def exps(u):
                    if u >= 2:
                        act.wait_ge(*ready("pt_mm", l, (u - 2) * TT + TT - 1))
                        act.wait_ge(*ready("scale", l, u - 2))
                    for i in range(TT):
                        n = u * TT + i
                        N = (i + 1) * P
                        act.wait_ge(*ready("nmx", l, n))
                        act.activation(Pt[:, u % 2, OFF[i]:OFF[i] + N], score_bank[n % 4][:, 0:N], ACT.Exp,
                                       bias=nmx[:, n % 8:n % 8 + 1],
                                       accum_out=ssum[:, u % 2, i:i + 1]).then_inc(*signal("p", l, n))

                def turned(u):
                    if u >= 2:
                        act.wait_ge(*ready("pv", l, u - 2))
                    for i in range(TT):
                        n = u * TT + i
                        act.wait_ge(*ready("pt_mm", l, n))
                        act.copy(PT[:, u % 2, 0:i + 1, i * P:(i + 1) * P],
                                 turn_bank[n % 2][:, 0:(i + 1) * P].rearrange("p (k q) -> p k q", q=P)
                                 ).then_inc(*signal("pt", l, n))

                for u in range(NU):
                    exps(u)
                    if u >= 1:
                        turned(u - 1)
                turned(NU - 1)
                for m in range(WR, KC):
                    w_hi(NW * l + NF + m)
                if l == 0:
                    for f in range(LEAD):
                        gu_hi_part(0, f)
                    for f in range(LEAD):
                        wd_hi_part(0, f)
                else:
                    for f in range(LEAD):
                        expert_hi(act, 0, f)
                norm_rms((l, "ffn"), [(xT[:, k, :], P, ready("x_mixed", l, k)) for k in range(KC)], DM)
                halves((l, "ffn"))
                if l == 0:
                    with act.Fori(0, HALVES - 1) as e:
                        dense_half(e, True)
                        act.wait_ge(D["down_mm"], e * KC + 2 * KC)
                        for f in range(LEAD):
                            wd_hi_part(e + 1, f)
                    dense_half(HALVES - 1, False)
                else:
                    act.wait_ge(*ready("late_consts"))
                    act.activation(wrt_hi, wrt_.rearrange("p (k e) -> p k e", k=KC), ACT.Copy,
                                   scale=SW).then_inc(*signal("router_hi"))
                    for i in range(TT):
                        act.wait_ge(*ready("tok_h_mm", i))
                        act.copy(tok_h[:, i, :], bank[ring_of[("tok_h", i)]][:, :].bitcast(BF16)
                                 ).then_inc(*signal("tok_h", i))
                    act.wait_ge(*ready("lg_sub"))
                    act.activation(lg, lg, ACT.Exp).then_inc(*signal("lg_exp"))
                    act.wait_ge(*ready("flag"))
                    experts_act(act)
            norm_rms((DEPTH, "final"), [(xT[:, k, :], P, x_ready(DEPTH, 0) if k == 0 else None)
                                        for k in range(KC)], DM)

        @block.vector
        def _(dve):
            chained = sem("dve_chained")
            chain = [0]

            def link(ins):
                chain[0] += 1
                ins.then_inc(chained, 1)
                dve.wait_ge(chained, chain[0])

            def normed(tag, parts, name):
                dve.wait_ge(*ready("rms", *tag))
                dve.reciprocal(rstd, rms).then_inc(*signal("rstd", *tag))
                dve.wait_ge(*ready("rstd", *tag))
                for k, (dst, src, gain, r) in enumerate(parts):
                    if name == "hf" and k >= 2:
                        dve.wait_ge(*ready("hl", *tag, k - 2))
                    dve.scalar_tensor_tensor(out=dst, in0=src, scalar=gain, in1=rstd[0:r, :], op0=ALU.mult,
                                             op1=ALU.mult).then_inc(*signal(name, *tag, k))
                    if name == "hf" and k >= 1:
                        lower_half(tag, k - 1)
                if name == "hf":
                    lower_half(tag, KC - 1)

            def lower_half(tag, k):
                dve.wait_ge(*ready("hh", *tag, k))
                dve.scalar_tensor_tensor(out=hl[:, k, :], in0=hf[:, k % 2, :], scalar=SX, in1=hh[:, k, :],
                                         op0=ALU.mult, op1=ALU.subtract).then_inc(*signal("hl", *tag, k))

            def w_remainder(J):
                dve.wait_ge(*ready("w_hi", J))
                dve.scalar_tensor_tensor(out=wring_lo[:, J % WR, :, :], in0=wstage[:, J % WS, :, :], scalar=SW,
                                         in1=wring_hi[:, J % WR, :, :], op0=ALU.mult,
                                         op1=ALU.subtract).then_inc(*signal("w_lo", J))

            def keep(chunk, src, label):
                link(dve.tensor_scalar(mixh[:, chunk, :], src, SX, None, ALU.mult))
                dve.scalar_tensor_tensor(out=mixl[:, chunk, :], in0=src, scalar=SX, in1=mixh[:, chunk, :],
                                         op0=ALU.mult, op1=ALU.subtract).then_inc(*signal(*label))

            def rope(dst, src, rotated, cos, sin, a, b, label):
                link(dve.tensor_tensor(a, src, cos, ALU.mult))
                link(dve.tensor_tensor(b, rotated, sin, ALU.mult))
                if dst.shape != a.shape:
                    a, b = (v.unsqueeze(1).broadcast_to(list(dst.shape)) for v in (a, b))
                dve.tensor_tensor(dst, a, b, ALU.add).then_inc(*signal(*label))

            def gu_remainder(e, f):
                dve.wait_ge(D["hi_ready"], e * FC + f + 1)
                dve.scalar_tensor_tensor(out=gu_lo_[:, f % GS, :], in0=dw[:, f % WS, 0:2 * DM], scalar=SW,
                                         in1=gu_hi_[:, f % GS, :], op0=ALU.mult,
                                         op1=ALU.subtract).then_inc(D["lo_ready"], 1)

            def wd_remainder(e, f):
                dve.wait_ge(D["wd_hi_ready"], e * FC + f + 1)
                dve.scalar_tensor_tensor(out=wd_lo[:, f, :], in0=dw[:, f % WS, 2 * DM:], scalar=SW,
                                         in1=wd_hi[:, f, :], op0=ALU.mult,
                                         op1=ALU.subtract).then_inc(D["wd_lo_ready"], 1)

            parted = sem("dense_parted")

            def dense_half(e, ahead):
                for f in range(FC):
                    dve.wait_ge(D["silu"], e * FC + f + 1)
                    dve.wait_ge(D["up_mm"], e * FC + FC + f + 1)
                    if f >= 2:
                        dve.wait_ge(D["act_ready"], e * FC + f - 1)
                    dve.scalar_tensor_tensor(out=af[:, f % 2, :], in0=bank[2 * (f % 2) + 1][:, :],
                                             scalar=1.0 / SW, in1=sg[:, f % 2, :], op0=ALU.mult,
                                             op1=ALU.mult).then_inc(D["product"], 1)
                    dve.wait_ge(D["product"], e * FC + FC + f + 1)
                    dve.tensor_copy(act_hi[:, f, :], af[:, f % 2, :]).then_inc(parted, 1)
                    dve.wait_ge(parted, e * FC + f + 1)
                    dve.tensor_tensor(act_lo[:, f, :], af[:, f % 2, :], act_hi[:, f, :],
                                      ALU.subtract).then_inc(D["act_ready"], 1)
                    if f + LEAD < FC:
                        gu_remainder(e, f + LEAD)
                        wd_remainder(e, f + LEAD)
                    elif ahead:
                        gu_remainder(e + 1, f + LEAD - FC)
                dve.wait_ge(D["y_added"], e * KC + KC)
                for m in range(KC):
                    dve.wait_ge(D["down_mm"], e * KC + KC + m + 1)
                    dve.scalar_tensor_tensor(out=xT[:, m, :], in0=bank[4 + m % 4][:, :],
                                             scalar=1.0 / (SW * SX), in1=xT[:, m, :], op0=ALU.mult,
                                             op1=ALU.add).then_inc(D["y_added"], 1)

            dve.sem_inc(D["product"], FC)
            dve.sem_inc(D["y_added"], KC)
            dve.sem_inc(D["wd_lo_ready"], FC)
            dve.sem_inc(M["product"], FC)
            dve.sem_inc(M["lo_ready"], FC)
            dve.wait_ge(*ready("first_consts"))
            for l in range(DEPTH):
                y, ay, e_, w, w2, p_, dneg, dpos = (lc[:, 2 * i:2 * i + 2] for i in range(8))
                if l > 0:
                    dve.wait_ge(*ready("lru_tanh", l - 1, LC - 1))
                link(dve.tensor_scalar(y, par(l, "lam", 0, LC), -1.0, None, ALU.mult))
                dve.tensor_tensor(ay, y, par(l, "lam", 0, LC), ALU.max).then_inc(*signal("lam_abs", l))
                dve.wait_ge(*ready("lam_exp", l))
                link(dve.tensor_scalar(w, e_, 2.0, None, ALU.add))
                link(dve.reciprocal(w, w))
                link(dve.tensor_tensor(w, w, e_, ALU.mult))
                link(dve.tensor_tensor(w2, w, w, ALU.mult))
                link(dve.tensor_scalar(p_, w2, 1.0 / 19, 1.0 / 17, ALU.mult, ALU.add))
                for n in range(15, 0, -2):
                    link(dve.tensor_tensor(p_, p_, w2, ALU.mult))
                    link(dve.tensor_scalar(p_, p_, 1.0 / n, None, ALU.add))
                link(dve.tensor_tensor(p_, p_, w, ALU.mult))
                link(dve.tensor_scalar(p_, p_, 16.0, None, ALU.mult))
                link(dve.tensor_scalar(y, y, 0.0, 8.0, ALU.max, ALU.mult))
                link(dve.tensor_tensor(dpos, y, p_, ALU.add))
                link(dve.tensor_scalar(lc[:, 10:12], dpos, -1.0, None, ALU.mult))
                dve.tensor_copy(lc[:, 12:14], dpos).then_inc(*signal("decay", l))

                for J in range(NW * l, NW * l + WS):
                    w_remainder(J)
                normed((l, "mix"), [(hf[:, k % 2, :], xT[:, k, :], par(l, "norm_mix", k), P) for k in range(KC)], "hf")
                for J in range(NW * l + WS, NW * l + WR):
                    w_remainder(J)

                def feat(j):
                    w_remainder(NW * l + j + WR)

                def wtok_lower(_):
                    dve.wait_ge(*ready("wtok_hi", l))
                    dve.scalar_tensor_tensor(out=wtok_lo, in0=wtok, scalar=SW, in1=wtok_hi, op0=ALU.mult,
                                             op1=ALU.subtract).then_inc(*signal("wtok_lo", l))

                def conv(c):
                    dve.wait_ge(*ready("feat", l, feat_index("x", c)))
                    link(dve.memset(xl[:, c, 0:CONV - 1], 0.0))
                    link(dve.tensor_scalar(tmp[:, c, :], xl[:, c, 0:T], par(l, "conv_w", c * CONV),
                                           par(l, "conv_b", c), ALU.mult, ALU.add))
                    for k in range(1, CONV):
                        ins = dve.scalar_tensor_tensor(out=tmp[:, c, :], in0=xl[:, c, k:k + T],
                                                       scalar=par(l, "conv_w", c * CONV + k), in1=tmp[:, c, :],
                                                       op0=ALU.mult, op1=ALU.add)
                        if k < CONV - 1:
                            link(ins)
                    ins.then_inc(*signal("conv", l, c))

                gates = vtok[:, :, 2 * P:].rearrange("p i (h b) -> p i h b", b=3)

                def gate_sum(_):
                    dve.wait_ge(*ready("tok", l, TT - 1))
                    dve.tensor_tensor(vtok[:, :, 2 * P:], vtok[:, :, 2 * P:],
                                      par(l, "gate_b", 0, GATES).unsqueeze(1).broadcast_to([P, TT, GATES]),
                                      ALU.add).then_inc(*signal("gate_sum", l))

                def rope_step(which):
                    name, c = which
                    src = roped_tensor(name, c)
                    if l == 0 and name == "kpe":
                        dve.wait_ge(*ready("consts"))
                    dve.wait_ge(*ready("rot_mm", l, name, c))
                    b = bank[ring_of[("rot", l, name, c)]]
                    if name == "kpe":
                        rows = slice(NOPE, DQK)
                        rope(kh[rows, :, :], src, b[rows, :], cos32[rows, :], sin32[rows, :], tmp[rows, 2, :],
                             tmp[rows, 3, :], ("roped", l, name, c))
                    else:
                        rope(src, src, b[:, :], cos64[:, :], sin64[:, :], tmp[:, 2, :], tmp[:, 3, :],
                             ("roped", l, name, c))
                    dve.wait_ge(*ready("roped", l, name, c))

                def latent(which):
                    if which == "q":
                        normed((l, "q"), [(qdn[:, 0, :], qdn[:, 0, :], par(l, "q_norm", 0), P),
                                          (qdn[0:Q_RANK - P, 1, :], qdn[0:Q_RANK - P, 1, :],
                                           par(l, "q_norm", 1)[0:Q_RANK - P, :], Q_RANK - P)], "latent")
                    else:
                        dve.wait_ge(*ready("latent", l, "q", 1))
                        normed((l, "kv"), [(kvdn, kvdn, par(l, "kv_norm"), P)], "latent")

                def qrot(h):
                    rows = slice(NOPE, DQK)
                    dve.wait_ge(*ready("qrot_mm", l, h))
                    b = bank[ring_of[("qrot", l, h)]]
                    rope(qh[rows, h, :], qh[rows, h, :], b[rows, :], cos32[rows, :], sin32[rows, :],
                         tmp[rows, 2, :], tmp[rows, 3, :], ("qrope", l, h))
                    dve.wait_ge(*ready("qrope", l, h))

                def window(s):
                    dve.wait_ge(*ready("cmp_w", l))
                    dve.wait_ge(*ready("kcg", l, s))
                    if s == 1:
                        dve.wait_ge(*ready("hid_mm", l, 0))
                    for l1 in range(2):
                        v = kcg.rearrange("p g (n u) -> p g n u", u=CMP_STRIDE)[:, :, l1:l1 + NCMP, 0:CMP_STRIDE:2]
                        v = v.rearrange("p g n u -> p u g n")
                        pos = cpos[:, s, l1 * 8:l1 * 8 + 8].unsqueeze(2).unsqueeze(3).broadcast_to([P, 8, 2, NCMP])
                        ins = dve.tensor_tensor(win[:, l1 * 8:l1 * 8 + 8, :, :], v, pos, ALU.add)
                    ins.then_inc(*signal("win", l, s))

                def cmp_scores(_):
                    dve.wait_ge(*ready("uv_mm", l, TT - 1))
                    for i in range(TT):
                        for g in range(2):
                            dve.wait_ge(*ready("sc_mm", l, i, g))
                            dve.tensor_tensor(Sc[:, i, 3 * g:3 * g + 3, :],
                                              bank[ring_of[("sc", l, i, g)]][:, 0:3 * NCMP]
                                              .rearrange("p (h n) -> p h n", h=3),
                                              cmask[:, i, :].unsqueeze(1).broadcast_to([P, 3, NCMP]),
                                              ALU.add).then_inc(*signal("sc", l, i, g))

                def cmp_max(_):
                    dve.wait_ge(*ready("sc", l, TT - 1, 1))
                    link(dve.tensor_reduce(cmx, Sc, AX_X, ALU.max))
                    dve.tensor_tensor(Sc, Sc, cmx.unsqueeze(3).broadcast_to([P, TT, HEADS, NCMP]),
                                      ALU.subtract).then_inc(*signal("sc_sub", l))

                def lru_decay(_):
                    for c in range(LC):
                        dve.wait_ge(*ready("lru_tanh", l, c))
                        link(dve.tensor_tensor(sq[:, c, :], xl[:, c, 0:T], xl[:, c, 0:T], ALU.mult))
                        dve.scalar_tensor_tensor(out=tmp[:, 2 + c, :], in0=sq[:, c, :], scalar=1.0,
                                                 in1=tmp[:, 2 + c, :], op0=ALU.add,
                                                 op1=ALU.mult).then_inc(*signal("lru_square", l, c))
                        ix = [rms, rstd][c]
                        link(dve.tensor_tensor(ix, ix, tmp[:, c, :], ALU.mult))

                def cmp_probs(_):
                    dve.wait_ge(*ready("sc_exp", l))
                    dve.wait_ge(*ready("gates", l))
                    link(dve.tensor_reduce(csum, Sc, AX_X, ALU.add))
                    link(dve.tensor_scalar(csum, csum, 1e-30, None, ALU.max))
                    link(dve.reciprocal(csum, csum))
                    link(dve.tensor_tensor(csum, csum, gates[:, :, :, 0], ALU.mult))
                    link(dve.tensor_tensor(csum, csum, crow[:, :].unsqueeze(2).broadcast_to([P, TT, HEADS]),
                                           ALU.mult))
                    dve.tensor_tensor(Sc, Sc, csum.unsqueeze(3).broadcast_to([P, TT, HEADS, NCMP]),
                                      ALU.mult).then_inc(*signal("pc", l))

                def lru_scan(_):
                    for c in range(LC):
                        dve.wait_ge(*ready("lru_root", l, c))
                        ix = [rms, rstd][c]
                        link(dve.tensor_tensor(ix, ix, tmp[:, 2 + c, :], ALU.mult))
                        link(dve.tensor_tensor_scan(tmp[:, c, :], xl[:, c, 0:T], ix, 0.0, ALU.mult, ALU.add))

                def lru_finish():
                    dve.wait_ge(*ready("gelu_y", l))
                    for c in range(LC):
                        link(dve.tensor_tensor(tmp[:, c, :], tmp[:, c, :], yl[:, c, :], ALU.mult))
                        keep(c, tmp[:, c, :], ("lru_out", l, c))

                part = {"feat": feat, "wtok": wtok_lower, "norm": latent, "conv": conv, "rope": rope_step,
                        "qrot": qrot, "win": window, "cmp_scores": cmp_scores, "lru_decay": lru_decay,
                        "cmp_max": cmp_max, "lru_root": lru_scan, "gates": gate_sum, "cmp_probs": cmp_probs}
                for step, which in PREPARE:
                    if step in part:
                        part[step](which)

                def maximum(u, i):
                    n = u * TT + i
                    dve.wait_ge(*ready("s_mm", l, n))
                    m = n % 8
                    dve.tensor_reduce(nmx[:, m:m + 1], score_bank[n % 4][:, 0:(i + 1) * P], AX_X, ALU.max,
                                      negate=True).then_inc(*signal("nmx", l, n))

                def scales(u):
                    kind, h, br = UNITS[u]
                    dve.wait_ge(*ready("p", l, u * TT + TT - 1))
                    r = rsum[:, u % 2, :]
                    link(dve.tensor_scalar(r, ssum[:, u % 2, :], 1e-30, None, ALU.max))
                    ins = dve.reciprocal(r, r)
                    if kind == "nsa":
                        link(ins)
                        ins = dve.tensor_tensor(r, r, gates[:, :, h, br], ALU.mult)
                    ins.then_inc(*signal("scale", l, u))
                    dve.wait_ge(*ready("scale", l, u))

                def scaled(u, i):
                    v = Pt[:, u % 2, OFF[i]:OFF[i] + (i + 1) * P]
                    dve.tensor_scalar(v, v, rsum[:, u % 2, i:i + 1], None,
                                      ALU.mult).then_inc(*signal("pn", l, u * TT + i))

                def collect(u):
                    chunk, p0, opens, closes = unit_out(u)
                    if closes:
                        dve.wait_ge(*ready("pv", l, u))
                        keep(chunk, out_bank[chunk % 2][:, :], ("mix", l, chunk))

                for u in range(NU):
                    for i in range(TT):
                        maximum(u, i)
                        if u >= 1:
                            if i == 0:
                                scales(u - 1)
                            scaled(u - 1, i)
                    if u == 1:
                        lru_finish()
                    if u >= 2:
                        collect(u - 2)
                scales(NU - 1)
                for i in range(TT):
                    scaled(NU - 1, i)
                collect(NU - 2)
                collect(NU - 1)
                for m in range(KC):
                    dve.wait_ge(*ready("w_used", NW * l + NF + m))
                    dve.scalar_tensor_tensor(out=xT[:, m, :], in0=bank[ring_of[("out", l, m)]][:, :],
                                             scalar=1.0 / (SW * SX), in1=xT[:, m, :], op0=ALU.mult,
                                             op1=ALU.add).then_inc(*signal("x_mixed", l, m))
                    if m + WR < KC:
                        w_remainder(NW * l + NF + m + WR)
                dve.wait_ge(*ready("x_mixed", l, KC - 1))
                if l == 0:
                    for f in range(LEAD):
                        gu_remainder(0, f)
                    for f in range(LEAD):
                        wd_remainder(0, f)
                else:
                    for f in range(LEAD):
                        expert_remainder(dve, 0, f)
                normed((l, "ffn"), [(hf[:, k % 2, :], xT[:, k, :], par(l, "norm_ffn", k), P) for k in range(KC)], "hf")
                if l == 0:
                    with dve.Fori(0, HALVES - 1) as e:
                        dense_half(e, True)
                        for f in range(LEAD):
                            wd_remainder(e + 1, f)
                    dense_half(HALVES - 1, False)
                    dve.wait_ge(D["y_added"], KC * (HALVES + 1))
                else:
                    dve.wait_ge(*ready("router_hi"))
                    dve.scalar_tensor_tensor(out=wrt_lo, in0=wrt_.rearrange("p (k e) -> p k e", k=KC), scalar=SW,
                                             in1=wrt_hi, op0=ALU.mult, op1=ALU.subtract).then_inc(*signal("router_lo"))
                    dve.wait_ge(*ready("router_mm"))
                    dve.tensor_scalar(lg, bank[ring_of[("router",)]][:, 0:TT * NE].rearrange("p (i e) -> p i e", i=TT),
                                      1.0 / (SW * SX), None, ALU.mult).then_inc(*signal("lg"))
                    dve.wait_ge(*ready("lg"))
                    for i in range(TT):
                        dve.wait_ge(*ready("tok_l_mm", i))
                        dve.tensor_copy(tok_l[:, i, :], bank[ring_of[("tok_l", i)]][:, :].bitcast(F16)
                                        ).then_inc(*signal("tok_l", i))
                    full = [P, TT, NE, NE]
                    of_j, of_e = lg.unsqueeze(2).broadcast_to(full), lg.unsqueeze(3).broadcast_to(full)
                    link(dve.tensor_reduce(rmx, lg, AX_X, ALU.max))
                    link(dve.tensor_tensor(cmp1, of_j, of_e, ALU.is_gt))
                    link(dve.tensor_tensor(cmp2, of_j, of_e, ALU.is_equal))
                    link(dve.tensor_tensor(cmp2, cmp2, tri[:, :].rearrange("p (e j) -> p e j", e=NE).unsqueeze(1)
                                           .broadcast_to(full), ALU.mult))
                    link(dve.tensor_tensor(cmp1, cmp1, cmp2, ALU.add))
                    link(dve.tensor_reduce(sel, cmp1, AX_X, ALU.add))
                    dve.tensor_scalar(sel, sel, 1.5, None, ALU.is_lt).then_inc(*signal("sel"))
                    dve.tensor_tensor(lg, lg, rmx.unsqueeze(2).broadcast_to([P, TT, NE]),
                                      ALU.subtract).then_inc(*signal("lg_sub"))
                    dve.wait_ge(*ready("lg_exp"))
                    dve.wait_ge(*ready("sel"))
                    link(dve.tensor_tensor(gate, sel, lg, ALU.mult))
                    link(dve.tensor_reduce(rsm, gate, AX_X, ALU.add))
                    link(dve.reciprocal(rsm, rsm))
                    link(dve.tensor_tensor(gate, gate, rsm.unsqueeze(2).broadcast_to([P, TT, NE]), ALU.mult))
                    link(dve.memset(yT_[:, KC * CAP:], 0.0))
                    link(dve.memset(hot[:, :, CAP:], 0.0))
                    link(dve.memset(g3_, 0.0))
                    for c in range(3):
                        link(dve.tensor_copy(g3[:, :, :, c], gate))
                        if c < 2:
                            link(dve.tensor_tensor(gate, gate, g3[:, :, :, c], ALU.subtract))
                    dve.wait_ge(*ready("count_mm"))
                    b = bank[ring_of[("count",)]]
                    link(dve.scalar_tensor_tensor(out=posm, in0=b[:, 0:TT * NE].rearrange("p (i e) -> p i e", i=TT),
                                                  scalar=1.0, in1=sel, op0=ALU.add, op1=ALU.mult))
                    link(dve.tensor_scalar(posm_, posm_, -1.0, None, ALU.add))
                    dve.tensor_reduce(cmax, b[:, TT * NE:(TT + 1) * NE], AX_X, ALU.max).then_inc(*signal("places"))
                    dve.wait_ge(*ready("places"))
                    dve.tensor_copy(flag[:, :], cmax).then_inc(*signal("flag"))
                    dve.wait_ge(*ready("flag"))
                    dve.sem_inc(*signal("routed"))
                    experts_dve(dve)
                    dve.memset(cmax, 0.0).then_inc(*signal("moe_added"))
            normed((DEPTH, "final"), [(outf[:, k, :], xT[:, k, :], gfin[:, k:k + 1], P) for k in range(KC)], "h")

        @block.gpsimd
        def _(pool):
            pool.wait_ge(*ready("consts"))
            pool.tensor_copy(identb, ident[:, :]).then_inc(*signal("identb"))
            pool.tensor_copy(identh, ident[:, :]).then_inc(*signal("identb"))
            pool.tensor_copy(diagb, diag).then_inc(*signal("identb"))
            for l in range(DEPTH):
                for s, src in enumerate((kcT, vcT)):
                    if s == 0:
                        pool.wait_ge(*ready("roped", l, "kc", 0))
                    else:
                        pool.wait_ge(*ready("feat", l, feat_index("vc", 0)))
                        pool.wait_ge(*ready("win", l, 0))
                    for g in range(2):
                        rows = src[g * HD:(g + 1) * HD, :]
                        pool.dma_start(kcg[0:HD, g, :], rows).then_inc(*signal("kcg", l, s, by=16))
                        pool.dma_start(kcg[HD:P, g, 0:T - 1], rows[:, 1:T]).then_inc(*signal("kcg", l, s, by=16))

        @block.sync
        def _(sp):
            for k in range(0, KC, 2):
                sp.dma_start(xT[:, k:k + 2, :], io["x"][:, k * T:(k + 2) * T].rearrange("p (k t) -> p k t", k=2)
                             ).then_inc(*signal(f"x_loaded{k // 2}", by=16))
            for name, dst in (("ones", ones), ("eps", eps), ("pp", pp)):
                sp.dma_start(dst[:, :], io[name]).then_inc(*signal("first_consts", by=16))

            def chunk(J):
                if J >= WS:
                    sp.wait_ge(*ready("w_lo", J - WS))
                sp.dma_start(wstage[:, J % WS, :, :], io["w_chunk"][J]).then_inc(*signal(f"wstage{J % WS}", J, by=16))

            for J in range(WS):
                chunk(J)
            for name, dst in (("ident", ident), ("diag", diag), ("rot64", rot64), ("rot32", rot32), ("cos64", cos64),
                              ("sin64", sin64), ("cos32", cos32), ("sin32", sin32), ("crow", crow)):
                sp.dma_start(dst[:, :], io[name]).then_inc(*signal("consts", by=16))
            sp.dma_start(cmask, io["cmask"]).then_inc(*signal("consts", by=16))
            for l in range(DEPTH):
                if l > 0:
                    sp.wait_ge(*x_ready(l, 0))
                for J in range(NW * l + WS, NW * (l + 1)):
                    chunk(J)
                    j = J - NW * l
                    if j == 3:
                        sp.dma_start(wuq, io["w_uq"][l]).then_inc(*signal("mla_w", l, by=16))
                        sp.dma_start(wukv, io["w_ukv"][l]).then_inc(*signal("mla_w", l, by=16))
                    if j == 5:
                        sp.dma_start(wtok, io["w_tok"][l]).then_inc(*signal("wtok", l, by=16))
                    if j == 6:
                        sp.dma_start(cw1, io["cmp_w1"][l]).then_inc(*signal("cmp_w", l, by=16))
                        sp.dma_start(cw2, io["cmp_w2"][l]).then_inc(*signal("cmp_w", l, by=16))
                        sp.dma_start(cpos, io["cmp_pos"][l]).then_inc(*signal("cmp_w", l, by=16))
                    if j == 7:
                        sp.dma_start(lruw, io["lru_w"][l]).then_inc(*signal("lru_w", l, by=16))
                    if j == 8 and l == 0:
                        for name, dst in (("lower", lower), ("iota", iota), ("tri", tri), ("gfin", gfin)):
                            sp.dma_start(dst[:, :], io[name]).then_inc(*signal("late_consts", by=16))
                        sp.dma_start(wrt_, io["router"]).then_inc(*signal("late_consts", by=16))
                sp.wait_ge(*ready("pv", l, NU - 1))
                sp.wait_ge(*ready("lru_out", l, LC - 1))
                if l == 1:
                    experts_sp(sp)
                    continue
                with sp.Fori(0, HALVES) as e:
                    for f in range(FC):
                        sp.wait_ge(D["wd_lo_ready"], e * FC + FC + last_in(WS, f) + 1)
                        sp.dma_start(dw[:, f % WS, :], io["dw"][bass.ds(e * FC + f, 1)]
                                     .rearrange("a p n -> p (a n)")).then_inc(dw_loaded[f % WS], 16)
                for J in range(NW * (l + 1), NW * (l + 1) + WS):
                    chunk(J)
            for k in range(KC):
                sp.wait_ge(*ready("h", DEPTH, "final", k))
                sp.dma_start(io["out"][:, k, :], outf[:, k, :]).then_inc(*signal("stored", by=16))
            sp.wait_ge(*ready("stored"))
        return raised_to


def tables(np):
    t = {}
    pos = np.arange(T, dtype=np.float32)

    def rope(d, rows, at):
        half = d // 2
        inv = (np.float32(10000.0) ** (-np.arange(half, dtype=np.float32) * np.float32(2.0) / np.float32(d)))
        ang = pos[:, None] * inv.astype(np.float32)[None, :]
        cos, sin = np.cos(ang).T, np.sin(ang).T
        c, s = np.zeros((P, T), np.float32), np.zeros((P, T), np.float32)
        for a in range(at, at + rows, d):
            c[a:a + half], c[a + half:a + d] = cos, cos
            s[a:a + half], s[a + half:a + d] = -sin, sin
        return c, s

    t["cos64"], t["sin64"] = rope(HD, P, 0)
    t["cos32"], t["sin32"] = rope(ROPE, ROPE, NOPE)
    t["ident"] = np.eye(P, dtype=np.float32)
    r = np.arange(P)
    t["rot64"] = (r[:, None] == (r ^ 32)[None, :]).astype(np.float32)
    t["rot32"] = ((r[:, None] % ROPE) == (np.arange(ROPE) ^ 16)[None, :]).astype(np.float32)
    t["ones"] = np.ones((P, P), np.float32)
    t["lower"] = (r[:, None] < r[None, :]).astype(np.float32)
    t["iota"] = np.tile(np.arange(ROUNDS * CAP, dtype=np.float32), (P, 1))
    t["diag"] = np.where(r[None, :] <= r[:, None], 0.0, NEG).astype(np.float32)
    end = np.arange(NCMP) * CMP_STRIDE + CMP_LEN - 1
    q = np.arange(TT)[None, :] * P + r[:, None]
    t["cmask"] = np.where(end[None, None, :] <= q[:, :, None], 0.0, NEG).astype(np.float32)
    t["crow"] = (q >= CMP_LEN - 1).astype(np.float32)
    e = np.arange(NE)
    t["tri"] = np.tile((e[None, :] < e[:, None]).astype(np.float32).reshape(1, -1), (P, 1))
    t["eps"] = np.full((P, 1), EPS, np.float32)
    return t


def kernel(x, norm_mix, w_in, lru_conv_w, lru_conv_b, lru_wa, lru_ba, lru_wx, lru_bx, lru_lambda,
           mla_q_norm, mla_w_uq, mla_kv_norm, mla_w_ukv, nsa_cmp_pos, nsa_cmp_w1, nsa_cmp_w2, nsa_gate_b,
           w_out, norm_ffn, ffn_w_gate, ffn_w_up, ffn_w_down, router_w, moe_w_gate, moe_w_up,
           moe_w_down, norm_final):
    import numpy as np
    import concourse.bacc as bacc
    from concourse.bass_utils import run_bass_kernel_spmd

    A = np.asarray
    w_in, w_out = A(w_in), A(w_out)
    arrays = tables(np)

    def cols(v, rows=P):
        v = A(v)
        return np.moveaxis(v.reshape(v.shape[0], -1, rows), 2, 0)

    pp = np.zeros((P, DEPTH, NPP), np.float32)

    def put(name, v):
        pp[:v.shape[0], :, PC[name]:PC[name] + v.shape[2]] = v

    put("norm_mix", cols(norm_mix))
    put("norm_ffn", cols(norm_ffn))
    put("conv_w", A(lru_conv_w).reshape(DEPTH, CONV, LC, P).transpose(3, 0, 2, 1).reshape(P, DEPTH, LC * CONV))
    put("conv_b", cols(lru_conv_b))
    put("ba", cols(lru_ba))
    put("bx", cols(lru_bx))
    put("lam", cols(lru_lambda))
    put("q_norm", cols(A(mla_q_norm)[:, :P]))
    pp[:Q_RANK - P, :, PC["q_norm"] + 1] = A(mla_q_norm)[:, P:].T
    put("kv_norm", cols(mla_kv_norm))
    pp[:, :, PC["gate_b"]:PC["gate_b"] + GATES] = A(nsa_gate_b)[None]
    arrays["pp"] = pp.reshape(P, DEPTH * NPP)
    arrays["gfin"] = A(norm_final).reshape(KC, P).T
    arrays["x"] = A(x)[0].T.reshape(KC, P, T).transpose(1, 0, 2).reshape(P, KC * T)

    heads = [np.r_[c * HD:(c + 1) * HD, (c + 3) * HD:(c + 4) * HD] for c in range(3)]
    where = {"x": (0, P), "y": (LRU_W, P), "qdn": (512, P), "kvdn": (704, P), "kpe": (832, ROPE), "q": (864, P),
             "kc": (1248, P), "vc": (1376, P), "ks": (1504, P), "kw": (1760, P)}
    chunks = np.zeros((DEPTH * NW, P, KC, P), np.float32)
    for l in range(DEPTH):
        w = w_in[l].reshape(KC, P, -1).transpose(1, 0, 2)
        for j, (name, c, rows, p0) in enumerate(FEAT):
            at = where[name][0] + c * P
            idx = where["q"][0] + heads[c] if name == "q" else np.arange(at, at + rows)
            chunks[l * NW + j, :, :, :rows] = w[:, :, idx]
        order = np.concatenate([np.arange(5 * P)] + [5 * P + h for h in heads])
        wo = w_out[l][order].reshape(KC, P, KC, P).transpose(2, 1, 0, 3)
        chunks[l * NW + NF:(l + 1) * NW] = wo
    arrays["w_chunk"] = chunks
    tok = np.r_[1632:1760, 1888:2016, 2016:2034]
    arrays["w_tok"] = w_in[:, :, tok].reshape(DEPTH, KC, P, TOKW).transpose(0, 2, 1, 3)
    wuq = np.zeros((DEPTH, P, 2, HEADS * DQK), np.float32)
    wuq[:, :, 0] = A(mla_w_uq)[:, :P]
    wuq[:, :Q_RANK - P, 1] = A(mla_w_uq)[:, P:]
    arrays["w_uq"] = wuq
    arrays["w_ukv"] = A(mla_w_ukv).reshape(DEPTH, P, HEADS, 2, HD).transpose(0, 1, 3, 2, 4).reshape(DEPTH, P, 2, -1)
    arrays["cmp_w1"] = A(nsa_cmp_w1).reshape(DEPTH, 2, LP, P, P).transpose(0, 3, 1, 2, 4)
    arrays["cmp_w2"] = A(nsa_cmp_w2).transpose(0, 2, 1, 3)
    arrays["cmp_pos"] = A(nsa_cmp_pos).reshape(DEPTH, 2, LP, P).transpose(0, 3, 1, 2)
    lru = np.zeros((DEPTH, P, 2, LC, P), np.float32)
    for w, v in enumerate((A(lru_wa), A(lru_wx))):
        for n in range(4):
            a = 64 * (n % 2)
            lru[:, a:a + 64, w, n // 2, a:a + 64] = v[:, n]
    arrays["lru_w"] = lru
    arrays["router"] = A(router_w)[0].reshape(KC, P, NE).transpose(1, 0, 2).reshape(P, KC * NE)

    def gate_up(g, u):
        both = np.stack([A(g), A(u)], 0)
        both = both.reshape(2, -1, KC, P, FC, P)
        return both.transpose(1, 4, 3, 0, 2, 5).reshape(-1, P, 2, KC, P)

    dense = [A(v)[0].reshape(DM, 2, FE).transpose(1, 0, 2) for v in (ffn_w_gate, ffn_w_up)]

    def chunked(g, u, d):
        w = np.empty((g.shape[0] * FC, P, 3, DM), np.float32)
        w[:, :, 0:2] = gate_up(g, u).reshape(-1, P, 2, DM)
        w[:, :, 2] = d.reshape(-1, P, DM)
        return w.reshape(-1, P, 3 * DM)

    arrays["dw"] = chunked(*dense, A(ffn_w_down)[0])
    arrays["ew"] = chunked(A(moe_w_gate)[0], A(moe_w_up)[0], A(moe_w_down)[0])

    def build(known):
        nc = bacc.Bacc("TRN2", target_bir_lowering=False, num_devices=1)
        io = {n: nc.dram_tensor(f"in_{n}", list(a.shape), F32, kind="ExternalInput").ap() for n, a in arrays.items()}
        io["out"] = nc.dram_tensor("out_x", [P, KC, T], F32, kind="ExternalOutput").ap()
        return nc, trunk(nc, io, known)

    _, counted = build({})
    nc, again = build(counted)
    assert again == counted
    r = run_bass_kernel_spmd(nc, [{f"in_{n}": np.ascontiguousarray(a, np.float32) for n, a in arrays.items()}],
                             core_ids=[0])
    out = r.results[0]["out_x"]
    return np.ascontiguousarray(out.transpose(1, 0, 2).reshape(DM, T).T[None])
```
